# Optimizing a Trainium2 kernel written in Bass

```python
import math
import jax, jax.numpy as jnp
from jax import lax
import numpy as np

D_MODEL = 2048
BATCH = 1
SEQ = 512
DEPTH = 1

CHUNK = 64
MEM_LEN = 256
EPS = 1e-6
GDN_HEAD_DIM = 128
GDN_WIDTH = D_MODEL // 2
GDN_HEADS = GDN_WIDTH // GDN_HEAD_DIM
CONV_WIDTH = 4
S5_WIDTH = D_MODEL // 2
S5_GROUP = 16
S5_GROUPS = S5_WIDTH // S5_GROUP
S5_STATE = 64
XA_HEADS = 4
XA_WIDTH = D_MODEL // 2
XA_HEAD_DIM = XA_WIDTH // XA_HEADS
N_BRANCHES = 3
IN_SPLITS = (3 * GDN_WIDTH, GDN_WIDTH, GDN_HEADS, GDN_HEADS, S5_WIDTH, S5_WIDTH, XA_WIDTH, XA_WIDTH, N_BRANCHES * D_MODEL)

kernel_name = 'hybrid_gdn_s5_memxattn_block'

def rmsnorm(x, g):
    xf = x.astype(jnp.float32)
    y = xf * lax.rsqrt(jnp.mean(xf * xf, axis=-1, keepdims=True) + EPS)
    return (y * g.astype(jnp.float32)).astype(x.dtype)

def l2norm(x):
    return x * lax.rsqrt(jnp.sum(x * x, axis=-1, keepdims=True) + EPS)

def split_columns(t, sizes):
    out = []
    start = 0
    for s in sizes:
        out.append(t[..., start:start + s])
        start += s
    return out

def causal_depthwise_conv(x, w):
    c = x.shape[-1]
    return lax.conv_general_dilated(x, w[:, None, :], window_strides=(1,), padding=[(w.shape[0] - 1, 0)],
                                    dimension_numbers=('NWC', 'WIO', 'NWC'), feature_group_count=c)

def chunked_gated_delta_rule(q, k, v, g, beta):
    bsz, s, h, dk = q.shape
    dv = v.shape[-1]
    n = s // CHUNK
    def to_chunks(t):
        t = t.reshape((bsz, n, CHUNK, h) + t.shape[3:])
        return jnp.swapaxes(t, 2, 3)
    q, k, v, g, beta = (to_chunks(t) for t in (q, k, v, g, beta))
    gc = jnp.cumsum(g, axis=-1)
    incl = jnp.tril(jnp.ones((CHUNK, CHUNK), dtype=bool))
    strict = jnp.tril(jnp.ones((CHUNK, CHUNK), dtype=bool), -1)
    decay = jnp.exp(jnp.where(incl, gc[..., :, None] - gc[..., None, :], -jnp.inf))
    k_beta = k * beta[..., None]
    lower = jnp.where(strict, jnp.einsum('bnhid,bnhjd->bnhij', k_beta, k) * decay, 0.0)
    eye = jnp.eye(CHUNK, dtype=q.dtype)
    rhs = jnp.concatenate([v * beta[..., None], k_beta * jnp.exp(gc)[..., None]], axis=-1)
    sol = lax.linalg.triangular_solve(eye + lower, rhs, left_side=True, lower=True, unit_diagonal=True)
    u_val, w_dec = sol[..., :dv], sol[..., dv:]
    qk = jnp.einsum('bnhid,bnhjd->bnhij', q, k) * decay
    q_dec = q * jnp.exp(gc)[..., None]
    k_dec = k * jnp.exp(gc[..., -1:] - gc)[..., None]
    g_last = jnp.exp(gc[..., -1])

    def step(state, inp):
        w_n, u_n, qd_n, qk_n, kd_n, gl_n = inp
        v_new = u_n - jnp.einsum('bhcd,bhde->bhce', w_n, state)
        o = jnp.einsum('bhcd,bhde->bhce', qd_n, state) + jnp.einsum('bhij,bhje->bhie', qk_n, v_new)
        state = state * gl_n[..., None, None] + jnp.einsum('bhcd,bhce->bhde', kd_n, v_new)
        return state, o

    xs = tuple(jnp.moveaxis(t, 1, 0) for t in (w_dec, u_val, q_dec, qk, k_dec, g_last))
    state0 = jnp.zeros((bsz, h, dk, dv), dtype=q.dtype)
    _, o = lax.scan(step, state0, xs)
    o = jnp.transpose(o, (1, 0, 3, 2, 4))
    return o.reshape(bsz, s, h, dv)

def gated_deltanet(qkv_raw, beta_raw, a_raw, conv_w, a_log, dt_bias, out_norm_g):
    bsz, s, _ = qkv_raw.shape
    qkv = jax.nn.silu(causal_depthwise_conv(qkv_raw, conv_w)).astype(jnp.float32)
    q, k, v = jnp.split(qkv, 3, axis=-1)
    q = q.reshape(bsz, s, GDN_HEADS, GDN_HEAD_DIM)
    k = k.reshape(bsz, s, GDN_HEADS, GDN_HEAD_DIM)
    v = v.reshape(bsz, s, GDN_HEADS, GDN_HEAD_DIM)
    q = l2norm(q) * (GDN_HEAD_DIM ** -0.5)
    k = l2norm(k)
    beta = jax.nn.sigmoid(beta_raw.astype(jnp.float32))
    g = -jnp.exp(a_log.astype(jnp.float32)) * jax.nn.softplus(a_raw.astype(jnp.float32) + dt_bias.astype(jnp.float32))
    o = chunked_gated_delta_rule(q, k, v, g, beta)
    o = rmsnorm(o, out_norm_g)
    return o.reshape(bsz, s, GDN_WIDTH).astype(qkv_raw.dtype)

def complex_linear_combine(e1, e2):
    a1r, a1i, b1r, b1i = e1
    a2r, a2i, b2r, b2i = e2
    return (a2r * a1r - a2i * a1i,
            a2r * a1i + a2i * a1r,
            a2r * b1r - a2i * b1i + b2r,
            a2r * b1i + a2i * b1r + b2i)

def s5_layer(xb, lam_re, lam_im, log_dt, b_re, b_im, c_re, c_im, d, w_glu):
    f32 = jnp.float32
    bsz, s, _ = xb.shape
    xf = xb.astype(f32)
    xg = xf.reshape(bsz, s, S5_GROUPS, S5_GROUP)
    lr, li = lam_re.astype(f32), lam_im.astype(f32)
    dt = jnp.exp(log_dt.astype(f32))[:, None]
    mag = jnp.exp(lr * dt)
    ab_re, ab_im = mag * jnp.cos(li * dt), mag * jnp.sin(li * dt)
    den = lr * lr + li * li
    nr, ni = ab_re - 1.0, ab_im
    coef_re = (nr * lr + ni * li) / den
    coef_im = (ni * lr - nr * li) / den
    br, bi = b_re.astype(f32), b_im.astype(f32)
    bb_re = coef_re[..., None] * br - coef_im[..., None] * bi
    bb_im = coef_re[..., None] * bi + coef_im[..., None] * br
    bu_re = jnp.einsum('bsgi,gpi->bsgp', xg, bb_re)
    bu_im = jnp.einsum('bsgi,gpi->bsgp', xg, bb_im)
    a_re = jnp.broadcast_to(ab_re, bu_re.shape)
    a_im = jnp.broadcast_to(ab_im, bu_im.shape)
    _, _, h_re, h_im = lax.associative_scan(complex_linear_combine, (a_re, a_im, bu_re, bu_im), axis=1)
    y = jnp.einsum('bsgp,gip->bsgi', h_re, c_re.astype(f32)) - jnp.einsum('bsgp,gip->bsgi', h_im, c_im.astype(f32))
    y = y.reshape(bsz, s, S5_WIDTH) + d.astype(f32) * xf
    y = jax.nn.gelu(y)
    val, gate = jnp.split(y @ w_glu.astype(f32), 2, axis=-1)
    return (val * jax.nn.sigmoid(gate)).astype(xb.dtype)

def memory_cross_attention(q_raw, mem_n, w_kv):
    bsz, s, _ = q_raw.shape
    k, v = jnp.split(mem_n @ w_kv, 2, axis=-1)
    q = q_raw.reshape(bsz, s, XA_HEADS, XA_HEAD_DIM)
    k = k.reshape(bsz, MEM_LEN, XA_HEADS, XA_HEAD_DIM)
    v = v.reshape(bsz, MEM_LEN, XA_HEADS, XA_HEAD_DIM)
    scores = jnp.einsum('bshd,bmhd->bhsm', q, k).astype(jnp.float32) * (XA_HEAD_DIM ** -0.5)
    p = jax.nn.softmax(scores, axis=-1).astype(v.dtype)
    o = jnp.einsum('bhsm,bmhd->bshd', p, v)
    return o.reshape(bsz, s, XA_WIDTH)

def setup_inputs(seed: int = 0) -> dict:
    key = jax.random.key(seed)
    ks = jax.random.split(key, 28)
    f32 = jnp.float32
    L, G, P = DEPTH, S5_GROUPS, S5_STATE
    def nrm(k, shape, scale):
        return jax.random.normal(k, shape, f32) * scale
    in_width = sum(IN_SPLITS)
    dt = jnp.exp(jax.random.uniform(ks[6], (L, GDN_HEADS), f32, math.log(1e-3), math.log(1e-1)))
    n_idx = jnp.arange(P, dtype=f32)
    return {
        'x': nrm(ks[0], (BATCH, SEQ, D_MODEL), 1.0),
        'mem': nrm(ks[1], (BATCH, MEM_LEN, D_MODEL), 1.0),
        'norm_g': 1.0 + nrm(ks[2], (L, D_MODEL), 0.02),
        'w_in': nrm(ks[3], (L, D_MODEL, in_width), D_MODEL ** -0.5),
        'conv_w': nrm(ks[4], (L, CONV_WIDTH, 3 * GDN_WIDTH), CONV_WIDTH ** -0.5),
        'gdn_a_log': jnp.log(jax.random.uniform(ks[5], (L, GDN_HEADS), f32, 1.0, 16.0)),
        'gdn_dt_bias': dt + jnp.log(-jnp.expm1(-dt)),
        'gdn_norm_g': 1.0 + nrm(ks[7], (L, GDN_HEAD_DIM), 0.02),
        's5_lambda_re': -0.5 + nrm(ks[8], (L, G, P), 0.01),
        's5_lambda_im': math.pi * n_idx + nrm(ks[9], (L, G, P), 0.01),
        's5_log_dt': jax.random.uniform(ks[10], (L, G), f32, math.log(1e-3), math.log(1e-1)),
        's5_b_re': nrm(ks[11], (L, G, P, S5_GROUP), (2 * S5_GROUP) ** -0.5),
        's5_b_im': nrm(ks[12], (L, G, P, S5_GROUP), (2 * S5_GROUP) ** -0.5),
        's5_c_re': nrm(ks[13], (L, G, S5_GROUP, P), (2 * P) ** -0.5),
        's5_c_im': nrm(ks[14], (L, G, S5_GROUP, P), (2 * P) ** -0.5),
        's5_d': nrm(ks[15], (L, S5_WIDTH), 1.0),
        's5_w_glu': nrm(ks[16], (L, S5_WIDTH, 2 * S5_WIDTH), S5_WIDTH ** -0.5),
        'mem_norm_g': 1.0 + nrm(ks[17], (L, D_MODEL), 0.02),
        'w_kv_mem': nrm(ks[18], (L, D_MODEL, 2 * XA_WIDTH), D_MODEL ** -0.5),
        'w_br_a': nrm(ks[19], (L, GDN_WIDTH, D_MODEL), GDN_WIDTH ** -0.5),
        'w_br_b': nrm(ks[20], (L, S5_WIDTH, D_MODEL), S5_WIDTH ** -0.5),
        'w_br_c': nrm(ks[21], (L, XA_WIDTH, D_MODEL), XA_WIDTH ** -0.5),
        'w_out': nrm(ks[22], (L, D_MODEL, D_MODEL), D_MODEL ** -0.5),
        'final_g': 1.0 + nrm(ks[23], (D_MODEL,), 0.02),
    }

def reference(x, mem, norm_g, w_in, conv_w, gdn_a_log, gdn_dt_bias, gdn_norm_g,
              s5_lambda_re, s5_lambda_im, s5_log_dt, s5_b_re, s5_b_im, s5_c_re, s5_c_im, s5_d, s5_w_glu,
              mem_norm_g, w_kv_mem, w_br_a, w_br_b, w_br_c, w_out, final_g):
    bsz, s, _ = x.shape
    h = x
    for l in range(DEPTH):
        u = rmsnorm(h, norm_g[l])
        proj = u @ w_in[l]
        qkv_a, z_a, beta_raw, a_raw, x_b, z_b, q_c, z_c, gate_raw = split_columns(proj, IN_SPLITS)
        o_a = gated_deltanet(qkv_a, beta_raw, a_raw, conv_w[l], gdn_a_log[l], gdn_dt_bias[l], gdn_norm_g[l])
        p_a = (o_a * jax.nn.silu(z_a)) @ w_br_a[l]
        o_b = s5_layer(x_b, s5_lambda_re[l], s5_lambda_im[l], s5_log_dt[l], s5_b_re[l], s5_b_im[l],
                       s5_c_re[l], s5_c_im[l], s5_d[l], s5_w_glu[l])
        p_b = (o_b * jax.nn.silu(z_b)) @ w_br_b[l]
        o_c = memory_cross_attention(q_c, rmsnorm(mem, mem_norm_g[l]), w_kv_mem[l])
        p_c = (o_c * jax.nn.silu(z_c)) @ w_br_c[l]
        gates = jax.nn.sigmoid(gate_raw.astype(jnp.float32)).astype(x.dtype).reshape(bsz, s, N_BRANCHES, D_MODEL)
        merged = gates[:, :, 0] * p_a + gates[:, :, 1] * p_b + gates[:, :, 2] * p_c
        h = h + merged @ w_out[l]
    return rmsnorm(h, final_g)


_drawn_inputs = setup_inputs


def setup_inputs(seed=0):
    import zlib

    import numpy as np

    out = dict(_drawn_inputs(seed))
    spreads = {}
    factors = {'norm_g': 5.057,
     'gdn_norm_g': 31.615,
     's5_lambda_re': 64.0,
     's5_lambda_im': 64.0,
     's5_log_dt': 64.0,
     's5_b_re': 64.0,
     's5_b_im': 64.0,
     's5_c_re': 64.0,
     's5_c_im': 64.0,
     'mem_norm_g': 8.0,
     'final_g': 8.274}
    for name, (base, spread) in spreads.items():
        noise = np.random.default_rng([zlib.crc32(name.encode()), seed]).standard_normal(out[name].shape)
        drawn = base * np.exp(spread * noise) if base else spread * noise
        out[name] = __import__('jax').numpy.asarray(drawn.astype(out[name].dtype))
    for name, factor in factors.items():
        out[name] = (out[name] * factor).astype(out[name].dtype)
    return out
```

```python
from contextlib import ExitStack

import numpy as np
import concourse.bass as bass
from concourse import mybir

F32 = mybir.dt.float32
F32R = mybir.dt.float32r
ALU = mybir.AluOpType
ACT = mybir.ActivationFunctionType
AX_X = mybir.AxisListType.X

P = 128
S = 512
D = 2048
KD = D // P
NT = S // P
W = 1024
KW = W // P
MEM = 256
MT = MEM // P
HEADS = 8
XH = 4
GS = 16
NS = 64
PAIRS = 32
EPS = 1e-6
Q0, K0, V0, ZA0, BA0 = 0, W, 2 * W, 3 * W, 4 * W
XB0 = BA0 + 2 * HEADS
ZB0, QC0, ZC0 = XB0 + W, XB0 + 2 * W, XB0 + 3 * W
G0 = XB0 + 4 * W
CONV = 4
LEVELS = [2 ** n for n in range(7)]
MATS = ["ident", "upper", "strict", "ones"] + [f"low{s}" for s in LEVELS] + ["up1"]
C_T = len(MATS) * P
C_COL = C_T + S
COLS = ["eps", "eps128", "quarter", "even", "odd", "neven", "nodd"]
NCONST = C_COL + len(COLS)
TWO_PI = 2 * np.pi
PI_A = 6.28125
PI_B = float(np.float32(int((TWO_PI - PI_A) * 2 ** 20) / 2 ** 20))
PI_C = float(TWO_PI - PI_A - PI_B)
ROUND = 1.5 * 2 ** 23
ROUND14 = 1.5 * 2 ** 9


def constants():
    c = np.zeros((P, NCONST), np.float32)
    i, j = np.indices((P, P))
    m = {"ident": i == j, "upper": i <= j, "strict": i > j, "ones": i >= 0}
    for s in LEVELS:
        m[f"low{s}"] = (i // s % 2 == 1) & (j // s == i // s - 1)
    m["up1"] = m["low1"].T
    for n, name in enumerate(MATS):
        c[:, n * P:(n + 1) * P] = m[name]
    c[:, C_T:C_T + S] = np.arange(S)
    g2 = np.arange(P) // GS % 2
    for n, v in enumerate([EPS, P * EPS, np.pi / 2, g2 == 0, g2 == 1, -(g2 == 0).astype(float), -(g2 == 1).astype(float)]):
        c[:, C_COL + n] = v
    return c



def at(j):
    return j[0] + j[1]


def count(j, first, per):
    return j[0] * per + (first + per * j[1])


def wait(e, s, value):
    if isinstance(value, int) and value <= 0:
        return
    e.wait_ge(s, value)


def wait_apart(k, e, s, value):
    wait(e, s, value)
    if not isinstance(value, int):
        e.sem_inc(k.sp_waits if e is k.sp else k.pool_waits, 1)


class Handles:
    pass


def build(nc, x, mem, norm_g, w_in, conv_w, a_log, dt_bias, gdn_g, lam_re, lam_im, log_dt, b_re, b_im,
          c_re, c_im, s5_d, w_glu, mem_g, w_kv, w_a, w_b, w_c, w_out, final_g, consts, out):
    with ExitStack() as ctx:
        k = Handles()
        k.nc = nc
        k.x, k.mem, k.out = x[0], mem[0], out[0]
        k.norm_g, k.mem_g, k.gdn_g, k.s5_d, k.final_g = norm_g[0], mem_g[0], gdn_g[0], s5_d[0], final_g
        k.w_in, k.conv_w, k.w_glu, k.w_kv, k.w_out = w_in[0], conv_w[0], w_glu[0], w_kv[0], w_out[0]
        k.branch_w = [w_c[0], w_b[0], w_a[0]]
        k.a_log, k.dt_bias, k.consts = a_log[0], dt_bias[0], consts
        k.lam_re, k.lam_im, k.log_dt = lam_re[0], lam_im[0], log_dt[0]
        k.b_re, k.b_im, k.c_re, k.c_im = b_re[0], b_im[0], c_re[0], c_im[0]
        k.gated_d = [nc.dram_tensor(f"gated_{n}", [W, S], F32, kind="Internal").ap() for n in "cba"]
        k.y_d = nc.dram_tensor("s5_out", [W, S], F32, kind="Internal").ap()
        k.zb_d = nc.dram_tensor("z_b", [W, S], F32, kind="Internal").ap()

        def sb(where, name, shape, dt=F32):
            return where.enter_context(nc.sbuf_tensor(name, [P] + shape, dt))

        def sems(*names):
            return [ctx.enter_context(nc.semaphore(name)) for name in names]

        k.ps = [ctx.enter_context(nc.psum_tensor(f"bank{n}", [P, S], F32)) for n in range(8)]

        k.uh = sb(ctx, "uh", [KD, S], F32R)
        k.ul = sb(ctx, "ul", [KD, S], F32R)
        k.raw0 = sb(ctx, "raw0", [2048])
        k.raw1 = sb(ctx, "raw1", [2048])
        k.wh0 = sb(ctx, "wh0", [2048], F32R)
        k.wh1 = sb(ctx, "wh1", [2048], F32R)
        k.wl0 = sb(ctx, "wl0", [2048], F32R)
        k.wl1 = sb(ctx, "wl1", [2048], F32R)
        k.cst = sb(ctx, "cst", [NCONST])
        k.prm1 = sb(ctx, "prm1", [P])
        k.prm2 = sb(ctx, "prm2", [P])
        k.s5p = sb(ctx, "s5p", [5, PAIRS])
        k.hp = sb(ctx, "hp", [4, NT, HEADS])
        k.stat = sb(ctx, "stat", [40])
        k.raw, k.wh, k.wl = [k.raw0, k.raw1], [k.wh0, k.wh1], [k.wl0, k.wl1]
        k.mat = {name: k.cst[:, n * P:(n + 1) * P] for n, name in enumerate(MATS)}
        k.col = {name: k.cst[:, C_COL + n:C_COL + n + 1] for n, name in enumerate(COLS)}
        k.tvec = k.cst[:, C_T:C_T + S]

        with ExitStack() as area:
            k.mh = sb(area, "mh", [KD, MEM], F32R)
            k.ml = sb(area, "ml", [KD, MEM], F32R)
            with ExitStack() as a:
                k.xs = sb(a, "xs", [NT, D])
                k.junk = sb(a, "junk", [D])
                k.ut0 = sb(a, "ut0", [S])
                k.ut1 = sb(a, "ut1", [S])
                k.rows1 = sb(a, "rows1", [P])
                k.rows2 = sb(a, "rows2", [P])
                k.ldt2 = sb(a, "ldt2", [2])
                k.alog_b = sb(a, "alog_b", [HEADS])
                k.dtb_b = sb(a, "dtb_b", [HEADS])
                k.wba = sb(a, "wba", [KD * 16])
                k.wbah = sb(a, "wbah", [KD * 16], F32R)
                k.wbal = sb(a, "wbal", [KD * 16], F32R)
                k.tp = sb(a, "tp", [16, PAIRS])
            with ExitStack() as a:
                k.kt = sb(a, "kt", [2, MEM])
                k.vt = sb(a, "vt", [2, MEM])
                k.vx = sb(a, "vx", [MT, 256])
                k.qx = sb(a, "qx", [2, S])
                k.zx = sb(a, "zx", [2, S])
                k.px = sb(a, "px", [NT, MEM])
                k.ptx = sb(a, "ptx", [MT, S])
                k.ox = sb(a, "ox", [2, S])
        with ExitStack() as area:
            k.qraw = sb(area, "qraw", [S + 3])
            k.kraw = sb(area, "kraw", [S + 3])
            k.vraw = sb(area, "vraw", [S + 3])
            k.qc = sb(area, "qc", [S])
            k.kc = sb(area, "kc", [S])
            k.vc = sb(area, "vc", [S])
            k.rq = sb(area, "rq", [S])
            k.rk = sb(area, "rk", [S])
            k.zs = sb(area, "zs", [S])
            k.er = sb(area, "er", [NT, P])
            k.qd = sb(area, "qd", [NT, P])
            k.dl = sb(area, "dl", [NT, P])
            k.du = sb(area, "du", [NT, P])
            k.vb = sb(area, "vb", [NT, P])
            k.kbg = sb(area, "kbg", [NT, P])
            k.kd = sb(area, "kd", [NT, P])
            k.lt = sb(area, "lt", [NT, P])
            k.tl = sb(area, "tl", [NT, P])
            k.tu = sb(area, "tu", [NT, P])
            k.gx = sb(area, "gx", [NT, P])
            k.vn = sb(area, "vn", [NT, P])
            k.st = sb(area, "st", [P])
            k.cwh = sb(area, "cwh", [CONV, 3])
            k.hph = sb(area, "hph", [4, NT])
            k.s5h = sb(area, "s5h", [5, 4])
            k.dh = sb(area, "dh", [1])
            k.xb = sb(area, "xb", [S])
            k.braw = sb(area, "braw", [2, 4, GS])
            k.craw = sb(area, "craw", [2, NS])
            k.bt = sb(area, "bt", [6, 4, GS])
            k.bpad = sb(area, "bpad", [2, 4, 2, GS])
            k.cpad = sb(area, "cpad", [2, 2, NS])
            k.bc = sb(area, "bc", [4, P])
            k.tcos0 = sb(area, "tcos0", [S])
            k.tcos1 = sb(area, "tcos1", [S])
            k.tsin0 = sb(area, "tsin0", [S])
            k.tsin1 = sb(area, "tsin1", [S])
            k.karg = sb(area, "karg", [S])
            k.farg = sb(area, "farg", [S])
            k.ma = sb(area, "ma", [S])
            k.mb = sb(area, "mb", [S])
            k.gr0 = sb(area, "gr0", [S])
            k.gr1 = sb(area, "gr1", [S])
            k.gi0 = sb(area, "gi0", [S])
            k.gi1 = sb(area, "gi1", [S])
            k.hr = sb(area, "hr", [S])
            k.hi = sb(area, "hi", [S])
            k.pt = sb(area, "pt", [S])
            k.zbs = sb(area, "zbs", [S])
        with ExitStack() as area:
            k.zv0 = sb(area, "zv0", [S])
            k.zv1 = sb(area, "zv1", [S])
            k.gg0 = sb(area, "gg0", [S])
            k.gg1 = sb(area, "gg1", [S])
        with ExitStack() as area:
            k.merged = sb(area, "merged", [KD, S])
            with ExitStack() as b:
                k.gh = sb(b, "gh", [KW, S], F32R)
                k.gl = sb(b, "gl", [KW, S], F32R)
                with ExitStack() as a:
                    k.gst = sb(a, "gst", [KW, S])
                    k.sg0 = sb(a, "sg0", [S])
                    k.sg1 = sb(a, "sg1", [S])
                with ExitStack() as a:
                    k.yst = sb(a, "yst", [KW, S])
            with ExitStack() as b:
                k.hrow = sb(b, "hrow", [NT, D])
                k.xr = sb(b, "xr", [NT, S])
                k.fg = sb(b, "fg", [D])
                k.xsq = sb(b, "xsq", [S])
                k.ssq = sb(b, "ssq", [NT, 4])

        k.sp_waits, k.pool_waits, k.w_in0, k.w_in1, k.w_hi, k.w_lo = \
            sems("sp_waits", "pool_waits", "w_in0", "w_in1", "w_hi", "w_lo")
        k.w_used, k.phase_end = \
            sems("w_used", "phase_end")
        k.w_in_slot = [k.w_in0, k.w_in1]
        k.cst_in, k.rows_in, k.rows_zero, k.x_in, k.mem_in, k.wba_in = \
            sems("cst_in", "rows_in", "rows_zero", "x_in", "mem_in", "wba_in")
        k.prm_ps, k.prm, k.ldt_rows, k.x_sq, k.x_root, k.x_scale = \
            sems("prm_ps", "prm", "ldt_rows", "x_sq", "x_root", "x_scale")
        k.x_tr, k.u_f32, k.u_hi, k.u_lo, k.link, k.alink = \
            sems("x_tr", "u_f32", "u_hi", "u_lo", "link", "alink")
        k.wba_hi, k.wba_lo, k.ba_ps, k.g_done, k.gsum_ps, k.p_act = \
            sems("wba_hi", "wba_lo", "ba_ps", "g_done", "gsum_ps", "p_act")
        k.p_dve, = \
            sems("p_dve")
        k.xa_out, k.xa_vtr, k.xa_v, k.xa_sc, k.xa_max, k.xa_exp = \
            sems("xa_out", "xa_vtr", "xa_v", "xa_sc", "xa_max", "xa_exp")
        k.xa_sum, k.xa_p, k.xa_ptr, k.xa_pt, k.xa_o, k.xa_og = \
            sems("xa_sum", "xa_p", "xa_ptr", "xa_pt", "xa_o", "xa_og")
        k.xa_st0, k.xa_st1 = \
            sems("xa_st0", "xa_st1")
        k.mx_out, k.zb_st, k.pad_zero = \
            sems("mx_out", "zb_st", "pad_zero")
        k.sliced, k.conv, k.gu, k.silu, k.sq, k.ss = \
            sems("sliced", "conv", "gu", "silu", "sq", "ss")
        k.rsum, k.root, k.er_s, k.dd, k.dec, k.rn = \
            sems("rsum", "root", "er_s", "dd", "dec", "rn")
        k.qk, k.vtr, k.vb_s, k.ktr, k.kb, k.kk = \
            sems("qk", "vtr", "vb_s", "ktr", "kb", "kk")
        k.kq, k.pm, k.lm, k.qkt, k.ltr, k.lt_s = \
            sems("kq", "pm", "lm", "qkt", "ltr", "lt_s")
        k.tu_s, k.lx, k.xm, k.lp, k.tus, k.wt = \
            sems("tu_s", "lx", "xm", "lp", "tus", "wt")
        k.wtn, k.vp, k.vn_s, k.op, k.sp_s, k.st_s = \
            sems("wtn", "vp", "vn_s", "op", "sp_s", "st_s")
        k.osq, k.sso, k.oroot, k.orn, k.og, k.g_st = \
            sems("osq", "sso", "oroot", "orn", "og", "g_st")
        k.s5_in, k.s5_w, k.s5_tr, k.bc_s, k.args, k.tab = \
            sems("s5_in", "s5_w", "s5_tr", "bc_s", "args", "tab")
        k.bu, k.mod, k.dem, k.yp, k.ysum, k.y_st = \
            sems("bu", "mod", "dem", "yp", "ysum", "y_st")
        k.y_in, k.y_act, k.y_hi, k.y_lo, k.glu_ps, k.sig = \
            sems("y_in", "y_act", "y_hi", "y_lo", "glu_ps", "sig")
        k.zb_in0, k.zb_in1, k.gv0, k.gv1, k.gb_st0, k.gb_st1 = \
            sems("zb_in0", "zb_in1", "gv0", "gv1", "gb_st0", "gb_st1")
        k.ga_in, k.g_hi, k.g_lo, k.gate_ps, k.p_ps, k.gate_s = \
            sems("ga_in", "g_hi", "g_lo", "gate_ps", "p_ps", "gate_s")
        k.prod, k.mrg, k.m_hi, k.m_lo, k.o_ps, k.xr_in = \
            sems("prod", "mrg", "m_hi", "m_lo", "o_ps", "xr_in")
        k.fg_in, k.h_s, k.h_sq, k.fin, k.o_st = \
            sems("fg_in", "h_s", "h_sq", "fin", "o_st")

        block = ctx.enter_context(nc.Block())

        @block.sync
        def _(sp):
            k.sp = sp
            sync_program(k, sp)

        @block.gpsimd
        def _(pool):
            pool_program(k, pool)

        @block.scalar
        def _(act):
            scalar_program(k, act)

        @block.vector
        def _(dve):
            vector_program(k, dve)

        @block.tensor
        def _(pe):
            tensor_program(k, pe)


B_XA = 0
B_MIX = B_XA + 8 * XH
B_GLU = B_MIX + 6 * HEADS
B_BR = B_GLU + KW
B_OUT = B_BR + 3 * 24
N_BLOCKS = B_OUT + 16


def end_phase(k, e, n):
    e.drain().then_inc(k.phase_end, 1)
    e.wait_ge(k.phase_end, 4 * n)



def load_halves(k, sp, w0, per, j, sources):
    slot = w0 % 2
    wait_apart(k, sp, k.w_lo, count(j, w0 - 1, per))
    for half, src in enumerate(sources):
        n = src.shape[1]
        dst = k.raw[slot][:, half * 1024:(half + 1) * 1024].rearrange("p (k c) -> p k c", k=n)
        sp.dma_start(dst, src).then_inc(k.w_in_slot[slot], 16)


def columns(w, c, n=P):
    return w[:, bass.ds(c, n)].rearrange("(k p) c -> p k c", p=P)


def load_fm(k, sp, w0, per, j, w, c):
    v = columns(w, c)
    load_halves(k, sp, w0, per, j, [v[:, 0:8, :], v[:, 8:16, :]])


def load_fm8(k, sp, w0, per, j, w, c, c2):
    load_halves(k, sp, w0, per, j, [columns(w, c), columns(w, c2)])


def load_tm(k, sp, w0, per, j, w, rows, c):
    v = columns(w, c, S)
    load_halves(k, sp, w0, per, j, [v[:, rows:rows + 2, :], v[:, rows + 2:rows + 4, :]])


def split_hi(k, act, w0, per=0, j=(0, 0)):
    slot = w0 % 2
    wait(act, k.w_in_slot[slot], count(j, 32 * (w0 // 2 + 1), 16 * per))
    wait(act, k.w_used, count(j, w0 - 1, per))
    act.activation(k.wh[slot][:, :], k.raw[slot][:, :], ACT.Copy).then_inc(k.w_hi, 1)


def split_lo(k, dve, w0, per=0, j=(0, 0)):
    slot = w0 % 2
    wait(dve, k.w_hi, count(j, w0 + 1, per))
    wait(dve, k.w_used, count(j, w0 - 1, per))
    dve.tensor_tensor(k.wl[slot][:, :], k.raw[slot][:, :], k.wh[slot][:, :].bitcast(F32),
                      ALU.subtract).then_inc(k.w_lo, 1)


def mm3(pe, o, ah, al, bh, bl, start, stop):
    pe.matmul(o, ah, bh, start=start, stop=False)
    pe.matmul(o, ah, bl, start=False, stop=False)
    return pe.matmul(o, al, bh, start=False, stop=stop)


def row_tiles(k, pe, slot, o, tiles, at_tile, acth, actl, n_tiles):
    for n, t in enumerate(tiles):
        a = bass.ts(at_tile + n, P)
        mm = mm3(pe, o, k.wh[slot][:, a], k.wl[slot][:, a], acth[:, t, :], actl[:, t, :],
                 t == 0, t == n_tiles - 1)
    return mm


def quarter(k, pe, w0, per, j, q, acth, actl, n, outs, before):
    slot = w0 % 2
    if q == 0:
        wait(pe, k.w_lo, count(j, w0 + 1, per))
        wait(pe, outs, count(j, w0 - before - 1, per))
    mm = row_tiles(k, pe, slot, k.ps[slot][:, 0:n], range(4 * q, 4 * q + 4), 4 * q, acth, actl, KD)
    if q == 3:
        mm.then_inc(k.w_used, 1)


def sync_program(k, sp):
    sp.dma_start(k.cst[:, :], k.consts).then_inc(k.cst_in, 16)
    for m in range(NT):
        sp.dma_start(k.xs[:, m, :], k.x[m * P:(m + 1) * P, :]).then_inc(k.x_in, 16)
    sp.wait_ge(k.rows_zero, 1)
    sp.dma_start(k.rows1[0:96, :], k.conv_w.rearrange("j (t c) -> (j t) c", c=P)).then_inc(k.rows_in, 16)
    sp.dma_start(k.rows1[96:112, :], k.norm_g.rearrange("(t c) -> t c", c=P)).then_inc(k.rows_in, 16)
    sp.dma_start(k.rows1[112:128, :], k.mem_g.rearrange("(t c) -> t c", c=P)).then_inc(k.rows_in, 16)
    sp.dma_start(k.rows2[0:32, :], k.lam_re.rearrange("(q g) s -> q (g s)", g=2)).then_inc(k.rows_in, 16)
    sp.dma_start(k.rows2[32:64, :], k.lam_im.rearrange("(q g) s -> q (g s)", g=2)).then_inc(k.rows_in, 16)
    sp.dma_start(k.rows2[96:104, :], k.s5_d.rearrange("(t c) -> t c", c=P)).then_inc(k.rows_in, 16)
    sp.dma_start(k.rows2[104:105, :], k.gdn_g.rearrange("(t c) -> t c", c=P)).then_inc(k.rows_in, 16)
    sp.dma_start(k.ldt2[64:96, :], k.log_dt.rearrange("(q g) -> q g", g=2)).then_inc(k.rows_in, 16)
    sp.dma_start(k.alog_b[:, :], k.a_log.partition_broadcast(P)).then_inc(k.rows_in, 16)
    sp.dma_start(k.dtb_b[:, :], k.dt_bias.partition_broadcast(P)).then_inc(k.rows_in, 16)
    sp.dma_start(k.wba[:, :].rearrange("p (k c) -> p k c", c=16), columns(k.w_in, BA0, 16)).then_inc(k.wba_in, 16)
    sp.wait_ge(k.x_tr, KD)
    for m in range(MT):
        sp.dma_start(k.xs[:, m, :], k.mem[m * P:(m + 1) * P, :]).then_inc(k.mem_in, 16)

    def attention_loads(j):
        for b, (w, c0) in enumerate(((k.w_kv, 0), (k.w_kv, W), (k.w_in, QC0), (k.w_in, ZC0))):
            for t in range(2):
                load_fm(k, sp, B_XA + 2 * b + t, 8, j, w, count(j, c0 + t * P, 2 * P))
    attention_loads((0, 0))
    with sp.Fori(1, XH) as i:
        attention_loads((i, 0))

    def mixer_loads(j):
        for b, c0 in enumerate(MIX_COLS):
            load_fm(k, sp, B_MIX + b, 6, j, k.w_in, count(j, c0, P))

    def s5_loads(j):
        wait_apart(k, sp, k.s5_w, count(j, 0, 12))
        for n, b in enumerate((k.b_re, k.b_im)):
            sp.dma_start(k.braw[:, n, :, :], b[bass.ds(count(j, 0, 8), 8)].rearrange("(q g) s i -> (g s) q i", g=2)).then_inc(k.s5_in, 16)
        for n, c in enumerate((k.c_re, k.c_im)):
            sp.dma_start(k.craw[:, n, :], c[bass.ds(count(j, 0, 8), 8)].rearrange("g i s -> (g i) s")).then_inc(k.s5_in, 16)

    mixer_loads((0, 0))
    sp.wait_ge(k.phase_end, 8)
    s5_loads((0, 0))
    with sp.Fori(1, HEADS) as i:
        mixer_loads((i, 0))
        s5_loads((i, 0))

    with sp.Fori(0, KW // 2) as i:
        for t in range(2):
            c = count((i, 0), t * P, 2 * P)
            load_fm8(k, sp, B_GLU + t, 2, (i, 0), k.w_glu, c, c + W)

    for br, w in enumerate(k.branch_w):
        gate0 = G0 + (2, 1, 0)[br] * D
        with sp.Fori(0, KD // 4) as i:
            j = (i, 0)
            for pair in range(2):
                b = B_BR + 24 * br + 3 * pair
                c = count(j, 2 * pair * P, 4 * P)
                load_fm(k, sp, b, 6, j, k.w_in, c + gate0)
                load_fm(k, sp, b + 1, 6, j, k.w_in, c + (gate0 + P))
                load_fm8(k, sp, b + 2, 6, j, w, c, c + P)

    with sp.Fori(0, 4) as i:
        for kb in range(4):
            load_tm(k, sp, B_OUT + kb, 4, (i, 0), k.w_out, 4 * kb, i * S)


MIX_COLS = (Q0, K0, V0, ZB0, ZA0, XB0)


def pool_program(k, pool):
    pool.memset(k.rows2[:, :], 0.0).then_inc(k.rows_zero, 1)
    end_phase(k, pool, 1)

    def attention_store(j):
        for t in range(2):
            wait_apart(k, pool, k.xa_og, count(j, t + 1, 2))
            pool.dma_start(k.gated_d[0][bass.ds(count(j, t * P, 2 * P), P), :], k.ox[:, t, :]).then_inc([k.xa_st0, k.xa_st1][t], 16)
    with pool.Fori(0, XH) as i:
        attention_store((i, 0))
    pool.wait_ge(k.xa_st0, 16 * XH)
    pool.wait_ge(k.xa_st1, 16 * XH)
    end_phase(k, pool, 2)

    for t in (k.qraw, k.kraw, k.vraw):
        pool.memset(t[:, 0:3], 0.0).then_inc(k.pad_zero, 1)
    pool.memset(k.bpad[:, :, :, :, :], 0.0).then_inc(k.pad_zero, 1)

    def mixer(j):
        h, f = at(j), at(j)
        tcos, tsin, gr, gi = [k.tcos0, k.tcos1], [k.tsin0, k.tsin1], [k.gr0, k.gr1], [k.gi0, k.gi1]

        def arguments(q):
            hi_, lo_ = k.s5h[:, 1, q:q + 1], k.s5h[:, 2, q:q + 1]
            n = count(j, 7 * q, 28)
            if q == 0:
                wait_apart(k, pool, k.sliced, count(j, 4, 4))
            wait_apart(k, pool, k.tab, count(j, 3 * q, 12))
            ts, tt = pool.tensor_scalar, pool.tensor_tensor
            ts(k.karg[:, :], k.tvec, hi_, ROUND, ALU.mult, ALU.add).then_inc(k.args, 1)
            ts(k.farg[:, :], k.tvec, hi_, None, ALU.mult).then_inc(k.args, 1)
            wait_apart(k, pool, k.args, n + 1)
            ts(k.karg[:, :], k.karg[:, :], -ROUND, None, ALU.add).then_inc(k.args, 1)
            wait_apart(k, pool, k.args, n + 3)
            tt(k.farg[:, :], k.farg[:, :], k.karg[:, :], ALU.subtract).then_inc(k.args, 1)
            wait_apart(k, pool, k.args, n + 4)
            ts(k.karg[:, :], k.tvec, lo_, None, ALU.mult).then_inc(k.args, 1)
            wait_apart(k, pool, k.args, n + 5)
            tt(k.farg[:, :], k.farg[:, :], k.karg[:, :], ALU.add).then_inc(k.args, 1)
            wait_apart(k, pool, k.args, n + 6)
            ts(k.farg[:, :], k.farg[:, :], 0.4999999, -0.4999999, ALU.min, ALU.max).then_inc(k.args, 1)

        def turn_back(q):
            c, s, a, b = tcos[q % 2], tsin[q % 2], gr[q % 2], gi[q % 2]
            n = count(j, 6 * q, 24)
            wait_apart(k, pool, k.mod, count(j, 8 * q + 8, 32))
            wait_apart(k, pool, k.yp, count(j, q, 4))
            for o, (c1, c2, op) in ((k.hr, (c, s, ALU.subtract)), (k.hi, (s, c, ALU.add))):
                pool.tensor_tensor(o[:, :], c1[:, :], a[:, :], ALU.mult).then_inc(k.dem, 1)
                pool.tensor_tensor(k.pt[:, :], c2[:, :], b[:, :], ALU.mult).then_inc(k.dem, 1)
                wait_apart(k, pool, k.dem, n + 2)
                pool.tensor_tensor(o[:, :], o[:, :], k.pt[:, :], op).then_inc(k.dem, 1)
                wait_apart(k, pool, k.dem, n + 3)
                n = n + 3

        def masks():
            wait_apart(k, pool, k.dec, count(j, 2, 2))
            pool.tensor_tensor(k.dl[:, :, :], k.dl[:, :, :],
                               k.mat["strict"].unsqueeze(1).to_broadcast([P, NT, P]), ALU.mult).then_inc(k.pm, 1)
            wait_apart(k, pool, k.pm, count(j, 1, 4))
            pool.tensor_tensor(k.dl[:, :, :], k.dl[:, :, :],
                               k.hph[:, 0, :].unsqueeze(2).to_broadcast([P, NT, P]), ALU.mult).then_inc(k.pm, 1)
            wait_apart(k, pool, k.qk, count(j, 2, 2))
            pool.tensor_tensor(k.qd[:, :, :], k.qc[:, :].rearrange("p (n c) -> p n c", n=NT), k.er[:, :, :],
                               ALU.mult).then_inc(k.pm, 1)
            wait_apart(k, pool, k.kb, count(j, 2, 2))
            pool.tensor_tensor(k.du[:, :, :], k.du[:, :, :],
                               k.mat["upper"].unsqueeze(1).to_broadcast([P, NT, P]), ALU.mult).then_inc(k.pm, 1)

        arguments(0)
        arguments(1)
        turn_back(0)
        masks()
        arguments(2)
        turn_back(1)
        arguments(3)
        turn_back(2)
        turn_back(3)
        wait_apart(k, pool, k.ysum, count(j, 1, 1))
        pool.dma_start(k.y_d[bass.ds(f * P, P), :], k.ma[:, :]).then_inc(k.y_st, 16)
        wait_apart(k, pool, k.og, count(j, 2, 2))
        pool.dma_start(k.gated_d[2][bass.ds(h * P, P), :],
                       k.gx[:, :, :].rearrange("p n c -> p (n c)")).then_inc(k.g_st, 16)

    def gate_store(j):
        wait_apart(k, pool, k.mx_out, count(j, 4, 6))
        pool.dma_start(k.zb_d[bass.ds(at(j) * P, P), :], k.zbs[:, :]).then_inc(k.zb_st, 16)

    gate_store((0, 0))
    mixer((0, 0))
    gate_store((1, 0))
    with pool.Fori(2, HEADS) as i:
        mixer((i, -1))
        gate_store((i, 0))
    mixer((HEADS, -1))
    pool.wait_ge(k.zb_st, 16 * HEADS)
    pool.wait_ge(k.y_st, 16 * HEADS)
    pool.wait_ge(k.g_st, 16 * HEADS)
    end_phase(k, pool, 3)

    pool.dma_start(k.yst[:, :, :], k.y_d.rearrange("(t p) s -> p t s", p=P)).then_inc(k.y_in, 16)

    def glu(j):
        for t in range(2):
            zv, gg = [k.zv0, k.zv1][t], [k.gg0, k.gg1][t]
            row = count(j, t * P, 2 * P)
            wait_apart(k, pool, [k.gv0, k.gv1][t], count(j, 0, 2))
            pool.dma_start(zv[:, :], k.zb_d[bass.ds(row, P), :]).then_inc([k.zb_in0, k.zb_in1][t], 16)
            wait_apart(k, pool, [k.gv0, k.gv1][t], count(j, 2, 2))
            pool.dma_start(k.gated_d[1][bass.ds(row, P), :], gg[:, :]).then_inc([k.gb_st0, k.gb_st1][t], 16)
    glu((0, 0))
    with pool.Fori(1, KW // 2) as i:
        glu((i, 0))
    pool.wait_ge(k.gb_st0, 8 * KW)
    pool.wait_ge(k.gb_st1, 8 * KW)
    end_phase(k, pool, 4)

    for br in range(3):
        wait(pool, k.g_lo, KW * br)
        pool.dma_start(k.gst[:, :, :], k.gated_d[br].rearrange("(t p) s -> p t s", p=P)).then_inc(k.ga_in, 16)
    end_phase(k, pool, 5)

    pool.dma_start(k.fg[:, :], k.final_g.partition_broadcast(P)).then_inc(k.fg_in, 16)
    x_v = k.x.rearrange("(m p) c -> p m c", p=P)
    for c in range(4):
        for m in range(NT):
            wait(pool, k.h_s, 4 * (c - 1) + m + 1)
            pool.dma_start(k.xr[:, m, :], x_v[:, m, c * S:(c + 1) * S]).then_inc(k.xr_in, 16)
    for m in range(NT):
        pool.wait_ge(k.fin, m + 1)
        pool.dma_start(k.out[m * P:(m + 1) * P, :], k.hrow[:, m, :]).then_inc(k.o_st, 16)
    pool.wait_ge(k.o_st, 16 * NT)


def tensor_program(k, pe):
    ps, mat = k.ps, k.mat
    ident, ones = mat["ident"], mat["ones"]

    pe.wait_ge(k.cst_in, 16)
    pe.wait_ge(k.rows_in, 160)
    pe.wait_ge(k.ldt_rows, 1)
    pe.transpose(ps[4][:, 0:P], k.rows1[:, :], ident).then_inc(k.prm_ps, 1)
    pe.transpose(ps[5][:, 0:P], k.rows2[:, :], ident).then_inc(k.prm_ps, 1)
    for t in range(KD):
        pe.wait_ge(k.x_scale, NT)
        wait(pe, k.u_f32, t - 3)
        for m in range(NT):
            mm = pe.transpose(ps[t % 4][:, m * P:(m + 1) * P], k.xs[:, m, t * P:(t + 1) * P], ident)
        mm.then_inc(k.x_tr, 1)
    pe.wait_ge(k.u_lo, KD)
    pe.wait_ge(k.wba_lo, 1)
    for m in range(NT):
        for t in range(KD):
            a = bass.ts(m, P)
            mm = mm3(pe, ps[6][:, m * 16:(m + 1) * 16], k.uh[:, t, a], k.ul[:, t, a],
                     k.wbah[:, t * 16:(t + 1) * 16], k.wbal[:, t * 16:(t + 1) * 16], t == 0, t == KD - 1)
    mm.then_inc(k.ba_ps, 1)
    for t in range(KD):
        pe.wait_ge(k.x_scale, NT + MT)
        pe.wait_ge(k.u_f32, KD + t - 3)
        for m in range(MT):
            mm = pe.transpose(ps[t % 4][:, m * P:(m + 1) * P], k.xs[:, m, t * P:(t + 1) * P], ident)
        mm.then_inc(k.x_tr, 1)
    pe.wait_ge(k.g_done, 1)
    pe.matmul(ps[7][:, 0:NT * HEADS], mat["upper"], k.hp[:, 3, :, :], start=True, stop=True).then_inc(k.gsum_ps, 1)
    end_phase(k, pe, 1)

    def at_big(j, b, acts=None):
        hl, n = ((k.uh, k.ul), S) if b >= 4 else ((k.mh, k.ml), MEM)
        for q in range(4):
            quarter(k, pe, B_XA + b, 8, j, q, *hl, n, k.xa_out, 0)

    def at_values(j):
        pe.wait_ge(k.xa_out, count(j, 8, 8))
        wait(pe, k.xa_og, count(j, 0, 2))
        for m in range(MT):
            for t in range(2):
                mm = pe.transpose(ps[2][:, (2 * m + t) * P:(2 * m + t + 1) * P], k.vt[:, t, m * P:(m + 1) * P], ident)
        mm.then_inc(k.xa_vtr, 1)

    def at_scores(j, m):
        wait(pe, k.xa_exp, count(j, m - 1, 4))
        for t in range(2):
            mm = pe.matmul(ps[4 + m % 2][:, 0:MEM], k.qx[:, t, m * P:(m + 1) * P], k.kt[:, t, :], start=t == 0, stop=t == 1)
        mm.then_inc(k.xa_sc, 1)

    def at_turn(j, n):
        pe.wait_ge(k.xa_p, count(j, 4, 4))
        wait(pe, k.xa_pt, count(j, n, 2))
        for m in range(NT):
            mm = pe.transpose(ps[6 + n][:, m * P:(m + 1) * P], k.px[:, m, n * P:(n + 1) * P], ident)
        mm.then_inc(k.xa_ptr, 1)

    def at_output(j, t):
        pe.wait_ge(k.xa_v, count(j, 1, 1))
        pe.wait_ge(k.xa_pt, count(j, 2, 2))
        wait(pe, k.xa_og, count(j, t, 2))
        for m in range(MT):
            mm = pe.matmul(ps[2 + t][:, :], k.vx[:, m, t * P:(t + 1) * P], k.ptx[:, m, :], start=m == 0, stop=m == MT - 1)
        mm.then_inc(k.xa_o, 1)

    def at_small(j, n):
        if n == 0:
            at_values(j)
            at_scores(j, 0)
            at_scores(j, 1)
        if n == 1:
            at_scores(j, 2)
            at_scores(j, 3)
        if n in (2, 3):
            at_turn(j, n - 2)
        if n == 4:
            at_output(j, 0)
            at_output(j, 1)

    for b in range(8):
        at_big((0, 0), b)
    for b in range(8):
        at_small((0, 0), b)
        at_big((1, 0), b)
    with pe.Fori(2, XH) as i:
        for b in range(8):
            at_small((i, -1), b)
            at_big((i, 0), b)
    for n in range(5):
        at_small((XH, -1), n)
    end_phase(k, pe, 2)

    def big(j, b, *quarters):
        for q in quarters:
            quarter(k, pe, B_MIX + b, 6, j, q, k.uh, k.ul, S, k.mx_out, B_MIX)

    def chunks(t):
        return t[:, :].rearrange("p (n c) -> p n c", n=NT)

    def norms(j):
        pe.wait_ge(k.sq, count(j, 2, 2))
        wait(pe, k.og, count(j, 0, 2))
        pe.matmul(ps[2][:, :], ones, k.rq[:, :], start=True, stop=True)
        wait(pe, k.oroot, count(j, 0, 1))
        pe.matmul(ps[6][:, :], ones, k.rk[:, :], start=True, stop=True).then_inc(k.ss, 1)
        pe.wait_ge(k.gu, count(j, 1, 1))
        wait(pe, k.st_s, count(j, 0, 3))
        pe.matmul(ps[7][:, :], ones, k.gx[:, :, :], start=True, stop=True).then_inc(k.rsum, 1)

    def values(j):
        pe.wait_ge(k.silu, count(j, 3, 3))
        pe.wait_ge(k.root, count(j, 2, 2))
        for n in range(NT):
            mm = pe.transpose(ps[2][:, n * P:(n + 1) * P], k.vc[:, n * P:(n + 1) * P], ident)
        mm.then_inc(k.vtr, 1)

    def keys(j):
        pe.wait_ge(k.qk, count(j, 1, 2))
        for n in range(NT):
            mm = pe.transpose(ps[6][:, n * P:(n + 1) * P], k.kc[:, n * P:(n + 1) * P], ident)
        mm.then_inc(k.ktr, 1)

    def keys_keys(j):
        pe.wait_ge(k.er_s, count(j, 1, 1))
        pe.wait_ge(k.dd, count(j, 1, 3))
        for n in range(NT):
            c = bass.ts(n, P)
            mm = pe.matmul(ps[7][:, c], k.kc[:, c], k.kc[:, c], start=True, stop=True)
        mm.then_inc(k.kk, 1)

    def keys_queries(j):
        pe.wait_ge(k.qk, count(j, 2, 2))
        pe.wait_ge(k.vb_s, count(j, 1, 1))
        for n in range(NT):
            c = bass.ts(n, P)
            mm = pe.matmul(ps[2][:, c], k.kc[:, c], k.qc[:, c], start=True, stop=True)
        mm.then_inc(k.kq, 1)

    def turn_lower(j):
        pe.wait_ge(k.lm, count(j, 1, 1))
        pe.wait_ge(k.kb, count(j, 2, 2))
        for n in range(NT):
            mm = pe.transpose(ps[6][:, n * P:(n + 1) * P], k.dl[:, n, :], ident)
        mm.then_inc(k.ltr, 1)

    def level_x(j, l):
        pe.wait_ge(k.lt_s, count(j, 1, 1))
        if l == 1:
            pe.wait_ge(k.tu_s, count(j, 4, 4))
            pe.wait_ge(k.qkt, count(j, 1, 1))
        else:
            pe.wait_ge(k.tus, count(j, 2 * (l - 1), 11))
        for n in range(NT):
            mm = pe.matmul(ps[2][:, n * P:(n + 1) * P], k.lt[:, n, :], k.tl[:, n, :], start=True, stop=True)
        mm.then_inc(k.lx, 1)

    def level_p(j, l):
        pe.wait_ge(k.xm, count(j, l, 6))
        for n in range(NT):
            c = bass.ts(n, P)
            if l < 6:
                pe.matmul(ps[6][:, c], k.tu[:, n, :], k.gx[:, n, :], start=True, stop=True)
            mm = pe.matmul(ps[7][:, c], k.gx[:, n, :], k.tu[:, n, :], start=True, stop=True)
        mm.then_inc(k.lp, 1)

    def weights(j):
        pe.wait_ge(k.tus, count(j, 11, 11))
        for n in range(NT):
            mm = pe.matmul(ps[2][:, n * P:(n + 1) * P], k.kbg[:, n, :], k.tu[:, n, :], start=True, stop=True)
        mm.then_inc(k.wt, 1)

    def new_values(j, n):
        if n == 0:
            pe.wait_ge(k.wtn, count(j, 1, 1))
        else:
            pe.wait_ge(k.st_s, count(j, n, 3))
        pe.wait_ge(k.vn_s, count(j, n, 4)) if n else None
        c = bass.ts(n, P)
        mm = pe.matmul(ps[6][:, c], k.tu[:, n, :], k.vb[:, n, :], start=True, stop=n == 0)
        if n:
            mm = pe.matmul(ps[6][:, c], k.dl[:, n, :], k.st[:, :], start=False, stop=True)
        mm.then_inc(k.vp, 1)

    def chunk_output(j, n):
        pe.wait_ge(k.vn_s, count(j, n + 1, 4))
        c = bass.ts(n, P)
        if n < NT - 1:
            pe.matmul(ps[7][:, 0:P], k.kd[:, n, :], k.vn[:, n, :], start=True, stop=True).then_inc(k.sp_s, 1)
        if n == 0:
            pe.wait_ge(k.pm, count(j, 4, 4))
            pe.wait_ge(k.qkt, count(j, 1, 1))
        mm = pe.matmul(ps[2][:, c], k.vn[:, n, :], k.du[:, n, :], start=True, stop=n == 0)
        if n:
            mm = pe.matmul(ps[2][:, c], k.st[:, :], k.qd[:, n, :], start=False, stop=True)
        mm.then_inc(k.op, 1)

    def output_norm(j):
        pe.wait_ge(k.osq, count(j, 1, 1))
        pe.matmul(ps[6][:, :], ones, k.rk[:, :], start=True, stop=True).then_inc(k.sso, 1)

    def s5_matrices(j):
        pe.wait_ge(k.s5_w, count(j, 12, 12))
        wait(pe, k.ysum, count(j, 0, 1))
        for n, t in enumerate((k.bpad[:, 0], k.bpad[:, 1])):
            pe.transpose(ps[5][:, n * P:(n + 1) * P], t.rearrange("p q g i -> p (q g i)"), ident)
        for n in range(2):
            mm = pe.transpose(ps[5][:, (2 + n) * P:(3 + n) * P], k.cpad[:, n].rearrange("p g s -> p (g s)"), ident)
        mm.then_inc(k.s5_tr, 1)

    def s5_inputs(j, q):
        pe.wait_ge(k.bc_s, count(j, 1, 1))
        pe.wait_ge(k.mx_out, count(j, 6, 6))
        wait(pe, k.mod, count(j, 8 * q - 2, 32))
        r = slice(32 * q, 32 * q + 32)
        pe.matmul(ps[3][:, :], k.bc[r, 0, :], k.xb[r, :], start=True, stop=True)
        pe.matmul(ps[4][:, :], k.bc[r, 1, :], k.xb[r, :], start=True, stop=True).then_inc(k.bu, 1)

    def s5_outputs(j, q):
        pe.wait_ge(k.dem, count(j, 6 * q + 6, 24))
        r = slice(32 * q, 32 * q + 32)
        pe.matmul(ps[5][r, :], k.bc[:, 2, r], k.hr[:, :], start=True, stop=False)
        pe.matmul(ps[5][r, :], k.bc[:, 3, r], k.hi[:, :], start=False, stop=True).then_inc(k.yp, 1)

    def mixer(a, j):
        if a: big(a, 0, 0)
        if j: s5_matrices(j); s5_inputs(j, 0)
        if a: big(a, 0, 1, 2, 3)
        if j: norms(j)
        if a: big(a, 1, 0)
        if j: s5_inputs(j, 1); s5_outputs(j, 0)
        if a: big(a, 1, 1)
        if j: values(j)
        if a: big(a, 1, 2, 3)
        if j: keys(j); keys_keys(j)
        if a: big(a, 2, 0)
        if j: keys_queries(j); s5_inputs(j, 2); s5_outputs(j, 1)
        if a: big(a, 2, 1)
        if j: turn_lower(j)
        if a: big(a, 2, 2)
        if j: level_x(j, 1)
        if a: big(a, 2, 3)
        if j: level_p(j, 1)
        if a: big(a, 3, 0)
        if j: level_x(j, 2); s5_inputs(j, 3); s5_outputs(j, 2)
        if a: big(a, 3, 1)
        if j: level_p(j, 2)
        if a: big(a, 3, 2)
        if j: level_x(j, 3)
        if a: big(a, 3, 3)
        if j: level_p(j, 3)
        if a: big(a, 4, 0)
        if j: level_x(j, 4); s5_outputs(j, 3)
        if a: big(a, 4, 1)
        if j: level_p(j, 4)
        if a: big(a, 4, 2)
        if j: level_x(j, 5)
        if a: big(a, 4, 3)
        if j: level_p(j, 5)
        if a: big(a, 5, 0)
        if j: level_x(j, 6)
        if a: big(a, 5, 1)
        if j: level_p(j, 6); weights(j)
        if a: big(a, 5, 2)
        if j: new_values(j, 0); chunk_output(j, 0); new_values(j, 1); chunk_output(j, 1)
        if a: big(a, 5, 3)
        if j: new_values(j, 2); chunk_output(j, 2); new_values(j, 3); chunk_output(j, 3); output_norm(j)

    mixer((0, 0), None)
    mixer((1, 0), (0, 0))
    with pe.Fori(2, HEADS) as i:
        mixer((i, 0), (i, -1))
    mixer(None, (HEADS, -1))
    end_phase(k, pe, 3)

    def glu(j):
        for t in range(2):
            wait(pe, k.w_lo, count(j, B_GLU + t + 1, 2))
            wait(pe, [k.gv0, k.gv1][t], count(j, 0, 2))
            if t == 0:
                pe.wait_ge(k.y_lo, KW)
            row_tiles(k, pe, t, ps[t][:, :], range(KW), 0, k.gh, k.gl, KW)
            row_tiles(k, pe, t, ps[2 + t][:, :], range(KW), KW, k.gh, k.gl, KW).then_inc(k.w_used, 1)

    glu((0, 0))
    with pe.Fori(1, KW // 2) as i:
        glu((i, 0))
    end_phase(k, pe, 4)

    def merge(br, j):
        for pair in range(2):
            b0 = B_BR + 24 * br + 3 * pair
            for n in range(2):
                d = 2 * pair + n
                wait(pe, k.w_lo, count(j, b0 + n + 1, 6))
                wait(pe, k.gate_s, count(j, 16 * br + d - 3, 4))
                row_tiles(k, pe, (b0 + n) % 2, ps[d][:, :], range(KD), 0, k.uh, k.ul, KD).then_inc(k.w_used, 1)
            wait(pe, k.w_lo, count(j, b0 + 3, 6))
            if pair == 0:
                pe.wait_ge(k.g_lo, KW * (br + 1))
            for n in range(2):
                d = 2 * pair + n
                wait(pe, k.prod, count(j, 16 * br + d - 3, 4))
                mm = row_tiles(k, pe, b0 % 2, ps[4 + d][:, :], range(KW), n * KW, k.gh, k.gl, KW)
                mm.then_inc(k.w_used if n else k.p_ps, 1)

    for br in range(3):
        merge(br, (0, 0))
        with pe.Fori(1, KD // 4) as i:
            merge(br, (i, 0))
    end_phase(k, pe, 5)

    for c in range(4):
        for kb in range(4):
            b = B_OUT + 4 * c + kb
            slot = b % 2
            pe.wait_ge(k.w_lo, b + 1)
            if kb == 0:
                wait(pe, k.h_s, 4 * (c - 1))
            for m in range(NT):
                for n in range(4):
                    t = 4 * kb + n
                    if m == 0 and c == 0:
                        pe.wait_ge(k.m_lo, t + 1)
                    a, w = bass.ts(m, P), bass.ts(n, S)
                    mm = mm3(pe, ps[4 * (c % 2) + m][:, :], k.uh[:, t, a], k.ul[:, t, a],
                             k.wh[slot][:, w], k.wl[slot][:, w], t == 0, t == KD - 1)
                if kb == 3 and m < 3:
                    mm.then_inc(k.o_ps, 1)
            mm.then_inc(k.w_used, 1)


def scalar_program(k, act):
    ps, col = k.ps, k.col

    done = [0]

    def step(instruction):
        instruction.then_inc(k.alink, 1)
        done[0] += 1
        act.wait_ge(k.alink, done[0])

    act.wait_ge(k.cst_in, 16)
    act.wait_ge(k.x_in, 16 * NT)
    for m in range(NT):
        step(act.activation(k.junk[:, :], k.xs[:, m, :], ACT.Square, accum_out=k.stat[:, m:m + 1]))
    act.activation(k.stat[:, 8:12], k.stat[:, 0:4], ACT.Sqrt, bias=col["eps"], scale=1 / D).then_inc(k.x_root, 1)

    def tile_hi(hi, t, n):
        act.wait_ge(k.u_f32, t + 1)
        act.activation(hi, [k.ut0, k.ut1][t % 2][:, 0:n], ACT.Copy).then_inc(k.u_hi, 1)

    for t in range(KD):
        tile_hi(k.uh[:, t, :], t, S)
    act.wait_ge(k.wba_in, 16)
    act.activation(k.wbah[:, :], k.wba[:, :], ACT.Copy).then_inc(k.wba_hi, 1)
    act.wait_ge(k.mem_in, 16 * MT)
    for m in range(MT):
        step(act.activation(k.junk[:, :], k.xs[:, m, :], ACT.Square, accum_out=k.stat[:, 4 + m:5 + m]))
    act.activation(k.stat[:, 12:14], k.stat[:, 4:6], ACT.Sqrt, bias=col["eps"], scale=1 / D).then_inc(k.x_root, 1)
    for t in range(KD):
        tile_hi(k.mh[:, t, :], KD + t, MEM)
    tp = k.tp
    act.wait_ge(k.prm, 2)
    act.activation(tp[:, 0, :], k.prm2[:, 64:96], ACT.Exp).then_inc(k.p_act, 1)
    act.wait_ge(k.p_dve, 1)
    act.activation(tp[:, 2, :], tp[:, 1, :], ACT.Exp).then_inc(k.p_act, 1)
    act.wait_ge(k.p_dve, 2)
    step(act.activation(tp[:, 4, :], tp[:, 3, :], ACT.Sin, scale=TWO_PI))
    step(act.activation(tp[:, 5, :], tp[:, 3, :], ACT.Abs))
    act.activation(tp[:, 5, :], tp[:, 5, :], ACT.Sin, scale=-TWO_PI, bias=col["quarter"]).then_inc(k.p_act, 1)
    act.wait_ge(k.ba_ps, 1)
    ba = ps[6][:, 0:NT * 16].rearrange("p (m c) -> p m c", m=NT)
    act.activation(k.hp[:, 0, :, :], ba[:, :, 0:HEADS], ACT.Exp, scale=-1.0).then_inc(k.p_act, 1)
    act.wait_ge(k.p_dve, 3)
    step(act.activation(k.hp[:, 2, :, :], k.hp[:, 1, :, :], ACT.Abs))
    step(act.activation(k.hp[:, 2, :, :], k.hp[:, 2, :, :], ACT.Exp, scale=-1.0))
    act.activation(k.alog_b[:, :], k.alog_b[:, :], ACT.Exp).then_inc(k.p_act, 1)
    act.wait_ge(k.p_dve, 4)
    act.activation(k.hp[:, 2, :, :], k.hp[:, 2, :, :], ACT.Ln).then_inc(k.p_act, 1)
    act.wait_ge(k.gsum_ps, 1)
    act.activation(k.hp[:, 2, :, :], ps[7][:, 0:NT * HEADS].rearrange("p (m h) -> p m h", m=NT), ACT.Exp).then_inc(k.p_act, 1)
    split_hi(k, act, B_XA)
    end_phase(k, act, 1)

    def at_exp(j, m):
        act.wait_ge(k.xa_max, count(j, 2 * m + 2, 8))
        wait(act, k.xa_ptr, count(j, 0, 2))
        act.activation(k.px[:, m, :], ps[4 + m % 2][:, 0:MEM], ACT.Exp, bias=k.stat[:, 24 + m:25 + m],
                       scale=1 / 16, accum_out=k.stat[:, 28 + m:29 + m]).then_inc(k.xa_exp, 1)

    def at_out(j, b):
        act.wait_ge(k.w_used, count(j, B_XA + b + 1, 8))
        o = ps[b % 2]
        if b < 2 or b in (4, 5):
            wait(act, k.xa_sc, count(j, 0, 4))
        elif b < 4:
            wait(act, k.xa_vtr, count(j, 0, 1))
        else:
            wait(act, k.xa_og, count(j, 0, 2))
        t = b % 2
        if b < 4:
            act.activation([k.kt, k.vt][b // 2][:, t, :], o[:, 0:MEM], ACT.Copy).then_inc(k.xa_out, 1)
        else:
            act.activation([k.qx, k.zx][b // 2 - 2][:, t, :], o[:, :], ACT.Copy if b < 6 else ACT.Silu).then_inc(k.xa_out, 1)

    def attention(a, j):
        for b in range(8):
            if a: split_hi(k, act, B_XA + b + 1, 8, a)
            if j and b < 2: at_exp(j, 2 * b); at_exp(j, 2 * b + 1)
            if a: at_out(a, b)

    attention((0, 0), None)
    attention((1, 0), (0, 0))
    with act.Fori(2, XH) as i:
        attention((i, 0), (i, -1))
    attention(None, (XH, -1))
    end_phase(k, act, 2)

    def tile_out(a, b):
        act.wait_ge(k.w_used, count(a, B_MIX + b + 1, 6))
        o = ps[b % 2]
        if b < 3:
            wait(act, k.conv, count(a, 4 * b + 4 - 12, 12))
            act.activation([k.qraw, k.kraw, k.vraw][b][:, 3:3 + S], o[:, :], ACT.Copy).then_inc(k.mx_out, 1)
        elif b == 3:
            wait(act, k.zb_st, count(a, 0, 16))
            act.activation(k.zbs[:, :], o[:, :], ACT.Silu).then_inc(k.mx_out, 1)
        elif b == 4:
            wait(act, k.og, count(a, 0, 2))
            act.activation(k.zs[:, :], o[:, :], ACT.Silu).then_inc(k.mx_out, 1)
        else:
            wait(act, k.ysum, count(a, 0, 1))
            wait(act, k.bu, count(a, 0, 4))
            act.activation(k.xb[:, :], o[:, :], ACT.Copy).then_inc(k.mx_out, 1)

    def s5_tables(j, q):
        c, s = [k.tcos0, k.tcos1][q % 2], [k.tsin0, k.tsin1][q % 2]
        n = count(j, 3 * q, 12)
        act.wait_ge(k.args, count(j, 7 * q + 7, 28))
        wait(act, k.dem, count(j, 6 * (q - 1), 24))
        wait(act, k.mod, count(j, 8 * (q - 1), 32))
        act.activation(s[:, :], k.farg[:, :], ACT.Sin, scale=TWO_PI).then_inc(k.tab, 1)
        act.activation(c[:, :], k.farg[:, :], ACT.Abs).then_inc(k.tab, 1)
        act.wait_ge(k.tab, n + 2)
        act.activation(c[:, :], c[:, :], ACT.Sin, scale=-TWO_PI, bias=col["quarter"]).then_inc(k.tab, 1)

    def s5_matrices(j):
        act.wait_ge(k.s5_tr, count(j, 1, 1))
        wait(act, k.yp, count(j, 0, 4))
        act.activation(k.bc[:, :, :], ps[5][:, :].rearrange("p (n c) -> p n c", n=4), ACT.Copy).then_inc(k.bc_s, 1)

    def activations(j):
        for n, (t, sq) in enumerate(((k.qc, k.rq), (k.kc, k.rk), (k.vc, None))):
            act.wait_ge(k.conv, count(j, 4 * n + 4, 12))
            act.activation(t[:, :], t[:, :], ACT.Silu).then_inc(k.silu, 1)
            if sq is not None:
                act.wait_ge(k.silu, count(j, n + 1, 3))
                wait(act, k.og, count(j, 0, 2))
                act.activation(sq[:, :], t[:, :], ACT.Square).then_inc(k.sq, 1)

    def roots(j):
        act.wait_ge(k.ss, count(j, 1, 1))
        act.activation(k.rq[:, :], ps[2][:, :], ACT.Sqrt, bias=col["eps128"], scale=float(P)).then_inc(k.root, 1)
        act.activation(k.rk[:, :], ps[6][:, :], ACT.Sqrt, bias=col["eps"]).then_inc(k.root, 1)
        act.wait_ge(k.rsum, count(j, 1, 1))
        act.activation(k.er[:, :, :], ps[7][:, :].rearrange("p (n c) -> p n c", n=NT), ACT.Exp).then_inc(k.er_s, 1)
        act.wait_ge(k.dd, count(j, 2, 3))
        act.activation(k.du[:, :, :], k.du[:, :, :], ACT.Exp).then_inc(k.dec, 1)
        act.wait_ge(k.dd, count(j, 3, 3))
        act.activation(k.dl[:, :, :], k.dl[:, :, :], ACT.Exp, scale=-1.0).then_inc(k.dec, 1)

    def lower_turned(j):
        act.wait_ge(k.ltr, count(j, 1, 1))
        wait(act, k.lx, count(j, 0, 6))
        act.activation(k.lt[:, :, :], ps[6][:, :].rearrange("p (n c) -> p n c", n=NT), ACT.Copy).then_inc(k.lt_s, 1)

    def recurrence(j):
        act.wait_ge(k.wt, count(j, 1, 1))
        act.activation(k.dl[:, :, :], ps[2][:, :].rearrange("p (n c) -> p n c", n=NT), ACT.Copy, scale=-1.0).then_inc(k.wtn, 1)
        for n in range(NT):
            act.wait_ge(k.vp, count(j, n + 1, 4))
            act.activation(k.vn[:, n, :], ps[6][:, n * P:(n + 1) * P], ACT.Copy).then_inc(k.vn_s, 1)
        act.wait_ge(k.op, count(j, 4, 4))
        act.activation(k.rk[:, :], ps[2][:, :], ACT.Square).then_inc(k.osq, 1)
        act.wait_ge(k.sso, count(j, 1, 1))
        act.activation(k.rk[:, :], ps[6][:, :], ACT.Sqrt, bias=col["eps"], scale=1 / P).then_inc(k.oroot, 1)

    def mixer(a, j):
        split = lambda b: split_hi(k, act, B_MIX + b + 1, 6, a)
        if a: split(0)
        if j: s5_matrices(j); s5_tables(j, 0); activations(j)
        if a: tile_out(a, 0); split(1)
        if j: s5_tables(j, 1); roots(j)
        if a: tile_out(a, 1); split(2)
        if j: s5_tables(j, 2); lower_turned(j)
        if a: tile_out(a, 2); split(3)
        if j: s5_tables(j, 3)
        if a: tile_out(a, 3); split(4); split(5)
        if j: recurrence(j)
        if a: tile_out(a, 4); tile_out(a, 5)

    mixer((0, 0), None)
    mixer((1, 0), (0, 0))
    with act.Fori(2, HEADS) as i:
        mixer((i, 0), (i, -1))
    mixer(None, (HEADS, -1))
    end_phase(k, act, 3)

    act.wait_ge(k.y_in, 16)
    for t in range(KW):
        act.activation(k.yst[:, t, :], k.yst[:, t, :], ACT.Gelu_apprx_tanh).then_inc(k.y_act, 1)
    for t in range(KW):
        act.wait_ge(k.y_act, t + 1)
        act.activation(k.gh[:, t, :], k.yst[:, t, :], ACT.Copy).then_inc(k.y_hi, 1)
    def glu(j):
        for t in range(2):
            split_hi(k, act, B_GLU + t + 1, 2, j)
            act.wait_ge(k.w_used, count(j, B_GLU + t + 1, 2))
            wait(act, [k.gb_st0, k.gb_st1][t], count(j, 0, 16))
            act.activation([k.gg0, k.gg1][t][:, :], ps[2 + t][:, :], ACT.Sigmoid).then_inc(k.sig, 1)

    glu((0, 0))
    with act.Fori(1, KW // 2) as i:
        glu((i, 0))
    end_phase(k, act, 4)

    for br in range(3):
        def branch_hi():
            act.wait_ge(k.ga_in, 16 * (br + 1))
            for t in range(KW):
                act.activation(k.gh[:, t, :], k.gst[:, t, :], ACT.Copy).then_inc(k.g_hi, 1)
        wait(act, k.w_used, B_BR + 24 * br)
        branch_hi()
        def merge(j):
            for pair in range(2):
                b0 = B_BR + 24 * br + 3 * pair
                for n in range(2):
                    d = 2 * pair + n
                    split_hi(k, act, b0 + n + 1, 6, j)
                    act.wait_ge(k.w_used, count(j, b0 + n + 1, 6))
                    wait(act, k.prod, count(j, 16 * br + d - 1, 4))
                    if br:
                        wait(act, k.mrg, count(j, 16 * br + d - 17, 4))
                    act.activation([k.sg0, k.sg1][n][:, :], ps[d][:, :], ACT.Sigmoid).then_inc(k.gate_s, 1)
                split_hi(k, act, b0 + 3, 6, j)

        merge((0, 0))
        with act.Fori(1, KD // 4) as i:
            merge((i, 0))
    end_phase(k, act, 5)

    for t in range(KD):
        act.activation(k.uh[:, t, :], k.merged[:, t, :], ACT.Copy).then_inc(k.m_hi, 1)
    for c in range(4):
        for kb in range(4):
            w = B_OUT + 4 * c + kb + 1
            if w < N_BLOCKS:
                split_hi(k, act, w)
        for m in range(NT):
            n = 4 * c + m
            act.wait_ge(k.h_s, n + 1)
            wait(act, k.h_sq, n)
            act.activation(k.xsq[:, :], k.hrow[:, m, c * S:(c + 1) * S], ACT.Square,
                           accum_out=k.ssq[:, m, c:c + 1]).then_inc(k.h_sq, 1)
    act.wait_ge(k.p_dve, 6)
    act.activation(k.stat[:, 8:12], k.stat[:, 0:4], ACT.Sqrt, bias=col["eps"], scale=1 / D).then_inc(k.p_act, 1)


def vector_program(k, dve):
    ps, mat, col, stat, tp, hp = k.ps, k.mat, k.col, k.stat, k.tp, k.hp
    done = [0]

    def step(instruction):
        instruction.then_inc(k.link, 1)
        done[0] += 1
        dve.wait_ge(k.link, done[0])

    tt, ts, stt = dve.tensor_tensor, dve.tensor_scalar, dve.scalar_tensor_tensor

    dve.wait_ge(k.rows_in, 160)
    dve.tensor_copy(k.rows2[64:96, :].rearrange("q (g s) -> q g s", g=2),
                    k.ldt2[64:96, :].unsqueeze(2).to_broadcast([32, 2, NS])).then_inc(k.ldt_rows, 1)
    dve.wait_ge(k.prm_ps, 2)
    dve.tensor_copy(k.prm1[:, :], ps[4][:, 0:P]).then_inc(k.prm, 1)
    dve.tensor_copy(k.prm2[:, :], ps[5][:, 0:P]).then_inc(k.prm, 1)
    dve.wait_ge(k.prm, 2)

    def scale_rows(first, n, at_root):
        dve.wait_ge(k.x_root, at_root)
        step(dve.reciprocal(stat[:, 16 + first:16 + first + n], stat[:, 8 + first:8 + first + n]))
        for m in range(n):
            ts(k.xs[:, m, :], k.xs[:, m, :], stat[:, 16 + first + m:17 + first + m], None, ALU.mult).then_inc(k.x_scale, 1)

    def tile_out(t, gain, hi, lo, n):
        u = [k.ut0, k.ut1][t % 2]
        dve.wait_ge(k.x_tr, t + 1)
        wait(dve, k.u_hi, t - 1)
        wait(dve, k.u_lo, t - 1)
        ts(u[:, 0:n], ps[t % 4][:, 0:n], gain, None, ALU.mult).then_inc(k.u_f32, 1)
        dve.wait_ge(k.u_hi, t + 1)
        tt(lo, u[:, 0:n], hi.bitcast(F32), ALU.subtract).then_inc(k.u_lo, 1)

    scale_rows(0, NT, 1)
    for t in range(KD):
        tile_out(t, k.prm1[:, 96 + t:97 + t], k.uh[:, t, :], k.ul[:, t, :], S)
    dve.wait_ge(k.wba_hi, 1)
    tt(k.wbal[:, :], k.wba[:, :], k.wbah[:, :].bitcast(F32), ALU.subtract).then_inc(k.wba_lo, 1)
    scale_rows(4, MT, 2)
    for t in range(KD):
        tile_out(KD + t, k.prm1[:, 112 + t:113 + t], k.mh[:, t, :], k.ml[:, t, :], MEM)

    lr, li = k.prm2[:, 0:32], k.prm2[:, 32:64]
    T = lambda n: tp[:, n, :]
    dve.wait_ge(k.p_act, 1)
    tt(T(1), lr, T(0), ALU.mult).then_inc(k.p_dve, 1)
    step(tt(T(6), li, T(0), ALU.mult))
    step(ts(T(7), T(6), 1 / TWO_PI, ROUND, ALU.mult, ALU.add))
    step(ts(T(7), T(7), -ROUND, None, ALU.add))
    for part in (PI_A, PI_B, PI_C):
        step(stt(T(6), T(7), -part, T(6), ALU.mult, ALU.add))
    step(ts(T(8), T(6), 1 / TWO_PI, ROUND14, ALU.mult, ALU.add))
    step(ts(k.s5p[:, 1, :], T(8), -ROUND14, None, ALU.add))
    for part in (PI_A, PI_B, PI_C):
        step(stt(T(6), k.s5p[:, 1, :], -part, T(6), ALU.mult, ALU.add))
    step(ts(k.s5p[:, 2, :], T(6), 1 / TWO_PI, None, ALU.mult))
    step(tt(T(3), k.s5p[:, 1, :], k.s5p[:, 2, :], ALU.add))
    ts(T(3), T(3), 0.4999999, -0.4999999, ALU.min, ALU.max).then_inc(k.p_dve, 1)
    dve.wait_ge(k.p_act, 3)
    step(dve.tensor_copy(k.s5p[:, 0, :], T(2)))
    step(tt(T(5), T(2), T(5), ALU.mult))
    step(ts(T(5), T(5), -1.0, None, ALU.add))
    step(tt(T(4), T(2), T(4), ALU.mult))
    step(tt(T(9), lr, lr, ALU.mult))
    step(tt(T(10), li, li, ALU.mult))
    step(tt(T(9), T(9), T(10), ALU.add))
    step(dve.reciprocal(T(9), T(9)))
    for n, (a, b, op) in enumerate(((T(5), T(4), ALU.add), (T(4), T(5), ALU.subtract))):
        step(tt(T(11), a, lr, ALU.mult))
        step(tt(T(12), b, li, ALU.mult))
        step(tt(T(11), T(11), T(12), op))
        step(tt(k.s5p[:, 3 + n, :], T(11), T(9), ALU.mult))

    ba = ps[6][:, 0:NT * 16].rearrange("p (m c) -> p m c", m=NT)
    rep = lambda v: v.unsqueeze(1).to_broadcast([P, NT, HEADS])
    dve.wait_ge(k.p_act, 4)
    step(ts(hp[:, 0, :, :], hp[:, 0, :, :], 1.0, None, ALU.add))
    step(dve.reciprocal(hp[:, 0, :, :], hp[:, 0, :, :]))
    tt(hp[:, 1, :, :], ba[:, :, HEADS:16], rep(k.dtb_b[:, :]), ALU.add).then_inc(k.p_dve, 1)
    dve.wait_ge(k.p_act, 5)
    ts(hp[:, 2, :, :], hp[:, 2, :, :], 1.0, None, ALU.add).then_inc(k.p_dve, 1)
    dve.wait_ge(k.p_act, 6)
    step(stt(hp[:, 2, :, :], hp[:, 1, :, :], 0.0, hp[:, 2, :, :], ALU.max, ALU.add))
    step(tt(hp[:, 2, :, :], hp[:, 2, :, :], rep(k.alog_b[:, :]), ALU.mult))
    ts(hp[:, 3, :, :], hp[:, 2, :, :], -1.0, None, ALU.mult).then_inc(k.g_done, 1)
    dve.wait_ge(k.p_act, 7)
    step(dve.tensor_copy(hp[:, 1, :, :], ps[7][:, 0:NT * HEADS].rearrange("p (m h) -> p m h", m=NT)))
    step(tt(hp[:, 2, :, :], hp[:, 2, :, :], hp[:, 0, :, :], ALU.mult))
    split_lo(k, dve, B_XA)
    end_phase(k, dve, 1)

    def at_max(j, m):
        dve.wait_ge(k.xa_sc, count(j, m + 1, 4))
        wait(dve, k.xa_exp, count(j, m - 3, 4))
        dve.reduce_max(stat[:, 20 + m:21 + m], ps[4 + m % 2][:, 0:MEM], AX_X).then_inc(k.xa_max, 1)
        dve.wait_ge(k.xa_max, count(j, 2 * m + 1, 8))
        ts(stat[:, 24 + m:25 + m], stat[:, 20 + m:21 + m], -1 / 16, None, ALU.mult).then_inc(k.xa_max, 1)

    def at_norm(j, m):
        dve.wait_ge(k.xa_exp, count(j, m + 1, 4))
        dve.reciprocal(stat[:, 32 + m:33 + m], stat[:, 28 + m:29 + m]).then_inc(k.xa_sum, 1)
        dve.wait_ge(k.xa_sum, count(j, m + 1, 4))
        ts(k.px[:, m, :], k.px[:, m, :], stat[:, 32 + m:33 + m], None, ALU.mult).then_inc(k.xa_p, 1)

    def at_small(j, n):
        if n == 0:
            dve.wait_ge(k.xa_vtr, count(j, 1, 1))
            wait(dve, k.xa_o, count(j, 0, 2))
            dve.tensor_copy(k.vx[:, :, :], ps[2][:, :].rearrange("p (m c) -> p m c", m=MT)).then_inc(k.xa_v, 1)
        if n < 2:
            at_max(j, 2 * n)
            at_max(j, 2 * n + 1)
            at_norm(j, 2 * n)
            at_norm(j, 2 * n + 1)
        elif n < 4:
            dve.wait_ge(k.xa_ptr, count(j, n - 1, 2))
            wait(dve, k.xa_o, count(j, 0, 2))
            dve.tensor_copy(k.ptx[:, n - 2, :], ps[4 + n][:, :]).then_inc(k.xa_pt, 1)
        elif n == 4:
            for t in range(2):
                dve.wait_ge(k.xa_o, count(j, t + 1, 2))
                wait(dve, [k.xa_st0, k.xa_st1][t], count(j, 0, 16))
                tt(k.ox[:, t, :], ps[2 + t][:, :], k.zx[:, t, :], ALU.mult).then_inc(k.xa_og, 1)

    def attention(a, j):
        for b in range(8):
            if a: split_lo(k, dve, B_XA + b + 1, 8, a)
            if j: at_small(j, b)

    attention((0, 0), None)
    attention((1, 0), (0, 0))
    with dve.Fori(2, XH) as i:
        attention((i, 0), (i, -1))
    attention(None, (XH, -1))
    end_phase(k, dve, 2)

    def chunked(v):
        return v.rearrange("p (n c) -> p n c", n=NT)

    def rows(v):
        return v.unsqueeze(2).to_broadcast([P, NT, P])

    def rep_chunks(m):
        return m.unsqueeze(1).to_broadcast([P, NT, P])

    def head_parameters(j):
        h = at(j)
        wait(dve, k.args, count(j, 0, 28))
        wait(dve, k.pm, count(j, 0, 4))
        dve.tensor_copy(k.s5h[:, :, :], k.s5p[:, :, bass.ds(4 * h, 4)]).then_inc(k.sliced, 1)
        dve.tensor_copy(k.cwh[:, :, :], k.prm1[:, 0:96].rearrange("p (n r h) -> p n r h", n=CONV, r=3)[:, :, :, bass.ds(h, 1)]).then_inc(k.sliced, 1)
        dve.tensor_copy(k.hph[:, :, :], hp[:, :, :, bass.ds(h, 1)]).then_inc(k.sliced, 1)
        dve.tensor_copy(k.dh[:, :], k.prm2[:, 96:104][:, bass.ds(h, 1)]).then_inc(k.sliced, 1)
        dve.wait_ge(k.sliced, count(j, 4, 4))

    def s5_matrices(j):
        w = k.s5_w
        dve.wait_ge(k.s5_in, count(j, 64, 64))
        cre, cim = (k.s5h[:, n, :].unsqueeze(2).to_broadcast([P, 4, GS]) for n in (3, 4))
        br, bi = k.braw[:, 0, :, :], k.braw[:, 1, :, :]
        for n, (b, c) in enumerate(((br, cre), (bi, cim), (bi, cre), (br, cim))):
            tt(k.bt[:, n, :, :], b, c, ALU.mult).then_inc(w, 1)
        dve.wait_ge(w, count(j, 4, 12))
        wait(dve, k.s5_tr, count(j, 0, 1))
        for n, op in ((0, ALU.subtract), (1, ALU.add)):
            for g in range(2):
                r = slice(64 * g, 64 * g + 64)
                tt(k.bpad[r, n, :, g, :], k.bt[r, 2 * n, :, :], k.bt[r, 2 * n + 1, :, :], op).then_inc(w, 1)
        for n, names in enumerate((("even", "odd"), ("neven", "nodd"))):
            for g in range(2):
                ts(k.cpad[:, n, g, :], k.craw[:, n, :], col[names[g]], None, ALU.mult).then_inc(w, 1)

    def convolve(j, part):
        src, dst = [k.qraw, k.kraw, k.vraw][part], [k.qc, k.kc, k.vc][part]
        n = count(j, 4 * part, 12)
        dve.wait_ge(k.mx_out, count(j, part + 1, 6))
        wait(dve, k.kq, count(j, 0, 1))
        wait(dve, k.kk, count(j, 0, 1))
        wait(dve, k.vtr, count(j, 0, 1))
        ts(dst[:, :], src[:, 0:S], k.cwh[:, 0, part:part + 1], None, ALU.mult).then_inc(k.conv, 1)
        for t in range(1, CONV):
            dve.wait_ge(k.conv, n + t)
            stt(dst[:, :], src[:, t:t + S], k.cwh[:, t, part:part + 1], dst[:, :], ALU.mult, ALU.add).then_inc(k.conv, 1)

    def log_decays(j):
        wait(dve, k.g_st, count(j, 0, 16))
        tt(k.gx[:, :, :], rep_chunks(mat["upper"]), rows(k.hph[:, 3, :]), ALU.mult).then_inc(k.gu, 1)

    def differences(j):
        dve.wait_ge(k.rsum, count(j, 1, 1))
        dve.wait_ge(k.er_s, count(j, 1, 1))
        wait(dve, k.vp, count(j, 0, 4))
        wait(dve, k.op, count(j, 0, 4))
        tt(k.dl[:, :, :], chunked(ps[7][:, :]), rows(k.hph[:, 1, :]), ALU.subtract).then_inc(k.dd, 1)
        dve.wait_ge(k.dd, count(j, 1, 3))
        ts(k.du[:, :, :], k.dl[:, :, :], 0.0, None, ALU.min).then_inc(k.dd, 1)
        ts(k.dl[:, :, :], k.dl[:, :, :], 0.0, None, ALU.max).then_inc(k.dd, 1)

    def normed(j):
        dve.wait_ge(k.root, count(j, 2, 2))
        dve.reciprocal(k.rk[:, :], k.rk[:, :]).then_inc(k.rn, 1)
        dve.reciprocal(k.rq[:, :], k.rq[:, :]).then_inc(k.rn, 1)
        dve.wait_ge(k.rn, count(j, 1, 2))
        tt(k.kc[:, :], k.kc[:, :], k.rk[:, :], ALU.mult).then_inc(k.qk, 1)
        dve.wait_ge(k.rn, count(j, 2, 2))
        tt(k.qc[:, :], k.qc[:, :], k.rq[:, :], ALU.mult).then_inc(k.qk, 1)

    def values(j):
        dve.wait_ge(k.vtr, count(j, 1, 1))
        tt(k.vb[:, :, :], chunked(ps[2][:, :]), rows(k.hph[:, 0, :]), ALU.mult).then_inc(k.vb_s, 1)

    def keys(j):
        dve.wait_ge(k.ktr, count(j, 1, 1))
        dve.wait_ge(k.dec, count(j, 2, 2))
        wait(dve, k.wt, count(j, 0, 1))
        wait(dve, k.sp_s, count(j, 0, 3))
        tt(k.kbg[:, :, :], chunked(ps[6][:, :]), rows(k.hph[:, 2, :]), ALU.mult).then_inc(k.kb, 1)
        tt(k.kd[:, :, :], chunked(ps[6][:, :]), k.du[:, :, P - 1:P].to_broadcast([P, NT, P]), ALU.mult).then_inc(k.kb, 1)

    def system(j):
        dve.wait_ge(k.kk, count(j, 1, 1))
        dve.wait_ge(k.pm, count(j, 2, 4))
        tt(k.dl[:, :, :], chunked(ps[7][:, :]), k.dl[:, :, :], ALU.mult).then_inc(k.lm, 1)

    def queries(j):
        dve.wait_ge(k.kq, count(j, 1, 1))
        dve.wait_ge(k.pm, count(j, 4, 4))
        tt(k.du[:, :, :], chunked(ps[2][:, :]), k.du[:, :, :], ALU.mult).then_inc(k.qkt, 1)

    def first_level(j):
        dve.wait_ge(k.lm, count(j, 1, 1))
        wait(dve, k.lx, count(j, 0, 6))
        tt(k.tl[:, :, :], k.dl[:, :, :], rep_chunks(mat["low1"]), ALU.mult).then_inc(k.tu_s, 1)
        dve.wait_ge(k.lt_s, count(j, 1, 1))
        tt(k.tu[:, :, :], k.lt[:, :, :], rep_chunks(mat["up1"]), ALU.mult).then_inc(k.tu_s, 1)
        dve.wait_ge(k.tu_s, count(j, 1, 4))
        tt(k.tl[:, :, :], rep_chunks(mat["ident"]), k.tl[:, :, :], ALU.subtract).then_inc(k.tu_s, 1)
        dve.wait_ge(k.tu_s, count(j, 2, 4))
        tt(k.tu[:, :, :], rep_chunks(mat["ident"]), k.tu[:, :, :], ALU.subtract).then_inc(k.tu_s, 1)

    def level_x(j, l):
        dve.wait_ge(k.lx, count(j, l, 6))
        tt(k.gx[:, :, :], chunked(ps[2][:, :]), rep_chunks(mat[f"low{2 ** l}"]), ALU.mult).then_inc(k.xm, 1)

    def level_p(j, l):
        dve.wait_ge(k.lp, count(j, l, 6))
        if l < 6:
            tt(k.tl[:, :, :], k.tl[:, :, :], chunked(ps[6][:, :]), ALU.subtract).then_inc(k.tus, 1)
        tt(k.tu[:, :, :], k.tu[:, :, :], chunked(ps[7][:, :]), ALU.subtract).then_inc(k.tus, 1)

    def state(j, n):
        dve.wait_ge(k.sp_s, count(j, n + 1, 3))
        dve.wait_ge(k.op, count(j, n + 1, 4))
        if n == 0:
            dve.tensor_copy(k.st[:, :], ps[7][:, 0:P]).then_inc(k.st_s, 1)
        else:
            stt(k.st[:, :], k.st[:, :], k.er[:, n, P - 1:P], ps[7][:, 0:P], ALU.mult, ALU.add).then_inc(k.st_s, 1)

    def gated(j):
        dve.wait_ge(k.oroot, count(j, 1, 1))
        dve.reciprocal(k.rq[:, :], k.rk[:, :]).then_inc(k.orn, 1)
        dve.wait_ge(k.orn, count(j, 1, 1))
        stt(k.gx[:, :, :], chunked(ps[2][:, :]), k.prm2[:, 104:105], chunked(k.rq[:, :]), ALU.mult, ALU.mult).then_inc(k.og, 1)
        dve.wait_ge(k.og, count(j, 1, 2))
        dve.wait_ge(k.mx_out, count(j, 5, 6))
        tt(k.gx[:, :, :], k.gx[:, :, :], chunked(k.zs[:, :]), ALU.mult).then_inc(k.og, 1)

    def s5_states(j, q):
        c, s = [k.tcos0, k.tcos1][q % 2], [k.tsin0, k.tsin1][q % 2]
        gr, gi = [k.gr0, k.gr1][q % 2], [k.gi0, k.gi1][q % 2]
        n = count(j, 8 * q, 32)
        re, im = ps[3], ps[4]
        dve.wait_ge(k.tab, count(j, 3 * q + 3, 12))
        dve.wait_ge(k.bu, count(j, q + 1, 4))
        wait(dve, k.dem, count(j, 6 * (q - 1), 24))
        if q == 0:
            wait(dve, k.y_st, count(j, 0, 16))
        for at_, g, (x1, x2, op) in ((n, gr, (re, im, ALU.add)), (n + 3, gi, (im, re, ALU.subtract))):
            tt(k.ma[:, :], x1[:, :], c[:, :], ALU.mult).then_inc(k.mod, 1)
            tt(k.mb[:, :], x2[:, :], s[:, :], ALU.mult).then_inc(k.mod, 1)
            dve.wait_ge(k.mod, at_ + 2)
            tt(g[:, :], k.ma[:, :], k.mb[:, :], op).then_inc(k.mod, 1)
            dve.wait_ge(k.mod, at_ + 3)
        for g in (gr, gi):
            dve.tensor_tensor_scan(g[:, :], k.s5h[:, 0, q:q + 1].to_broadcast([P, S]), g[:, :], 0.0,
                                   ALU.mult, ALU.add).then_inc(k.mod, 1)

    def s5_sum(j):
        dve.wait_ge(k.yp, count(j, 4, 4))
        stt(k.ma[:, :], k.xb[:, :], k.dh[:, 0:1], ps[5][:, :], ALU.mult, ALU.add).then_inc(k.ysum, 1)

    def mixer(a, j):
        split = lambda b: split_lo(k, dve, B_MIX + b + 1, 6, a)
        if a: split(0)
        if j: head_parameters(j); s5_matrices(j); convolve(j, 0); convolve(j, 1); convolve(j, 2); log_decays(j); s5_states(j, 0)
        if a: split(1)
        if j: differences(j); normed(j); values(j); s5_states(j, 1); keys(j); system(j)
        if a: split(2)
        if j: queries(j); first_level(j); s5_states(j, 2); level_x(j, 1)
        if a: split(3)
        if j: level_p(j, 1); level_x(j, 2); s5_states(j, 3); level_p(j, 2); level_x(j, 3); level_p(j, 3)
        if a: split(4)
        if j: level_x(j, 4); level_p(j, 4); s5_sum(j); level_x(j, 5); level_p(j, 5)
        if a: split(5)
        if j: level_x(j, 6); level_p(j, 6); state(j, 0); state(j, 1); state(j, 2); gated(j)

    mixer((0, 0), None)
    dve.wait_ge(k.pad_zero, 4)
    mixer((1, 0), (0, 0))
    with dve.Fori(2, HEADS) as i:
        mixer((i, 0), (i, -1))
    mixer(None, (HEADS, -1))
    end_phase(k, dve, 3)

    for t in range(KW):
        dve.wait_ge(k.y_hi, t + 1)
        tt(k.gl[:, t, :], k.yst[:, t, :], k.gh[:, t, :].bitcast(F32), ALU.subtract).then_inc(k.y_lo, 1)
    def glu(j):
        for t in range(2):
            gg, zv, gv = [k.gg0, k.gg1][t], [k.zv0, k.zv1][t], [k.gv0, k.gv1][t]
            split_lo(k, dve, B_GLU + t + 1, 2, j)
            dve.wait_ge(k.sig, count(j, t + 1, 2))
            tt(gg[:, :], ps[t][:, :], gg[:, :], ALU.mult).then_inc(gv, 1)
            dve.wait_ge(gv, count(j, 1, 2))
            dve.wait_ge([k.zb_in0, k.zb_in1][t], count(j, 16, 16))
            tt(gg[:, :], gg[:, :], zv[:, :], ALU.mult).then_inc(gv, 1)

    glu((0, 0))
    with dve.Fori(1, KW // 2) as i:
        glu((i, 0))
    end_phase(k, dve, 4)

    for br in range(3):
        for t in range(KW):
            dve.wait_ge(k.g_hi, KW * br + t + 1)
            tt(k.gl[:, t, :], k.gst[:, t, :], k.gh[:, t, :].bitcast(F32), ALU.subtract).then_inc(k.g_lo, 1)
        def merge(j):
            for pair in range(2):
                b0 = B_BR + 24 * br + 3 * pair
                for n in range(3):
                    split_lo(k, dve, b0 + n + 1, 6, j)
                for n in range(2):
                    d = 2 * pair + n
                    t = 16 * br + d
                    sg = [k.sg0, k.sg1][n]
                    m = k.merged[:, bass.ds(count(j, d, 4), 1), :]
                    if n == 0:
                        dve.wait_ge(k.p_ps, count(j, 8 * br + pair + 1, 2))
                    else:
                        dve.wait_ge(k.w_used, count(j, b0 + 3, 6))
                    dve.wait_ge(k.gate_s, count(j, t + 1, 4))
                    o = m if br == 0 else sg[:, :].unsqueeze(1)
                    tt(o, ps[4 + d][:, :].unsqueeze(1), sg[:, :].unsqueeze(1), ALU.mult).then_inc(k.prod, 1)
                    if br:
                        dve.wait_ge(k.prod, count(j, t + 1, 4))
                        tt(m, m, sg[:, :].unsqueeze(1), ALU.add).then_inc(k.mrg, 1)

        merge((0, 0))
        with dve.Fori(1, KD // 4) as i:
            merge((i, 0))
    end_phase(k, dve, 5)

    for t in range(KD):
        dve.wait_ge(k.m_hi, t + 1)
        tt(k.ul[:, t, :], k.merged[:, t, :], k.uh[:, t, :].bitcast(F32), ALU.subtract).then_inc(k.m_lo, 1)
    for c in range(4):
        for kb in range(4):
            w = B_OUT + 4 * c + kb + 1
            if w < N_BLOCKS:
                split_lo(k, dve, w)
        dve.wait_ge(k.xr_in, 64 * (c + 1))
        for m in range(NT):
            if m < 3:
                dve.wait_ge(k.o_ps, 3 * c + m + 1)
            else:
                dve.wait_ge(k.w_used, B_OUT + 4 * c + 4)
            tt(k.hrow[:, m, c * S:(c + 1) * S], ps[4 * (c % 2) + m][:, :], k.xr[:, m, :],
               ALU.add).then_inc(k.h_s, 1)
    dve.wait_ge(k.h_sq, 16)
    dve.reduce_sum(stat[:, 0:4], k.ssq[:, :, :], AX_X).then_inc(k.p_dve, 2)
    dve.wait_ge(k.p_act, 8)
    step(dve.reciprocal(stat[:, 16:20], stat[:, 8:12]))
    dve.wait_ge(k.fg_in, 16)
    for m in range(NT):
        stt(k.hrow[:, m, :], k.hrow[:, m, :], stat[:, 16 + m:17 + m], k.fg[:, :], ALU.mult, ALU.mult).then_inc(k.fin, 1)


_INS = ["x", "mem", "norm_g", "w_in", "conv_w", "gdn_a_log", "gdn_dt_bias", "gdn_norm_g", "s5_lambda_re",
        "s5_lambda_im", "s5_log_dt", "s5_b_re", "s5_b_im", "s5_c_re", "s5_c_im", "s5_d", "s5_w_glu",
        "mem_norm_g", "w_kv_mem", "w_br_a", "w_br_b", "w_br_c", "w_out", "final_g"]


def kernel(**inputs):
    import concourse.bacc as _bacc
    from concourse.bass_utils import run_bass_kernel_spmd as _run

    nc = _bacc.Bacc("TRN2", target_bir_lowering=False, num_devices=1)
    arrays, args = {}, []
    for name in _INS + ["consts"]:
        a = constants() if name == "consts" else np.ascontiguousarray(inputs[name])
        arrays[f"in_{name}_dram"] = a
        args.append(nc.dram_tensor(f"in_{name}_dram", a.shape, mybir.dt.from_np(a.dtype), kind="ExternalInput").ap())
    args.append(nc.dram_tensor("out_0_dram", (1, S, D), F32, kind="ExternalOutput").ap())
    build(nc, *args)
    r = _run(nc, [arrays], core_ids=[0])
    return r.results[0]["out_0_dram"]
```

```python
from contextlib import ExitStack

import numpy as np
import concourse.bass as bass
from concourse import mybir

F32 = mybir.dt.float32
F32R = mybir.dt.float32r
ALU = mybir.AluOpType
ACT = mybir.ActivationFunctionType
AX_X = mybir.AxisListType.X

P = 128
S = 512
D = 2048
KD = D // P
NT = S // P
W = 1024
KW = W // P
MEM = 256
MT = MEM // P
HEADS = 8
XH = 4
GS = 16
NS = 64
PAIRS = 32
EPS = 1e-6
Q0, K0, V0, ZA0, BA0 = 0, W, 2 * W, 3 * W, 4 * W
XB0 = BA0 + 2 * HEADS
ZB0, QC0, ZC0 = XB0 + W, XB0 + 2 * W, XB0 + 3 * W
G0 = XB0 + 4 * W
CONV = 4
LEVELS = [2 ** n for n in range(7)]
MATS = ["ident", "upper", "strict", "ones"] + [f"low{s}" for s in LEVELS] + ["up1"]
C_T = len(MATS) * P
C_COL = C_T + S
COLS = ["eps", "eps128", "quarter", "even", "odd", "neven", "nodd"]
NCONST = C_COL + len(COLS)
TWO_PI = 2 * np.pi
PI_A = 6.28125
PI_B = float(np.float32(int((TWO_PI - PI_A) * 2 ** 20) / 2 ** 20))
PI_C = float(TWO_PI - PI_A - PI_B)
ROUND = 1.5 * 2 ** 23
ROUND14 = 1.5 * 2 ** 9


def constants():
    c = np.zeros((P, NCONST), np.float32)
    i, j = np.indices((P, P))
    m = {"ident": i == j, "upper": i <= j, "strict": i > j, "ones": i >= 0}
    for s in LEVELS:
        m[f"low{s}"] = (i // s % 2 == 1) & (j // s == i // s - 1)
    m["up1"] = m["low1"].T
    for n, name in enumerate(MATS):
        c[:, n * P:(n + 1) * P] = m[name]
    c[:, C_T:C_T + S] = np.arange(S)
    g2 = np.arange(P) // GS % 2
    for n, v in enumerate([EPS, P * EPS, np.pi / 2, g2 == 0, g2 == 1, -(g2 == 0).astype(float), -(g2 == 1).astype(float)]):
        c[:, C_COL + n] = v
    return c



def at(j):
    return j[0] + j[1]


def count(j, first, per):
    return j[0] * per + (first + per * j[1])


def wait(e, s, value):
    if isinstance(value, int) and value <= 0:
        return
    e.wait_ge(s, value)


def wait_apart(k, e, s, value):
    wait(e, s, value)
    if not isinstance(value, int):
        e.sem_inc(k.sp_waits if e is k.sp else k.pool_waits, 1)


class Handles:
    pass


def build(nc, x, mem, norm_g, w_in, conv_w, a_log, dt_bias, gdn_g, lam_re, lam_im, log_dt, b_re, b_im,
          c_re, c_im, s5_d, w_glu, mem_g, w_kv, w_a, w_b, w_c, w_out, final_g, consts, out):
    with ExitStack() as ctx:
        k = Handles()
        k.nc = nc
        k.x, k.mem, k.out = x[0], mem[0], out[0]
        k.norm_g, k.mem_g, k.gdn_g, k.s5_d, k.final_g = norm_g[0], mem_g[0], gdn_g[0], s5_d[0], final_g
        k.w_in, k.conv_w, k.w_glu, k.w_kv, k.w_out = w_in[0], conv_w[0], w_glu[0], w_kv[0], w_out[0]
        k.branch_w = [w_c[0], w_b[0], w_a[0]]
        k.a_log, k.dt_bias, k.consts = a_log[0], dt_bias[0], consts
        k.lam_re, k.lam_im, k.log_dt = lam_re[0], lam_im[0], log_dt[0]
        k.b_re, k.b_im, k.c_re, k.c_im = b_re[0], b_im[0], c_re[0], c_im[0]
        k.gated_d = [nc.dram_tensor(f"gated_{n}", [W, S], F32, kind="Internal").ap() for n in "cba"]
        k.y_d = nc.dram_tensor("s5_out", [W, S], F32, kind="Internal").ap()
        k.zb_d = nc.dram_tensor("z_b", [W, S], F32, kind="Internal").ap()

        def sb(where, name, shape, dt=F32):
            return where.enter_context(nc.sbuf_tensor(name, [P] + shape, dt))

        def sems(*names):
            return [ctx.enter_context(nc.semaphore(name)) for name in names]

        k.ps = [ctx.enter_context(nc.psum_tensor(f"bank{n}", [P, S], F32)) for n in range(8)]

        k.uh = sb(ctx, "uh", [KD, S], F32R)
        k.ul = sb(ctx, "ul", [KD, S], F32R)
        k.raw0 = sb(ctx, "raw0", [2048])
        k.raw1 = sb(ctx, "raw1", [2048])
        k.wh0 = sb(ctx, "wh0", [2048], F32R)
        k.wh1 = sb(ctx, "wh1", [2048], F32R)
        k.wl0 = sb(ctx, "wl0", [2048], F32R)
        k.wl1 = sb(ctx, "wl1", [2048], F32R)
        k.cst = sb(ctx, "cst", [NCONST])
        k.prm1 = sb(ctx, "prm1", [P])
        k.prm2 = sb(ctx, "prm2", [P])
        k.s5p = sb(ctx, "s5p", [5, PAIRS])
        k.hp = sb(ctx, "hp", [4, NT, HEADS])
        k.stat = sb(ctx, "stat", [40])
        k.raw, k.wh, k.wl = [k.raw0, k.raw1], [k.wh0, k.wh1], [k.wl0, k.wl1]
        k.mat = {name: k.cst[:, n * P:(n + 1) * P] for n, name in enumerate(MATS)}
        k.col = {name: k.cst[:, C_COL + n:C_COL + n + 1] for n, name in enumerate(COLS)}
        k.tvec = k.cst[:, C_T:C_T + S]

        with ExitStack() as area:
            k.mh = sb(area, "mh", [KD, MEM], F32R)
            k.ml = sb(area, "ml", [KD, MEM], F32R)
            with ExitStack() as a:
                k.xs = sb(a, "xs", [NT, D])
                k.junk = sb(a, "junk", [D])
                k.ut0 = sb(a, "ut0", [S])
                k.ut1 = sb(a, "ut1", [S])
                k.rows1 = sb(a, "rows1", [P])
                k.rows2 = sb(a, "rows2", [P])
                k.ldt2 = sb(a, "ldt2", [2])
                k.alog_b = sb(a, "alog_b", [HEADS])
                k.dtb_b = sb(a, "dtb_b", [HEADS])
                k.wba = sb(a, "wba", [KD * 16])
                k.wbah = sb(a, "wbah", [KD * 16], F32R)
                k.wbal = sb(a, "wbal", [KD * 16], F32R)
                k.tp = sb(a, "tp", [16, PAIRS])
            with ExitStack() as a:
                k.kt = sb(a, "kt", [2, MEM])
                k.vt = sb(a, "vt", [2, MEM])
                k.vx = sb(a, "vx", [MT, 256])
                k.qx = sb(a, "qx", [2, S])
                k.zx = sb(a, "zx", [2, S])
                k.px = sb(a, "px", [NT, MEM])
                k.ptx = sb(a, "ptx", [MT, S])
                k.ox = sb(a, "ox", [2, S])
        with ExitStack() as area:
            k.qraw = sb(area, "qraw", [S + 3])
            k.kraw = sb(area, "kraw", [S + 3])
            k.vraw = sb(area, "vraw", [S + 3])
            k.qc = sb(area, "qc", [S])
            k.kc = sb(area, "kc", [S])
            k.vc = sb(area, "vc", [S])
            k.rq = sb(area, "rq", [S])
            k.rk = sb(area, "rk", [S])
            k.zs = sb(area, "zs", [S])
            k.zk = sb(area, "zk", [S])
            k.er = sb(area, "er", [NT, P])
            k.qd = sb(area, "qd", [NT, P])
            k.dl = sb(area, "dl", [NT, P])
            k.du = sb(area, "du", [NT, P])
            k.vb = sb(area, "vb", [NT, P])
            k.kbg = sb(area, "kbg", [NT, P])
            k.kd = sb(area, "kd", [NT, P])
            k.lt = sb(area, "lt", [NT, P])
            k.tl = sb(area, "tl", [NT, P])
            k.tu = sb(area, "tu", [NT, P])
            k.gx = sb(area, "gx", [NT, P])
            k.vn = sb(area, "vn", [NT, P])
            k.st = sb(area, "st", [P])
            k.cwh = sb(area, "cwh", [CONV, 3])
            k.hph = sb(area, "hph", [4, NT])
            k.s5h = sb(area, "s5h", [5, 4])
            k.dh = sb(area, "dh", [1])
            k.xb = sb(area, "xb", [S])
            k.braw = sb(area, "braw", [2, 4, GS])
            k.craw = sb(area, "craw", [2, NS])
            k.bt = sb(area, "bt", [6, 4, GS])
            k.bpad = sb(area, "bpad", [2, 4, 2, GS])
            k.cpad = sb(area, "cpad", [2, 2, NS])
            k.bc = sb(area, "bc", [4, P])
            k.tcos0 = sb(area, "tcos0", [S])
            k.tcos1 = sb(area, "tcos1", [S])
            k.tsin0 = sb(area, "tsin0", [S])
            k.tsin1 = sb(area, "tsin1", [S])
            k.karg = sb(area, "karg", [S])
            k.farg = sb(area, "farg", [S])
            k.ma = sb(area, "ma", [S])
            k.mb = sb(area, "mb", [S])
            k.gr0 = sb(area, "gr0", [S])
            k.gr1 = sb(area, "gr1", [S])
            k.gi0 = sb(area, "gi0", [S])
            k.gi1 = sb(area, "gi1", [S])
            k.hr = sb(area, "hr", [S])
            k.hi = sb(area, "hi", [S])
            k.pt = sb(area, "pt", [S])
            k.zbs = sb(area, "zbs", [S])
        with ExitStack() as area:
            k.zv0 = sb(area, "zv0", [S])
            k.zv1 = sb(area, "zv1", [S])
            k.gg0 = sb(area, "gg0", [S])
            k.gg1 = sb(area, "gg1", [S])
        with ExitStack() as area:
            k.merged = sb(area, "merged", [KD, S])
            with ExitStack() as b:
                k.gh = sb(b, "gh", [KW, S], F32R)
                k.gl = sb(b, "gl", [KW, S], F32R)
                with ExitStack() as a:
                    k.gst = sb(a, "gst", [KW, S])
                    k.sg0 = sb(a, "sg0", [S])
                    k.sg1 = sb(a, "sg1", [S])
                with ExitStack() as a:
                    k.yst = sb(a, "yst", [KW, S])
            with ExitStack() as b:
                k.hrow = sb(b, "hrow", [NT, D])
                k.xr = sb(b, "xr", [NT, S])
                k.fg = sb(b, "fg", [D])
                k.xsq = sb(b, "xsq", [S])
                k.ssq = sb(b, "ssq", [NT, 4])

        k.sp_waits, k.pool_waits, k.w_in0, k.w_in1, k.w_hi, k.w_lo = \
            sems("sp_waits", "pool_waits", "w_in0", "w_in1", "w_hi", "w_lo")
        k.w_used, k.phase_end = \
            sems("w_used", "phase_end")
        k.w_in_slot = [k.w_in0, k.w_in1]
        k.cst_in, k.rows_in, k.rows_zero, k.x_in, k.mem_in, k.wba_in = \
            sems("cst_in", "rows_in", "rows_zero", "x_in", "mem_in", "wba_in")
        k.prm_ps, k.prm, k.ldt_rows, k.x_sq, k.x_root, k.x_scale = \
            sems("prm_ps", "prm", "ldt_rows", "x_sq", "x_root", "x_scale")
        k.x_tr, k.u_f32, k.u_hi, k.u_lo, k.link, k.alink = \
            sems("x_tr", "u_f32", "u_hi", "u_lo", "link", "alink")
        k.wba_hi, k.wba_lo, k.ba_ps, k.g_done, k.gsum_ps, k.p_act = \
            sems("wba_hi", "wba_lo", "ba_ps", "g_done", "gsum_ps", "p_act")
        k.p_dve, = \
            sems("p_dve")
        k.xa_out, k.xa_vtr, k.xa_v, k.xa_sc, k.xa_max, k.xa_exp = \
            sems("xa_out", "xa_vtr", "xa_v", "xa_sc", "xa_max", "xa_exp")
        k.xa_sum, k.xa_p, k.xa_ptr, k.xa_pt, k.xa_o, k.xa_og = \
            sems("xa_sum", "xa_p", "xa_ptr", "xa_pt", "xa_o", "xa_og")
        k.xa_st0, k.xa_st1 = \
            sems("xa_st0", "xa_st1")
        k.mx_out, k.zb_st, k.pad_zero, k.z_kept = \
            sems("mx_out", "zb_st", "pad_zero", "z_kept")
        k.sliced, k.conv, k.gu, k.silu, k.sq, k.ss = \
            sems("sliced", "conv", "gu", "silu", "sq", "ss")
        k.rsum, k.root, k.er_s, k.dd, k.dec, k.rn = \
            sems("rsum", "root", "er_s", "dd", "dec", "rn")
        k.qk, k.vtr, k.vb_s, k.ktr, k.kb, k.kk = \
            sems("qk", "vtr", "vb_s", "ktr", "kb", "kk")
        k.kq, k.pm, k.lm, k.qkt, k.ltr, k.lt_s = \
            sems("kq", "pm", "lm", "qkt", "ltr", "lt_s")
        k.tu_s, k.lx, k.xm, k.lp, k.tus, k.wt = \
            sems("tu_s", "lx", "xm", "lp", "tus", "wt")
        k.wtn, k.vp, k.vn_s, k.op, k.sp_s, k.st_s = \
            sems("wtn", "vp", "vn_s", "op", "sp_s", "st_s")
        k.osq, k.sso, k.oroot, k.orn, k.og, k.g_st = \
            sems("osq", "sso", "oroot", "orn", "og", "g_st")
        k.s5_in, k.s5_w, k.s5_tr, k.bc_s, k.args, k.tab = \
            sems("s5_in", "s5_w", "s5_tr", "bc_s", "args", "tab")
        k.bu, k.mod, k.dem, k.yp, k.ysum, k.y_st = \
            sems("bu", "mod", "dem", "yp", "ysum", "y_st")
        k.y_in, k.y_act, k.y_hi, k.y_lo, k.glu_ps, k.sig = \
            sems("y_in", "y_act", "y_hi", "y_lo", "glu_ps", "sig")
        k.zb_in0, k.zb_in1, k.gv0, k.gv1, k.gb_st0, k.gb_st1 = \
            sems("zb_in0", "zb_in1", "gv0", "gv1", "gb_st0", "gb_st1")
        k.ga_in, k.g_hi, k.g_lo, k.gate_ps, k.p_ps, k.gate_s = \
            sems("ga_in", "g_hi", "g_lo", "gate_ps", "p_ps", "gate_s")
        k.prod, k.mrg, k.m_hi, k.m_lo, k.o_ps, k.xr_in = \
            sems("prod", "mrg", "m_hi", "m_lo", "o_ps", "xr_in")
        k.fg_in, k.h_s, k.h_sq, k.fin, k.o_st = \
            sems("fg_in", "h_s", "h_sq", "fin", "o_st")

        block = ctx.enter_context(nc.Block())

        @block.sync
        def _(sp):
            k.sp = sp
            sync_program(k, sp)

        @block.gpsimd
        def _(pool):
            pool_program(k, pool)

        @block.scalar
        def _(act):
            scalar_program(k, act)

        @block.vector
        def _(dve):
            vector_program(k, dve)

        @block.tensor
        def _(pe):
            tensor_program(k, pe)


B_XA = 0
B_MIX = B_XA + 8 * XH
B_GLU = B_MIX + 6 * HEADS
B_BR = B_GLU + KW
B_OUT = B_BR + 3 * 24
N_BLOCKS = B_OUT + 16


def end_phase(k, e, n):
    e.drain().then_inc(k.phase_end, 1)
    e.wait_ge(k.phase_end, 4 * n)



def load_halves(k, sp, w0, per, j, sources):
    slot = w0 % 2
    wait_apart(k, sp, k.w_lo, count(j, w0 - 1, per))
    for half, src in enumerate(sources):
        n = src.shape[1]
        dst = k.raw[slot][:, half * 1024:(half + 1) * 1024].rearrange("p (k c) -> p k c", k=n)
        sp.dma_start(dst, src).then_inc(k.w_in_slot[slot], 16)


def columns(w, c, n=P):
    return w[:, bass.ds(c, n)].rearrange("(k p) c -> p k c", p=P)


def load_fm(k, sp, w0, per, j, w, c):
    v = columns(w, c)
    load_halves(k, sp, w0, per, j, [v[:, 0:8, :], v[:, 8:16, :]])


def load_fm8(k, sp, w0, per, j, w, c, c2):
    load_halves(k, sp, w0, per, j, [columns(w, c), columns(w, c2)])


def load_tm(k, sp, w0, per, j, w, rows, c):
    v = columns(w, c, S)
    load_halves(k, sp, w0, per, j, [v[:, rows:rows + 2, :], v[:, rows + 2:rows + 4, :]])


def split_hi(k, act, w0, per=0, j=(0, 0)):
    slot = w0 % 2
    wait(act, k.w_in_slot[slot], count(j, 32 * (w0 // 2 + 1), 16 * per))
    wait(act, k.w_used, count(j, w0 - 1, per))
    act.activation(k.wh[slot][:, :], k.raw[slot][:, :], ACT.Copy).then_inc(k.w_hi, 1)


def split_lo(k, dve, w0, per=0, j=(0, 0)):
    slot = w0 % 2
    wait(dve, k.w_hi, count(j, w0 + 1, per))
    wait(dve, k.w_used, count(j, w0 - 1, per))
    dve.tensor_tensor(k.wl[slot][:, :], k.raw[slot][:, :], k.wh[slot][:, :].bitcast(F32),
                      ALU.subtract).then_inc(k.w_lo, 1)


def mm3(pe, o, ah, al, bh, bl, start, stop):
    pe.matmul(o, ah, bh, start=start, stop=False)
    pe.matmul(o, ah, bl, start=False, stop=False)
    return pe.matmul(o, al, bh, start=False, stop=stop)


def row_tiles(k, pe, slot, o, tiles, at_tile, acth, actl, n_tiles):
    for n, t in enumerate(tiles):
        a = bass.ts(at_tile + n, P)
        mm = mm3(pe, o, k.wh[slot][:, a], k.wl[slot][:, a], acth[:, t, :], actl[:, t, :],
                 t == 0, t == n_tiles - 1)
    return mm


def eighth(k, pe, w0, per, j, q, acth, actl, n, outs, before):
    slot = w0 % 2
    if q == 0:
        wait(pe, k.w_lo, count(j, w0 + 1, per))
        wait(pe, outs, count(j, w0 - before - 1, per))
    mm = row_tiles(k, pe, slot, k.ps[slot][:, 0:n], range(2 * q, 2 * q + 2), 2 * q, acth, actl, KD)
    if q == 7:
        mm.then_inc(k.w_used, 1)


def sync_program(k, sp):
    sp.dma_start(k.cst[:, :], k.consts).then_inc(k.cst_in, 16)
    for m in range(NT):
        sp.dma_start(k.xs[:, m, :], k.x[m * P:(m + 1) * P, :]).then_inc(k.x_in, 16)
    sp.wait_ge(k.rows_zero, 1)
    sp.dma_start(k.rows1[0:96, :], k.conv_w.rearrange("j (t c) -> (j t) c", c=P)).then_inc(k.rows_in, 16)
    sp.dma_start(k.rows1[96:112, :], k.norm_g.rearrange("(t c) -> t c", c=P)).then_inc(k.rows_in, 16)
    sp.dma_start(k.rows1[112:128, :], k.mem_g.rearrange("(t c) -> t c", c=P)).then_inc(k.rows_in, 16)
    sp.dma_start(k.rows2[0:32, :], k.lam_re.rearrange("(q g) s -> q (g s)", g=2)).then_inc(k.rows_in, 16)
    sp.dma_start(k.rows2[32:64, :], k.lam_im.rearrange("(q g) s -> q (g s)", g=2)).then_inc(k.rows_in, 16)
    sp.dma_start(k.rows2[96:104, :], k.s5_d.rearrange("(t c) -> t c", c=P)).then_inc(k.rows_in, 16)
    sp.dma_start(k.rows2[104:105, :], k.gdn_g.rearrange("(t c) -> t c", c=P)).then_inc(k.rows_in, 16)
    sp.dma_start(k.ldt2[64:96, :], k.log_dt.rearrange("(q g) -> q g", g=2)).then_inc(k.rows_in, 16)
    sp.dma_start(k.alog_b[:, :], k.a_log.partition_broadcast(P)).then_inc(k.rows_in, 16)
    sp.dma_start(k.dtb_b[:, :], k.dt_bias.partition_broadcast(P)).then_inc(k.rows_in, 16)
    sp.dma_start(k.wba[:, :].rearrange("p (k c) -> p k c", c=16), columns(k.w_in, BA0, 16)).then_inc(k.wba_in, 16)
    sp.wait_ge(k.x_tr, KD)
    for m in range(MT):
        sp.dma_start(k.xs[:, m, :], k.mem[m * P:(m + 1) * P, :]).then_inc(k.mem_in, 16)

    def attention_loads(j):
        for b, (w, c0) in enumerate(((k.w_kv, 0), (k.w_kv, W), (k.w_in, QC0), (k.w_in, ZC0))):
            for t in range(2):
                load_fm(k, sp, B_XA + 2 * b + t, 8, j, w, count(j, c0 + t * P, 2 * P))
    attention_loads((0, 0))
    with sp.Fori(1, XH) as i:
        attention_loads((i, 0))

    def mixer_loads(j):
        for b, c0 in enumerate(MIX_COLS):
            load_fm(k, sp, B_MIX + b, 6, j, k.w_in, count(j, c0, P))

    def s5_loads(j):
        wait_apart(k, sp, k.s5_w, count(j, 0, 13))
        for n, b in enumerate((k.b_re, k.b_im)):
            sp.dma_start(k.braw[:, n, :, :], b[bass.ds(count(j, 0, 8), 8)].rearrange("(q g) s i -> (g s) q i", g=2)).then_inc(k.s5_in, 16)
        for n, c in enumerate((k.c_re, k.c_im)):
            sp.dma_start(k.craw[:, n, :], c[bass.ds(count(j, 0, 8), 8)].rearrange("g i s -> (g i) s")).then_inc(k.s5_in, 16)

    mixer_loads((0, 0))
    sp.wait_ge(k.phase_end, 8)
    s5_loads((0, 0))
    with sp.Fori(1, HEADS) as i:
        mixer_loads((i, 0))
        s5_loads((i, 0))

    with sp.Fori(0, KW // 2) as i:
        for t in range(2):
            c = count((i, 0), t * P, 2 * P)
            load_fm8(k, sp, B_GLU + t, 2, (i, 0), k.w_glu, c, c + W)

    for br, w in enumerate(k.branch_w):
        gate0 = G0 + (2, 1, 0)[br] * D
        with sp.Fori(0, KD // 4) as i:
            j = (i, 0)
            for pair in range(2):
                b = B_BR + 24 * br + 3 * pair
                c = count(j, 2 * pair * P, 4 * P)
                load_fm(k, sp, b, 6, j, k.w_in, c + gate0)
                load_fm(k, sp, b + 1, 6, j, k.w_in, c + (gate0 + P))
                load_fm8(k, sp, b + 2, 6, j, w, c, c + P)

    with sp.Fori(0, 4) as i:
        for kb in range(4):
            load_tm(k, sp, B_OUT + kb, 4, (i, 0), k.w_out, 4 * kb, i * S)


MIX_COLS = (Q0, K0, V0, ZB0, ZA0, XB0)


def pool_program(k, pool):
    pool.memset(k.rows2[:, :], 0.0).then_inc(k.rows_zero, 1)
    end_phase(k, pool, 1)

    def attention_store(j):
        for t in range(2):
            wait_apart(k, pool, k.xa_og, count(j, t + 1, 2))
            pool.dma_start(k.gated_d[0][bass.ds(count(j, t * P, 2 * P), P), :], k.ox[:, t, :]).then_inc([k.xa_st0, k.xa_st1][t], 16)
    with pool.Fori(0, XH) as i:
        attention_store((i, 0))
    pool.wait_ge(k.xa_st0, 16 * XH)
    pool.wait_ge(k.xa_st1, 16 * XH)
    end_phase(k, pool, 2)

    for t in (k.qraw, k.kraw, k.vraw):
        pool.memset(t[:, 0:3], 0.0).then_inc(k.pad_zero, 1)
    pool.memset(k.bpad[:, :, :, :, :], 0.0).then_inc(k.pad_zero, 1)

    def mixer(j, l):
        tcos, tsin, gr, gi = [k.tcos0, k.tcos1], [k.tsin0, k.tsin1], [k.gr0, k.gr1], [k.gi0, k.gi1]

        def arguments(q):
            hi_, lo_ = k.s5h[:, 1, q:q + 1], k.s5h[:, 2, q:q + 1]
            n = count(j, 7 * q, 28)
            if q == 0:
                wait_apart(k, pool, k.sliced, count(j, 3, 3))
            wait_apart(k, pool, k.tab, count(j, 3 * q, 12))
            ts, tt = pool.tensor_scalar, pool.tensor_tensor
            ts(k.karg[:, :], k.tvec, hi_, ROUND, ALU.mult, ALU.add).then_inc(k.args, 1)
            ts(k.farg[:, :], k.tvec, hi_, None, ALU.mult).then_inc(k.args, 1)
            wait_apart(k, pool, k.args, n + 1)
            ts(k.karg[:, :], k.karg[:, :], -ROUND, None, ALU.add).then_inc(k.args, 1)
            wait_apart(k, pool, k.args, n + 3)
            tt(k.farg[:, :], k.farg[:, :], k.karg[:, :], ALU.subtract).then_inc(k.args, 1)
            wait_apart(k, pool, k.args, n + 4)
            ts(k.karg[:, :], k.tvec, lo_, None, ALU.mult).then_inc(k.args, 1)
            wait_apart(k, pool, k.args, n + 5)
            tt(k.farg[:, :], k.farg[:, :], k.karg[:, :], ALU.add).then_inc(k.args, 1)
            wait_apart(k, pool, k.args, n + 6)
            ts(k.farg[:, :], k.farg[:, :], 0.4999999, -0.4999999, ALU.min, ALU.max).then_inc(k.args, 1)

        def turn_back(q):
            c, s, a, b = tcos[q % 2], tsin[q % 2], gr[q % 2], gi[q % 2]
            n = count(j, 6 * q, 24)
            wait_apart(k, pool, k.mod, count(j, 8 * q + 8, 32))
            wait_apart(k, pool, k.yp, count(j, q, 4))
            for o, (c1, c2, op) in ((k.hr, (c, s, ALU.subtract)), (k.hi, (s, c, ALU.add))):
                pool.tensor_tensor(o[:, :], c1[:, :], a[:, :], ALU.mult).then_inc(k.dem, 1)
                pool.tensor_tensor(k.pt[:, :], c2[:, :], b[:, :], ALU.mult).then_inc(k.dem, 1)
                wait_apart(k, pool, k.dem, n + 2)
                pool.tensor_tensor(o[:, :], o[:, :], k.pt[:, :], op).then_inc(k.dem, 1)
                wait_apart(k, pool, k.dem, n + 3)
                n = n + 3

        def masks():
            wait_apart(k, pool, k.dec, count(j, 2, 2))
            pool.tensor_tensor(k.dl[:, :, :], k.dl[:, :, :],
                               k.mat["strict"].unsqueeze(1).to_broadcast([P, NT, P]), ALU.mult).then_inc(k.pm, 1)
            wait_apart(k, pool, k.pm, count(j, 1, 4))
            pool.tensor_tensor(k.dl[:, :, :], k.dl[:, :, :],
                               k.hph[:, 0, :].unsqueeze(2).to_broadcast([P, NT, P]), ALU.mult).then_inc(k.pm, 1)
            pool.tensor_tensor(k.du[:, :, :], k.du[:, :, :],
                               k.mat["upper"].unsqueeze(1).to_broadcast([P, NT, P]), ALU.mult).then_inc(k.pm, 1)

        def decayed_queries():
            wait_apart(k, pool, k.qk, count(j, 2, 2))
            pool.tensor_tensor(k.qd[:, :, :], k.qc[:, :].rearrange("p (n c) -> p n c", n=NT), k.er[:, :, :],
                               ALU.mult).then_inc(k.pm, 1)

        def store_s5():
            wait_apart(k, pool, k.ysum, count(l, 1, 1))
            pool.dma_start(k.y_d[bass.ds(at(l) * P, P), :], k.ma[:, :]).then_inc(k.y_st, 16)

        def store_head():
            wait_apart(k, pool, k.og, count(l, 2, 2))
            pool.dma_start(k.gated_d[2][bass.ds(at(l) * P, P), :],
                           k.kbg[:, :, :].rearrange("p n c -> p (n c)")).then_inc(k.g_st, 16)

        if j: arguments(0)
        if l: store_s5()
        if j: arguments(1); turn_back(0)
        if l: store_head()
        if j: masks(); arguments(2); decayed_queries(); turn_back(1); arguments(3); turn_back(2); turn_back(3)

    def gate_store(j):
        wait_apart(k, pool, k.mx_out, count(j, 4, 6))
        pool.dma_start(k.zb_d[bass.ds(at(j) * P, P), :], k.zbs[:, :]).then_inc(k.zb_st, 16)

    gate_store((0, 0))
    mixer((0, 0), None)
    gate_store((1, 0))
    with pool.Fori(2, HEADS) as i:
        mixer((i, -1), (i, -2))
        gate_store((i, 0))
    mixer((HEADS, -1), (HEADS, -2))
    mixer(None, (HEADS, -1))
    pool.wait_ge(k.zb_st, 16 * HEADS)
    pool.wait_ge(k.y_st, 16 * HEADS)
    pool.wait_ge(k.g_st, 16 * HEADS)
    end_phase(k, pool, 3)

    pool.dma_start(k.yst[:, :, :], k.y_d.rearrange("(t p) s -> p t s", p=P)).then_inc(k.y_in, 16)

    def glu(j):
        for t in range(2):
            zv, gg = [k.zv0, k.zv1][t], [k.gg0, k.gg1][t]
            row = count(j, t * P, 2 * P)
            wait_apart(k, pool, [k.gv0, k.gv1][t], count(j, 0, 2))
            pool.dma_start(zv[:, :], k.zb_d[bass.ds(row, P), :]).then_inc([k.zb_in0, k.zb_in1][t], 16)
            wait_apart(k, pool, [k.gv0, k.gv1][t], count(j, 2, 2))
            pool.dma_start(k.gated_d[1][bass.ds(row, P), :], gg[:, :]).then_inc([k.gb_st0, k.gb_st1][t], 16)
    glu((0, 0))
    with pool.Fori(1, KW // 2) as i:
        glu((i, 0))
    pool.wait_ge(k.gb_st0, 8 * KW)
    pool.wait_ge(k.gb_st1, 8 * KW)
    end_phase(k, pool, 4)

    for br in range(3):
        wait(pool, k.g_lo, KW * br)
        pool.dma_start(k.gst[:, :, :], k.gated_d[br].rearrange("(t p) s -> p t s", p=P)).then_inc(k.ga_in, 16)
    end_phase(k, pool, 5)

    pool.dma_start(k.fg[:, :], k.final_g.partition_broadcast(P)).then_inc(k.fg_in, 16)
    x_v = k.x.rearrange("(m p) c -> p m c", p=P)
    for c in range(4):
        for m in range(NT):
            wait(pool, k.h_s, 4 * (c - 1) + m + 1)
            pool.dma_start(k.xr[:, m, :], x_v[:, m, c * S:(c + 1) * S]).then_inc(k.xr_in, 16)
    for m in range(NT):
        pool.wait_ge(k.fin, m + 1)
        pool.dma_start(k.out[m * P:(m + 1) * P, :], k.hrow[:, m, :]).then_inc(k.o_st, 16)
    pool.wait_ge(k.o_st, 16 * NT)


def tensor_program(k, pe):
    ps, mat = k.ps, k.mat
    ident, ones = mat["ident"], mat["ones"]

    pe.wait_ge(k.cst_in, 16)
    pe.wait_ge(k.rows_in, 160)
    pe.wait_ge(k.ldt_rows, 1)
    pe.transpose(ps[4][:, 0:P], k.rows1[:, :], ident).then_inc(k.prm_ps, 1)
    pe.transpose(ps[5][:, 0:P], k.rows2[:, :], ident).then_inc(k.prm_ps, 1)
    for t in range(KD):
        pe.wait_ge(k.x_scale, NT)
        wait(pe, k.u_f32, t - 3)
        for m in range(NT):
            mm = pe.transpose(ps[t % 4][:, m * P:(m + 1) * P], k.xs[:, m, t * P:(t + 1) * P], ident)
        mm.then_inc(k.x_tr, 1)
    pe.wait_ge(k.u_lo, KD)
    pe.wait_ge(k.wba_lo, 1)
    for m in range(NT):
        for t in range(KD):
            a = bass.ts(m, P)
            mm = mm3(pe, ps[6][:, m * 16:(m + 1) * 16], k.uh[:, t, a], k.ul[:, t, a],
                     k.wbah[:, t * 16:(t + 1) * 16], k.wbal[:, t * 16:(t + 1) * 16], t == 0, t == KD - 1)
    mm.then_inc(k.ba_ps, 1)
    for t in range(KD):
        pe.wait_ge(k.x_scale, NT + MT)
        pe.wait_ge(k.u_f32, KD + t - 3)
        for m in range(MT):
            mm = pe.transpose(ps[t % 4][:, m * P:(m + 1) * P], k.xs[:, m, t * P:(t + 1) * P], ident)
        mm.then_inc(k.x_tr, 1)
    pe.wait_ge(k.g_done, 1)
    pe.matmul(ps[7][:, 0:NT * HEADS], mat["upper"], k.hp[:, 3, :, :], start=True, stop=True).then_inc(k.gsum_ps, 1)
    end_phase(k, pe, 1)

    def at_big(j, b, acts=None):
        hl, n = ((k.uh, k.ul), S) if b >= 4 else ((k.mh, k.ml), MEM)
        for q in range(8):
            eighth(k, pe, B_XA + b, 8, j, q, *hl, n, k.xa_out, 0)

    def at_values(j):
        pe.wait_ge(k.xa_out, count(j, 8, 8))
        wait(pe, k.xa_og, count(j, 0, 2))
        for m in range(MT):
            for t in range(2):
                mm = pe.transpose(ps[2][:, (2 * m + t) * P:(2 * m + t + 1) * P], k.vt[:, t, m * P:(m + 1) * P], ident)
        mm.then_inc(k.xa_vtr, 1)

    def at_scores(j, m):
        wait(pe, k.xa_exp, count(j, m - 1, 4))
        for t in range(2):
            mm = pe.matmul(ps[4 + m % 2][:, 0:MEM], k.qx[:, t, m * P:(m + 1) * P], k.kt[:, t, :], start=t == 0, stop=t == 1)
        mm.then_inc(k.xa_sc, 1)

    def at_turn(j, n):
        pe.wait_ge(k.xa_p, count(j, 4, 4))
        wait(pe, k.xa_pt, count(j, n, 2))
        for m in range(NT):
            mm = pe.transpose(ps[6 + n][:, m * P:(m + 1) * P], k.px[:, m, n * P:(n + 1) * P], ident)
        mm.then_inc(k.xa_ptr, 1)

    def at_output(j, t):
        pe.wait_ge(k.xa_v, count(j, 1, 1))
        pe.wait_ge(k.xa_pt, count(j, 2, 2))
        wait(pe, k.xa_og, count(j, t, 2))
        for m in range(MT):
            mm = pe.matmul(ps[2 + t][:, :], k.vx[:, m, t * P:(t + 1) * P], k.ptx[:, m, :], start=m == 0, stop=m == MT - 1)
        mm.then_inc(k.xa_o, 1)

    def at_small(j, n):
        if n == 0:
            at_values(j)
            at_scores(j, 0)
            at_scores(j, 1)
        if n == 1:
            at_scores(j, 2)
            at_scores(j, 3)
        if n in (2, 3):
            at_turn(j, n - 2)
        if n == 4:
            at_output(j, 0)
            at_output(j, 1)

    for b in range(8):
        at_big((0, 0), b)
    for b in range(8):
        at_small((0, 0), b)
        at_big((1, 0), b)
    with pe.Fori(2, XH) as i:
        for b in range(8):
            at_small((i, -1), b)
            at_big((i, 0), b)
    for n in range(5):
        at_small((XH, -1), n)
    end_phase(k, pe, 2)

    def big(j, b, *eighths):
        for q in eighths:
            eighth(k, pe, B_MIX + b, 6, j, q, k.uh, k.ul, S, k.mx_out, B_MIX)

    def norm_keys(j):
        pe.wait_ge(k.sq, count(j, 2, 2))
        wait(pe, k.oroot, count(j, 0, 1))
        pe.matmul(ps[6][:, :], ones, k.rk[:, :], start=True, stop=True).then_inc(k.ss, 1)
        pe.wait_ge(k.gu, count(j, 1, 1))
        wait(pe, k.st_s, count(j, 0, 3))
        pe.matmul(ps[7][:, :], ones, k.gx[:, :, :], start=True, stop=True).then_inc(k.rsum, 1)

    def norm_queries(j):
        wait(pe, k.og, count(j, 0, 2))
        pe.matmul(ps[2][:, :], ones, k.rq[:, :], start=True, stop=True).then_inc(k.ss, 1)

    def values(j):
        pe.wait_ge(k.silu, count(j, 3, 3))
        pe.wait_ge(k.root, count(j, 2, 2))
        for n in range(NT):
            mm = pe.transpose(ps[2][:, n * P:(n + 1) * P], k.vc[:, n * P:(n + 1) * P], ident)
        mm.then_inc(k.vtr, 1)

    def keys(j):
        pe.wait_ge(k.qk, count(j, 1, 2))
        for n in range(NT):
            mm = pe.transpose(ps[6][:, n * P:(n + 1) * P], k.kc[:, n * P:(n + 1) * P], ident)
        mm.then_inc(k.ktr, 1)

    def keys_keys(j):
        pe.wait_ge(k.er_s, count(j, 1, 1))
        pe.wait_ge(k.dd, count(j, 1, 3))
        for n in range(NT):
            c = bass.ts(n, P)
            mm = pe.matmul(ps[7][:, c], k.kc[:, c], k.kc[:, c], start=True, stop=True)
        mm.then_inc(k.kk, 1)

    def keys_queries(j):
        pe.wait_ge(k.qk, count(j, 2, 2))
        pe.wait_ge(k.vb_s, count(j, 1, 1))
        for n in range(NT):
            c = bass.ts(n, P)
            mm = pe.matmul(ps[2][:, c], k.kc[:, c], k.qc[:, c], start=True, stop=True)
        mm.then_inc(k.kq, 1)

    def turn_lower(j):
        pe.wait_ge(k.lm, count(j, 1, 1))
        pe.wait_ge(k.kb, count(j, 2, 2))
        for n in range(NT):
            mm = pe.transpose(ps[6][:, n * P:(n + 1) * P], k.dl[:, n, :], ident)
        mm.then_inc(k.ltr, 1)

    def level_x(j, l):
        pe.wait_ge(k.lt_s, count(j, 1, 1))
        if l == 1:
            pe.wait_ge(k.tu_s, count(j, 4, 4))
            pe.wait_ge(k.qkt, count(j, 1, 1))
        else:
            pe.wait_ge(k.tus, count(j, 2 * (l - 1), 11))
        for n in range(NT):
            mm = pe.matmul(ps[2][:, n * P:(n + 1) * P], k.lt[:, n, :], k.tl[:, n, :], start=True, stop=True)
        mm.then_inc(k.lx, 1)

    def level_p(j, l):
        pe.wait_ge(k.xm, count(j, l, 6))
        for n in range(NT):
            c = bass.ts(n, P)
            if l < 6:
                pe.matmul(ps[6][:, c], k.tu[:, n, :], k.gx[:, n, :], start=True, stop=True)
            mm = pe.matmul(ps[7][:, c], k.gx[:, n, :], k.tu[:, n, :], start=True, stop=True)
        mm.then_inc(k.lp, 1)

    def weights(j):
        pe.wait_ge(k.tus, count(j, 11, 11))
        for n in range(NT):
            mm = pe.matmul(ps[2][:, n * P:(n + 1) * P], k.kbg[:, n, :], k.tu[:, n, :], start=True, stop=True)
        mm.then_inc(k.wt, 1)

    def new_values(j, n):
        if n == 0:
            pe.wait_ge(k.wtn, count(j, 1, 1))
        else:
            pe.wait_ge(k.st_s, count(j, n, 3))
        pe.wait_ge(k.vn_s, count(j, n, 4)) if n else None
        c = bass.ts(n, P)
        mm = pe.matmul(ps[6][:, c], k.tu[:, n, :], k.vb[:, n, :], start=True, stop=n == 0)
        if n:
            mm = pe.matmul(ps[6][:, c], k.dl[:, n, :], k.st[:, :], start=False, stop=True)
        mm.then_inc(k.vp, 1)

    def chunk_output(j, n):
        pe.wait_ge(k.vn_s, count(j, n + 1, 4))
        c = bass.ts(n, P)
        if n < NT - 1:
            pe.matmul(ps[7][:, 0:P], k.kd[:, n, :], k.vn[:, n, :], start=True, stop=True).then_inc(k.sp_s, 1)
        if n == 0:
            pe.wait_ge(k.pm, count(j, 4, 4))
            pe.wait_ge(k.qkt, count(j, 1, 1))
        mm = pe.matmul(ps[2][:, c], k.vn[:, n, :], k.du[:, n, :], start=True, stop=n == 0)
        if n:
            mm = pe.matmul(ps[2][:, c], k.st[:, :], k.qd[:, n, :], start=False, stop=True)
        mm.then_inc(k.op, 1)

    def output_norm(j):
        pe.wait_ge(k.osq, count(j, 1, 1))
        pe.matmul(ps[6][:, :], ones, k.lt[:, :, :], start=True, stop=True).then_inc(k.sso, 1)

    def s5_matrices(j):
        pe.wait_ge(k.s5_w, count(j, 13, 13))
        wait(pe, k.ysum, count(j, 0, 1))
        for n, t in enumerate((k.bpad[:, 0], k.bpad[:, 1])):
            pe.transpose(ps[5][:, n * P:(n + 1) * P], t.rearrange("p q g i -> p (q g i)"), ident)
        for n in range(2):
            mm = pe.transpose(ps[5][:, (2 + n) * P:(3 + n) * P], k.cpad[:, n].rearrange("p g s -> p (g s)"), ident)
        mm.then_inc(k.s5_tr, 1)

    def s5_inputs(j, q):
        pe.wait_ge(k.bc_s, count(j, 1, 1))
        pe.wait_ge(k.mx_out, count(j, 6, 6))
        wait(pe, k.mod, count(j, 8 * q - 2, 32))
        r = slice(32 * q, 32 * q + 32)
        pe.matmul(ps[3][:, :], k.bc[r, 0, :], k.xb[r, :], start=True, stop=True)
        pe.matmul(ps[4][:, :], k.bc[r, 1, :], k.xb[r, :], start=True, stop=True).then_inc(k.bu, 1)

    def s5_outputs(j, q):
        pe.wait_ge(k.dem, count(j, 6 * q + 6, 24))
        r = slice(32 * q, 32 * q + 32)
        pe.matmul(ps[5][r, :], k.bc[:, 2, r], k.hr[:, :], start=True, stop=False)
        pe.matmul(ps[5][r, :], k.bc[:, 3, r], k.hi[:, :], start=False, stop=True).then_inc(k.yp, 1)

    def mixer(a, j, l):
        if a: big(a, 0, 0)
        if l: weights(l)
        if a: big(a, 0, 1)
        if l: new_values(l, 0)
        if a: big(a, 0, 2)
        if l: chunk_output(l, 0)
        if a: big(a, 0, 3)
        if l: new_values(l, 1)
        if a: big(a, 0, 4)
        if l: chunk_output(l, 1); s5_outputs(l, 3)
        if a: big(a, 0, 5)
        if l: new_values(l, 2)
        if a: big(a, 0, 6)
        if l: chunk_output(l, 2)
        if a: big(a, 0, 7)
        if l: new_values(l, 3)
        if j: s5_matrices(j)
        if a: big(a, 1, 0)
        if l: chunk_output(l, 3)
        if a: big(a, 1, 1)
        if j: s5_inputs(j, 0)
        if a: big(a, 1, 2)
        if l: output_norm(l)
        if a: big(a, 1, 3, 4, 5)
        if j: norm_keys(j)
        if a: big(a, 1, 6, 7); big(a, 2, 0, 1)
        if j: norm_queries(j)
        if a: big(a, 2, 2)
        if j: keys(j); keys_keys(j); s5_inputs(j, 1)
        if a: big(a, 2, 3, 4)
        if j: values(j); s5_outputs(j, 0)
        if a: big(a, 2, 5, 6)
        if j: turn_lower(j)
        if a: big(a, 2, 7); big(a, 3, 0)
        if j: keys_queries(j)
        if a: big(a, 3, 1, 2)
        if j: level_x(j, 1); s5_inputs(j, 2)
        if a: big(a, 3, 3, 4)
        if j: level_p(j, 1)
        if a: big(a, 3, 5, 6)
        if j: level_x(j, 2)
        if a: big(a, 3, 7)
        if j: s5_outputs(j, 1)
        if a: big(a, 4, 0)
        if j: level_p(j, 2)
        if a: big(a, 4, 1, 2)
        if j: level_x(j, 3)
        if a: big(a, 4, 3, 4)
        if j: level_p(j, 3); s5_inputs(j, 3)
        if a: big(a, 4, 5, 6)
        if j: level_x(j, 4)
        if a: big(a, 4, 7); big(a, 5, 0)
        if j: level_p(j, 4)
        if a: big(a, 5, 1)
        if j: s5_outputs(j, 2)
        if a: big(a, 5, 2)
        if j: level_x(j, 5)
        if a: big(a, 5, 3)
        if j: level_p(j, 5)
        if a: big(a, 5, 4, 5)
        if j: level_x(j, 6)
        if a: big(a, 5, 6)
        if j: level_p(j, 6)
        if a: big(a, 5, 7)

    mixer((0, 0), None, None)
    mixer((1, 0), (0, 0), None)
    with pe.Fori(2, HEADS) as i:
        mixer((i, 0), (i, -1), (i, -2))
    mixer(None, (HEADS, -1), (HEADS, -2))
    mixer(None, None, (HEADS, -1))
    end_phase(k, pe, 3)

    def glu(j):
        for t in range(2):
            wait(pe, k.w_lo, count(j, B_GLU + t + 1, 2))
            wait(pe, [k.gv0, k.gv1][t], count(j, 0, 2))
            if t == 0:
                pe.wait_ge(k.y_lo, KW)
            row_tiles(k, pe, t, ps[t][:, :], range(KW), 0, k.gh, k.gl, KW)
            row_tiles(k, pe, t, ps[2 + t][:, :], range(KW), KW, k.gh, k.gl, KW).then_inc(k.w_used, 1)

    glu((0, 0))
    with pe.Fori(1, KW // 2) as i:
        glu((i, 0))
    end_phase(k, pe, 4)

    def merge(br, j):
        for pair in range(2):
            b0 = B_BR + 24 * br + 3 * pair
            for n in range(2):
                d = 2 * pair + n
                wait(pe, k.w_lo, count(j, b0 + n + 1, 6))
                wait(pe, k.gate_s, count(j, 16 * br + d - 3, 4))
                row_tiles(k, pe, (b0 + n) % 2, ps[d][:, :], range(KD), 0, k.uh, k.ul, KD).then_inc(k.w_used, 1)
            wait(pe, k.w_lo, count(j, b0 + 3, 6))
            if pair == 0:
                pe.wait_ge(k.g_lo, KW * (br + 1))
            for n in range(2):
                d = 2 * pair + n
                wait(pe, k.prod, count(j, 16 * br + d - 3, 4))
                mm = row_tiles(k, pe, b0 % 2, ps[4 + d][:, :], range(KW), n * KW, k.gh, k.gl, KW)
                mm.then_inc(k.w_used if n else k.p_ps, 1)

    for br in range(3):
        merge(br, (0, 0))
        with pe.Fori(1, KD // 4) as i:
            merge(br, (i, 0))
    end_phase(k, pe, 5)

    for c in range(4):
        for kb in range(4):
            b = B_OUT + 4 * c + kb
            slot = b % 2
            pe.wait_ge(k.w_lo, b + 1)
            if kb == 0:
                wait(pe, k.h_s, 4 * (c - 1))
            for m in range(NT):
                for n in range(4):
                    t = 4 * kb + n
                    if m == 0 and c == 0:
                        pe.wait_ge(k.m_lo, t + 1)
                    a, w = bass.ts(m, P), bass.ts(n, S)
                    mm = mm3(pe, ps[4 * (c % 2) + m][:, :], k.uh[:, t, a], k.ul[:, t, a],
                             k.wh[slot][:, w], k.wl[slot][:, w], t == 0, t == KD - 1)
                if kb == 3 and m < 3:
                    mm.then_inc(k.o_ps, 1)
            mm.then_inc(k.w_used, 1)


def scalar_program(k, act):
    ps, col = k.ps, k.col

    done = [0]

    def step(instruction):
        instruction.then_inc(k.alink, 1)
        done[0] += 1
        act.wait_ge(k.alink, done[0])

    act.wait_ge(k.cst_in, 16)
    act.wait_ge(k.x_in, 16 * NT)
    for m in range(NT):
        step(act.activation(k.junk[:, :], k.xs[:, m, :], ACT.Square, accum_out=k.stat[:, m:m + 1]))
    act.activation(k.stat[:, 8:12], k.stat[:, 0:4], ACT.Sqrt, bias=col["eps"], scale=1 / D).then_inc(k.x_root, 1)

    def tile_hi(hi, t, n):
        act.wait_ge(k.u_f32, t + 1)
        act.activation(hi, [k.ut0, k.ut1][t % 2][:, 0:n], ACT.Copy).then_inc(k.u_hi, 1)

    for t in range(KD):
        tile_hi(k.uh[:, t, :], t, S)
    act.wait_ge(k.wba_in, 16)
    act.activation(k.wbah[:, :], k.wba[:, :], ACT.Copy).then_inc(k.wba_hi, 1)
    act.wait_ge(k.mem_in, 16 * MT)
    for m in range(MT):
        step(act.activation(k.junk[:, :], k.xs[:, m, :], ACT.Square, accum_out=k.stat[:, 4 + m:5 + m]))
    act.activation(k.stat[:, 12:14], k.stat[:, 4:6], ACT.Sqrt, bias=col["eps"], scale=1 / D).then_inc(k.x_root, 1)
    for t in range(KD):
        tile_hi(k.mh[:, t, :], KD + t, MEM)
    tp = k.tp
    act.wait_ge(k.prm, 2)
    act.activation(tp[:, 0, :], k.prm2[:, 64:96], ACT.Exp).then_inc(k.p_act, 1)
    act.wait_ge(k.p_dve, 1)
    act.activation(tp[:, 2, :], tp[:, 1, :], ACT.Exp).then_inc(k.p_act, 1)
    act.wait_ge(k.p_dve, 2)
    step(act.activation(tp[:, 4, :], tp[:, 3, :], ACT.Sin, scale=TWO_PI))
    step(act.activation(tp[:, 5, :], tp[:, 3, :], ACT.Abs))
    act.activation(tp[:, 5, :], tp[:, 5, :], ACT.Sin, scale=-TWO_PI, bias=col["quarter"]).then_inc(k.p_act, 1)
    act.wait_ge(k.ba_ps, 1)
    ba = ps[6][:, 0:NT * 16].rearrange("p (m c) -> p m c", m=NT)
    act.activation(k.hp[:, 0, :, :], ba[:, :, 0:HEADS], ACT.Exp, scale=-1.0).then_inc(k.p_act, 1)
    act.wait_ge(k.p_dve, 3)
    step(act.activation(k.hp[:, 2, :, :], k.hp[:, 1, :, :], ACT.Abs))
    step(act.activation(k.hp[:, 2, :, :], k.hp[:, 2, :, :], ACT.Exp, scale=-1.0))
    act.activation(k.alog_b[:, :], k.alog_b[:, :], ACT.Exp).then_inc(k.p_act, 1)
    act.wait_ge(k.p_dve, 4)
    act.activation(k.hp[:, 2, :, :], k.hp[:, 2, :, :], ACT.Ln).then_inc(k.p_act, 1)
    act.wait_ge(k.gsum_ps, 1)
    act.activation(k.hp[:, 2, :, :], ps[7][:, 0:NT * HEADS].rearrange("p (m h) -> p m h", m=NT), ACT.Exp).then_inc(k.p_act, 1)
    split_hi(k, act, B_XA)
    end_phase(k, act, 1)

    def at_exp(j, m):
        act.wait_ge(k.xa_max, count(j, 2 * m + 2, 8))
        wait(act, k.xa_ptr, count(j, 0, 2))
        act.activation(k.px[:, m, :], ps[4 + m % 2][:, 0:MEM], ACT.Exp, bias=k.stat[:, 24 + m:25 + m],
                       scale=1 / 16, accum_out=k.stat[:, 28 + m:29 + m]).then_inc(k.xa_exp, 1)

    def at_out(j, b):
        act.wait_ge(k.w_used, count(j, B_XA + b + 1, 8))
        o = ps[b % 2]
        if b < 2 or b in (4, 5):
            wait(act, k.xa_sc, count(j, 0, 4))
        elif b < 4:
            wait(act, k.xa_vtr, count(j, 0, 1))
        else:
            wait(act, k.xa_og, count(j, 0, 2))
        t = b % 2
        if b < 4:
            act.activation([k.kt, k.vt][b // 2][:, t, :], o[:, 0:MEM], ACT.Copy).then_inc(k.xa_out, 1)
        else:
            act.activation([k.qx, k.zx][b // 2 - 2][:, t, :], o[:, :], ACT.Copy if b < 6 else ACT.Silu).then_inc(k.xa_out, 1)

    def attention(a, j):
        for b in range(8):
            if a: split_hi(k, act, B_XA + b + 1, 8, a)
            if j and b < 2: at_exp(j, 2 * b); at_exp(j, 2 * b + 1)
            if a: at_out(a, b)

    attention((0, 0), None)
    attention((1, 0), (0, 0))
    with act.Fori(2, XH) as i:
        attention((i, 0), (i, -1))
    attention(None, (XH, -1))
    end_phase(k, act, 2)

    def tile_out(a, b):
        act.wait_ge(k.w_used, count(a, B_MIX + b + 1, 6))
        o = ps[b % 2]
        if b < 3:
            wait(act, k.conv, count(a, 4 * b + 4 - 12, 12))
            act.activation([k.qraw, k.kraw, k.vraw][b][:, 3:3 + S], o[:, :], ACT.Copy).then_inc(k.mx_out, 1)
        elif b == 3:
            wait(act, k.zb_st, count(a, 0, 16))
            act.activation(k.zbs[:, :], o[:, :], ACT.Silu).then_inc(k.mx_out, 1)
        elif b == 4:
            wait(act, k.z_kept, count(a, 0, 1))
            act.activation(k.zs[:, :], o[:, :], ACT.Silu).then_inc(k.mx_out, 1)
        else:
            wait(act, k.ysum, count(a, 0, 1))
            wait(act, k.bu, count(a, 0, 4))
            act.activation(k.xb[:, :], o[:, :], ACT.Copy).then_inc(k.mx_out, 1)

    def s5_tables(j, q):
        c, s = [k.tcos0, k.tcos1][q % 2], [k.tsin0, k.tsin1][q % 2]
        n = count(j, 3 * q, 12)
        act.wait_ge(k.args, count(j, 7 * q + 7, 28))
        wait(act, k.dem, count(j, 6 * (q - 1), 24))
        wait(act, k.mod, count(j, 8 * (q - 1), 32))
        act.activation(s[:, :], k.farg[:, :], ACT.Sin, scale=TWO_PI).then_inc(k.tab, 1)
        act.activation(c[:, :], k.farg[:, :], ACT.Abs).then_inc(k.tab, 1)
        act.wait_ge(k.tab, n + 2)
        act.activation(c[:, :], c[:, :], ACT.Sin, scale=-TWO_PI, bias=col["quarter"]).then_inc(k.tab, 1)

    def s5_matrices(j):
        act.wait_ge(k.s5_tr, count(j, 1, 1))
        wait(act, k.yp, count(j, 0, 4))
        act.activation(k.bc[:, :, :], ps[5][:, :].rearrange("p (n c) -> p n c", n=4), ACT.Copy).then_inc(k.bc_s, 1)

    def activation_of(j, n):
        t, sq = ((k.qc, k.rq), (k.kc, k.rk), (k.vc, None))[n]
        act.wait_ge(k.conv, count(j, 4 * n + 4, 12))
        act.activation(t[:, :], t[:, :], ACT.Silu).then_inc(k.silu, 1)
        if sq is not None:
            act.wait_ge(k.silu, count(j, n + 1, 3))
            act.activation(sq[:, :], t[:, :], ACT.Square).then_inc(k.sq, 1)

    def key_root(j):
        act.wait_ge(k.ss, count(j, 1, 2))
        act.activation(k.rk[:, :], ps[6][:, :], ACT.Sqrt, bias=col["eps"]).then_inc(k.root, 1)
        act.wait_ge(k.rsum, count(j, 1, 1))
        act.activation(k.er[:, :, :], ps[7][:, :].rearrange("p (n c) -> p n c", n=NT), ACT.Exp).then_inc(k.er_s, 1)

    def query_root(j):
        act.wait_ge(k.ss, count(j, 2, 2))
        act.activation(k.rq[:, :], ps[2][:, :], ACT.Sqrt, bias=col["eps128"], scale=float(P)).then_inc(k.root, 1)

    def decays(j):
        act.wait_ge(k.dd, count(j, 2, 3))
        act.activation(k.du[:, :, :], k.du[:, :, :], ACT.Exp).then_inc(k.dec, 1)
        act.wait_ge(k.dd, count(j, 3, 3))
        act.activation(k.dl[:, :, :], k.dl[:, :, :], ACT.Exp, scale=-1.0).then_inc(k.dec, 1)

    def keep_z(j):
        wait(act, k.og, count(j, 0, 2))
        act.activation(k.zk[:, :], k.zs[:, :], ACT.Copy).then_inc(k.z_kept, 1)

    def lower_turned(j):
        act.wait_ge(k.ltr, count(j, 1, 1))
        wait(act, k.lx, count(j, 0, 6))
        wait(act, k.og, count(j, 0, 2))
        act.activation(k.lt[:, :, :], ps[6][:, :].rearrange("p (n c) -> p n c", n=NT), ACT.Copy).then_inc(k.lt_s, 1)

    def weights_out(l):
        act.wait_ge(k.wt, count(l, 1, 1))
        act.activation(k.dl[:, :, :], ps[2][:, :].rearrange("p (n c) -> p n c", n=NT), ACT.Copy, scale=-1.0).then_inc(k.wtn, 1)

    def new_values(l, n):
        act.wait_ge(k.vp, count(l, n + 1, 4))
        act.activation(k.vn[:, n, :], ps[6][:, n * P:(n + 1) * P], ACT.Copy).then_inc(k.vn_s, 1)

    def output_squares(l):
        act.wait_ge(k.op, count(l, 4, 4))
        act.activation(k.lt[:, :, :], ps[2][:, :].rearrange("p (n c) -> p n c", n=NT), ACT.Square).then_inc(k.osq, 1)

    def output_root(l):
        act.wait_ge(k.sso, count(l, 1, 1))
        act.activation(k.lt[:, :, :], ps[6][:, :].rearrange("p (n c) -> p n c", n=NT), ACT.Sqrt, bias=col["eps"],
                       scale=1 / P).then_inc(k.oroot, 1)

    def mixer(a, j, l):
        split = lambda b: split_hi(k, act, B_MIX + b + 1, 6, a)
        if a: split(0)
        if l: weights_out(l); new_values(l, 0); new_values(l, 1); new_values(l, 2)
        if j: tile_out(j, 5)
        if l: new_values(l, 3)
        if j: activation_of(j, 0)
        if a: tile_out(a, 0); split(1)
        if l: output_squares(l)
        if j: s5_matrices(j); activation_of(j, 1); activation_of(j, 2); s5_tables(j, 0)
        if l: output_root(l)
        if j: key_root(j); s5_tables(j, 1)
        if a: tile_out(a, 1); split(2)
        if j: query_root(j); decays(j); keep_z(j)
        if a: tile_out(a, 2); split(3)
        if j: lower_turned(j); s5_tables(j, 2)
        if a: tile_out(a, 3); split(4)
        if j: s5_tables(j, 3)
        if a: tile_out(a, 4); split(5)

    mixer((0, 0), None, None)
    mixer((1, 0), (0, 0), None)
    with act.Fori(2, HEADS) as i:
        mixer((i, 0), (i, -1), (i, -2))
    mixer(None, (HEADS, -1), (HEADS, -2))
    mixer(None, None, (HEADS, -1))
    end_phase(k, act, 3)

    act.wait_ge(k.y_in, 16)
    for t in range(KW):
        act.activation(k.yst[:, t, :], k.yst[:, t, :], ACT.Gelu_apprx_tanh).then_inc(k.y_act, 1)
    for t in range(KW):
        act.wait_ge(k.y_act, t + 1)
        act.activation(k.gh[:, t, :], k.yst[:, t, :], ACT.Copy).then_inc(k.y_hi, 1)
    def glu(j):
        for t in range(2):
            split_hi(k, act, B_GLU + t + 1, 2, j)
            act.wait_ge(k.w_used, count(j, B_GLU + t + 1, 2))
            wait(act, [k.gb_st0, k.gb_st1][t], count(j, 0, 16))
            act.activation([k.gg0, k.gg1][t][:, :], ps[2 + t][:, :], ACT.Sigmoid).then_inc(k.sig, 1)

    glu((0, 0))
    with act.Fori(1, KW // 2) as i:
        glu((i, 0))
    end_phase(k, act, 4)

    for br in range(3):
        def branch_hi():
            act.wait_ge(k.ga_in, 16 * (br + 1))
            for t in range(KW):
                act.activation(k.gh[:, t, :], k.gst[:, t, :], ACT.Copy).then_inc(k.g_hi, 1)
        wait(act, k.w_used, B_BR + 24 * br)
        branch_hi()
        def merge(j):
            for pair in range(2):
                b0 = B_BR + 24 * br + 3 * pair
                for n in range(2):
                    d = 2 * pair + n
                    split_hi(k, act, b0 + n + 1, 6, j)
                    act.wait_ge(k.w_used, count(j, b0 + n + 1, 6))
                    wait(act, k.prod, count(j, 16 * br + d - 1, 4))
                    if br:
                        wait(act, k.mrg, count(j, 16 * br + d - 17, 4))
                    act.activation([k.sg0, k.sg1][n][:, :], ps[d][:, :], ACT.Sigmoid).then_inc(k.gate_s, 1)
                split_hi(k, act, b0 + 3, 6, j)

        merge((0, 0))
        with act.Fori(1, KD // 4) as i:
            merge((i, 0))
    end_phase(k, act, 5)

    for t in range(KD):
        act.activation(k.uh[:, t, :], k.merged[:, t, :], ACT.Copy).then_inc(k.m_hi, 1)
    for c in range(4):
        for kb in range(4):
            w = B_OUT + 4 * c + kb + 1
            if w < N_BLOCKS:
                split_hi(k, act, w)
        for m in range(NT):
            n = 4 * c + m
            act.wait_ge(k.h_s, n + 1)
            wait(act, k.h_sq, n)
            act.activation(k.xsq[:, :], k.hrow[:, m, c * S:(c + 1) * S], ACT.Square,
                           accum_out=k.ssq[:, m, c:c + 1]).then_inc(k.h_sq, 1)
    act.wait_ge(k.p_dve, 6)
    act.activation(k.stat[:, 8:12], k.stat[:, 0:4], ACT.Sqrt, bias=col["eps"], scale=1 / D).then_inc(k.p_act, 1)


def vector_program(k, dve):
    ps, mat, col, stat, tp, hp = k.ps, k.mat, k.col, k.stat, k.tp, k.hp
    done = [0]

    def step(instruction):
        instruction.then_inc(k.link, 1)
        done[0] += 1
        dve.wait_ge(k.link, done[0])

    tt, ts, stt = dve.tensor_tensor, dve.tensor_scalar, dve.scalar_tensor_tensor

    dve.wait_ge(k.rows_in, 160)
    dve.tensor_copy(k.rows2[64:96, :].rearrange("q (g s) -> q g s", g=2),
                    k.ldt2[64:96, :].unsqueeze(2).to_broadcast([32, 2, NS])).then_inc(k.ldt_rows, 1)
    dve.wait_ge(k.prm_ps, 2)
    dve.tensor_copy(k.prm1[:, :], ps[4][:, 0:P]).then_inc(k.prm, 1)
    dve.tensor_copy(k.prm2[:, :], ps[5][:, 0:P]).then_inc(k.prm, 1)
    dve.wait_ge(k.prm, 2)

    def scale_rows(first, n, at_root):
        dve.wait_ge(k.x_root, at_root)
        step(dve.reciprocal(stat[:, 16 + first:16 + first + n], stat[:, 8 + first:8 + first + n]))
        for m in range(n):
            ts(k.xs[:, m, :], k.xs[:, m, :], stat[:, 16 + first + m:17 + first + m], None, ALU.mult).then_inc(k.x_scale, 1)

    def tile_out(t, gain, hi, lo, n):
        u = [k.ut0, k.ut1][t % 2]
        dve.wait_ge(k.x_tr, t + 1)
        wait(dve, k.u_hi, t - 1)
        wait(dve, k.u_lo, t - 1)
        ts(u[:, 0:n], ps[t % 4][:, 0:n], gain, None, ALU.mult).then_inc(k.u_f32, 1)
        dve.wait_ge(k.u_hi, t + 1)
        tt(lo, u[:, 0:n], hi.bitcast(F32), ALU.subtract).then_inc(k.u_lo, 1)

    scale_rows(0, NT, 1)
    for t in range(KD):
        tile_out(t, k.prm1[:, 96 + t:97 + t], k.uh[:, t, :], k.ul[:, t, :], S)
    dve.wait_ge(k.wba_hi, 1)
    tt(k.wbal[:, :], k.wba[:, :], k.wbah[:, :].bitcast(F32), ALU.subtract).then_inc(k.wba_lo, 1)
    scale_rows(4, MT, 2)
    for t in range(KD):
        tile_out(KD + t, k.prm1[:, 112 + t:113 + t], k.mh[:, t, :], k.ml[:, t, :], MEM)

    lr, li = k.prm2[:, 0:32], k.prm2[:, 32:64]
    T = lambda n: tp[:, n, :]
    dve.wait_ge(k.p_act, 1)
    tt(T(1), lr, T(0), ALU.mult).then_inc(k.p_dve, 1)
    step(tt(T(6), li, T(0), ALU.mult))
    step(ts(T(7), T(6), 1 / TWO_PI, ROUND, ALU.mult, ALU.add))
    step(ts(T(7), T(7), -ROUND, None, ALU.add))
    for part in (PI_A, PI_B, PI_C):
        step(stt(T(6), T(7), -part, T(6), ALU.mult, ALU.add))
    step(ts(T(8), T(6), 1 / TWO_PI, ROUND14, ALU.mult, ALU.add))
    step(ts(k.s5p[:, 1, :], T(8), -ROUND14, None, ALU.add))
    for part in (PI_A, PI_B, PI_C):
        step(stt(T(6), k.s5p[:, 1, :], -part, T(6), ALU.mult, ALU.add))
    step(ts(k.s5p[:, 2, :], T(6), 1 / TWO_PI, None, ALU.mult))
    step(tt(T(3), k.s5p[:, 1, :], k.s5p[:, 2, :], ALU.add))
    ts(T(3), T(3), 0.4999999, -0.4999999, ALU.min, ALU.max).then_inc(k.p_dve, 1)
    dve.wait_ge(k.p_act, 3)
    step(dve.tensor_copy(k.s5p[:, 0, :], T(2)))
    step(tt(T(5), T(2), T(5), ALU.mult))
    step(ts(T(5), T(5), -1.0, None, ALU.add))
    step(tt(T(4), T(2), T(4), ALU.mult))
    step(tt(T(9), lr, lr, ALU.mult))
    step(tt(T(10), li, li, ALU.mult))
    step(tt(T(9), T(9), T(10), ALU.add))
    step(dve.reciprocal(T(9), T(9)))
    for n, (a, b, op) in enumerate(((T(5), T(4), ALU.add), (T(4), T(5), ALU.subtract))):
        step(tt(T(11), a, lr, ALU.mult))
        step(tt(T(12), b, li, ALU.mult))
        step(tt(T(11), T(11), T(12), op))
        step(tt(k.s5p[:, 3 + n, :], T(11), T(9), ALU.mult))

    ba = ps[6][:, 0:NT * 16].rearrange("p (m c) -> p m c", m=NT)
    rep = lambda v: v.unsqueeze(1).to_broadcast([P, NT, HEADS])
    dve.wait_ge(k.p_act, 4)
    step(ts(hp[:, 0, :, :], hp[:, 0, :, :], 1.0, None, ALU.add))
    step(dve.reciprocal(hp[:, 0, :, :], hp[:, 0, :, :]))
    tt(hp[:, 1, :, :], ba[:, :, HEADS:16], rep(k.dtb_b[:, :]), ALU.add).then_inc(k.p_dve, 1)
    dve.wait_ge(k.p_act, 5)
    ts(hp[:, 2, :, :], hp[:, 2, :, :], 1.0, None, ALU.add).then_inc(k.p_dve, 1)
    dve.wait_ge(k.p_act, 6)
    step(stt(hp[:, 2, :, :], hp[:, 1, :, :], 0.0, hp[:, 2, :, :], ALU.max, ALU.add))
    step(tt(hp[:, 2, :, :], hp[:, 2, :, :], rep(k.alog_b[:, :]), ALU.mult))
    ts(hp[:, 3, :, :], hp[:, 2, :, :], -1.0, None, ALU.mult).then_inc(k.g_done, 1)
    dve.wait_ge(k.p_act, 7)
    step(dve.tensor_copy(hp[:, 1, :, :], ps[7][:, 0:NT * HEADS].rearrange("p (m h) -> p m h", m=NT)))
    step(tt(hp[:, 2, :, :], hp[:, 2, :, :], hp[:, 0, :, :], ALU.mult))
    split_lo(k, dve, B_XA)
    end_phase(k, dve, 1)

    def at_max(j, m):
        dve.wait_ge(k.xa_sc, count(j, m + 1, 4))
        wait(dve, k.xa_exp, count(j, m - 3, 4))
        dve.reduce_max(stat[:, 20 + m:21 + m], ps[4 + m % 2][:, 0:MEM], AX_X).then_inc(k.xa_max, 1)
        dve.wait_ge(k.xa_max, count(j, 2 * m + 1, 8))
        ts(stat[:, 24 + m:25 + m], stat[:, 20 + m:21 + m], -1 / 16, None, ALU.mult).then_inc(k.xa_max, 1)

    def at_norm(j, m):
        dve.wait_ge(k.xa_exp, count(j, m + 1, 4))
        dve.reciprocal(stat[:, 32 + m:33 + m], stat[:, 28 + m:29 + m]).then_inc(k.xa_sum, 1)
        dve.wait_ge(k.xa_sum, count(j, m + 1, 4))
        ts(k.px[:, m, :], k.px[:, m, :], stat[:, 32 + m:33 + m], None, ALU.mult).then_inc(k.xa_p, 1)

    def at_small(j, n):
        if n == 0:
            dve.wait_ge(k.xa_vtr, count(j, 1, 1))
            wait(dve, k.xa_o, count(j, 0, 2))
            dve.tensor_copy(k.vx[:, :, :], ps[2][:, :].rearrange("p (m c) -> p m c", m=MT)).then_inc(k.xa_v, 1)
        if n < 2:
            at_max(j, 2 * n)
            at_max(j, 2 * n + 1)
            at_norm(j, 2 * n)
            at_norm(j, 2 * n + 1)
        elif n < 4:
            dve.wait_ge(k.xa_ptr, count(j, n - 1, 2))
            wait(dve, k.xa_o, count(j, 0, 2))
            dve.tensor_copy(k.ptx[:, n - 2, :], ps[4 + n][:, :]).then_inc(k.xa_pt, 1)
        elif n == 4:
            for t in range(2):
                dve.wait_ge(k.xa_o, count(j, t + 1, 2))
                wait(dve, [k.xa_st0, k.xa_st1][t], count(j, 0, 16))
                tt(k.ox[:, t, :], ps[2 + t][:, :], k.zx[:, t, :], ALU.mult).then_inc(k.xa_og, 1)

    def attention(a, j):
        for b in range(8):
            if a: split_lo(k, dve, B_XA + b + 1, 8, a)
            if j: at_small(j, b)

    attention((0, 0), None)
    attention((1, 0), (0, 0))
    with dve.Fori(2, XH) as i:
        attention((i, 0), (i, -1))
    attention(None, (XH, -1))
    end_phase(k, dve, 2)

    def chunked(v):
        return v.rearrange("p (n c) -> p n c", n=NT)

    def rows(v):
        return v.unsqueeze(2).to_broadcast([P, NT, P])

    def rep_chunks(m):
        return m.unsqueeze(1).to_broadcast([P, NT, P])

    def head_parameters(j):
        h = at(j)
        wait(dve, k.args, count(j, 0, 28))
        wait(dve, k.pm, count(j, 0, 4))
        dve.tensor_copy(k.s5h[:, :, :], k.s5p[:, :, bass.ds(4 * h, 4)]).then_inc(k.sliced, 1)
        dve.tensor_copy(k.cwh[:, :, :], k.prm1[:, 0:96].rearrange("p (n r h) -> p n r h", n=CONV, r=3)[:, :, :, bass.ds(h, 1)]).then_inc(k.sliced, 1)
        dve.tensor_copy(k.hph[:, :, :], hp[:, :, :, bass.ds(h, 1)]).then_inc(k.sliced, 1)
        dve.wait_ge(k.sliced, count(j, 3, 3))

    def s5_matrices(j):
        w = k.s5_w
        dve.tensor_copy(k.dh[:, :], k.prm2[:, 96:104][:, bass.ds(at(j), 1)]).then_inc(w, 1)
        dve.wait_ge(k.s5_in, count(j, 64, 64))
        cre, cim = (k.s5h[:, n, :].unsqueeze(2).to_broadcast([P, 4, GS]) for n in (3, 4))
        br, bi = k.braw[:, 0, :, :], k.braw[:, 1, :, :]
        for n, (b, c) in enumerate(((br, cre), (bi, cim), (bi, cre), (br, cim))):
            tt(k.bt[:, n, :, :], b, c, ALU.mult).then_inc(w, 1)
        dve.wait_ge(w, count(j, 5, 13))
        wait(dve, k.s5_tr, count(j, 0, 1))
        for n, op in ((0, ALU.subtract), (1, ALU.add)):
            for g in range(2):
                r = slice(64 * g, 64 * g + 64)
                tt(k.bpad[r, n, :, g, :], k.bt[r, 2 * n, :, :], k.bt[r, 2 * n + 1, :, :], op).then_inc(w, 1)
        for n, names in enumerate((("even", "odd"), ("neven", "nodd"))):
            for g in range(2):
                ts(k.cpad[:, n, g, :], k.craw[:, n, :], col[names[g]], None, ALU.mult).then_inc(w, 1)

    def convolve(j, part):
        src, dst = [k.qraw, k.kraw, k.vraw][part], [k.qc, k.kc, k.vc][part]
        n = count(j, 4 * part, 12)
        dve.wait_ge(k.mx_out, count(j, part + 1, 6))
        wait(dve, k.kq, count(j, 0, 1))
        wait(dve, k.kk, count(j, 0, 1))
        wait(dve, k.vtr, count(j, 0, 1))
        ts(dst[:, :], src[:, 0:S], k.cwh[:, 0, part:part + 1], None, ALU.mult).then_inc(k.conv, 1)
        for t in range(1, CONV):
            dve.wait_ge(k.conv, n + t)
            stt(dst[:, :], src[:, t:t + S], k.cwh[:, t, part:part + 1], dst[:, :], ALU.mult, ALU.add).then_inc(k.conv, 1)

    def log_decays(j):
        tt(k.gx[:, :, :], rep_chunks(mat["upper"]), rows(k.hph[:, 3, :]), ALU.mult).then_inc(k.gu, 1)

    def differences(j):
        dve.wait_ge(k.rsum, count(j, 1, 1))
        dve.wait_ge(k.er_s, count(j, 1, 1))
        wait(dve, k.vp, count(j, 0, 4))
        wait(dve, k.op, count(j, 0, 4))
        tt(k.dl[:, :, :], chunked(ps[7][:, :]), rows(k.hph[:, 1, :]), ALU.subtract).then_inc(k.dd, 1)
        dve.wait_ge(k.dd, count(j, 1, 3))
        ts(k.du[:, :, :], k.dl[:, :, :], 0.0, None, ALU.min).then_inc(k.dd, 1)
        ts(k.dl[:, :, :], k.dl[:, :, :], 0.0, None, ALU.max).then_inc(k.dd, 1)

    def normed_keys(j):
        dve.wait_ge(k.root, count(j, 1, 2))
        dve.reciprocal(k.rk[:, :], k.rk[:, :]).then_inc(k.rn, 1)
        dve.wait_ge(k.rn, count(j, 1, 2))
        tt(k.kc[:, :], k.kc[:, :], k.rk[:, :], ALU.mult).then_inc(k.qk, 1)

    def normed_queries(j):
        dve.wait_ge(k.root, count(j, 2, 2))
        dve.reciprocal(k.rq[:, :], k.rq[:, :]).then_inc(k.rn, 1)
        dve.wait_ge(k.rn, count(j, 2, 2))
        tt(k.qc[:, :], k.qc[:, :], k.rq[:, :], ALU.mult).then_inc(k.qk, 1)

    def values(j):
        dve.wait_ge(k.vtr, count(j, 1, 1))
        tt(k.vb[:, :, :], chunked(ps[2][:, :]), rows(k.hph[:, 0, :]), ALU.mult).then_inc(k.vb_s, 1)

    def keys(j):
        dve.wait_ge(k.ktr, count(j, 1, 1))
        dve.wait_ge(k.dec, count(j, 2, 2))
        wait(dve, k.wt, count(j, 0, 1))
        wait(dve, k.sp_s, count(j, 0, 3))
        dve.wait_ge(k.pm, count(j, 3, 4))
        wait(dve, k.g_st, count(j, 0, 16))
        tt(k.kbg[:, :, :], chunked(ps[6][:, :]), rows(k.hph[:, 2, :]), ALU.mult).then_inc(k.kb, 1)
        tt(k.kd[:, :, :], chunked(ps[6][:, :]), k.du[:, :, P - 1:P].to_broadcast([P, NT, P]), ALU.mult).then_inc(k.kb, 1)

    def system(j):
        dve.wait_ge(k.kk, count(j, 1, 1))
        dve.wait_ge(k.pm, count(j, 2, 4))
        tt(k.dl[:, :, :], chunked(ps[7][:, :]), k.dl[:, :, :], ALU.mult).then_inc(k.lm, 1)

    def queries(j):
        dve.wait_ge(k.kq, count(j, 1, 1))
        dve.wait_ge(k.pm, count(j, 3, 4))
        tt(k.du[:, :, :], chunked(ps[2][:, :]), k.du[:, :, :], ALU.mult).then_inc(k.qkt, 1)

    def first_level(j):
        dve.wait_ge(k.lm, count(j, 1, 1))
        wait(dve, k.lx, count(j, 0, 6))
        tt(k.tl[:, :, :], k.dl[:, :, :], rep_chunks(mat["low1"]), ALU.mult).then_inc(k.tu_s, 1)
        dve.wait_ge(k.lt_s, count(j, 1, 1))
        tt(k.tu[:, :, :], k.lt[:, :, :], rep_chunks(mat["up1"]), ALU.mult).then_inc(k.tu_s, 1)
        dve.wait_ge(k.tu_s, count(j, 1, 4))
        tt(k.tl[:, :, :], rep_chunks(mat["ident"]), k.tl[:, :, :], ALU.subtract).then_inc(k.tu_s, 1)
        dve.wait_ge(k.tu_s, count(j, 2, 4))
        tt(k.tu[:, :, :], rep_chunks(mat["ident"]), k.tu[:, :, :], ALU.subtract).then_inc(k.tu_s, 1)

    def level_x(j, l):
        dve.wait_ge(k.lx, count(j, l, 6))
        tt(k.gx[:, :, :], chunked(ps[2][:, :]), rep_chunks(mat[f"low{2 ** l}"]), ALU.mult).then_inc(k.xm, 1)

    def level_p(j, l):
        dve.wait_ge(k.lp, count(j, l, 6))
        if l < 6:
            tt(k.tl[:, :, :], k.tl[:, :, :], chunked(ps[6][:, :]), ALU.subtract).then_inc(k.tus, 1)
        tt(k.tu[:, :, :], k.tu[:, :, :], chunked(ps[7][:, :]), ALU.subtract).then_inc(k.tus, 1)

    def state(j, n):
        dve.wait_ge(k.sp_s, count(j, n + 1, 3))
        dve.wait_ge(k.op, count(j, n + 1, 4))
        if n == 0:
            dve.tensor_copy(k.st[:, :], ps[7][:, 0:P]).then_inc(k.st_s, 1)
        else:
            stt(k.st[:, :], k.st[:, :], k.er[:, n, P - 1:P], ps[7][:, 0:P], ALU.mult, ALU.add).then_inc(k.st_s, 1)

    def gated(j):
        dve.wait_ge(k.oroot, count(j, 1, 1))
        dve.reciprocal(k.tl[:, :, :], k.lt[:, :, :]).then_inc(k.orn, 1)
        dve.wait_ge(k.orn, count(j, 1, 1))
        stt(k.kbg[:, :, :], chunked(ps[2][:, :]), k.prm2[:, 104:105], k.tl[:, :, :], ALU.mult, ALU.mult).then_inc(k.og, 1)
        dve.wait_ge(k.og, count(j, 1, 2))
        dve.wait_ge(k.z_kept, count(j, 1, 1))
        tt(k.kbg[:, :, :], k.kbg[:, :, :], chunked(k.zk[:, :]), ALU.mult).then_inc(k.og, 1)

    def s5_states(j, q, part):
        c, s = [k.tcos0, k.tcos1][q % 2], [k.tsin0, k.tsin1][q % 2]
        gr, gi = [k.gr0, k.gr1][q % 2], [k.gi0, k.gi1][q % 2]
        n = count(j, 8 * q + 3 * part, 32)
        re, im = ps[3], ps[4]
        if part == 0:
            dve.wait_ge(k.tab, count(j, 3 * q + 3, 12))
            dve.wait_ge(k.bu, count(j, q + 1, 4))
            wait(dve, k.dem, count(j, 6 * (q - 1), 24))
            if q == 0:
                wait(dve, k.y_st, count(j, 0, 16))
        g, x1, x2, op = (gi, im, re, ALU.subtract) if part else (gr, re, im, ALU.add)
        tt(k.ma[:, :], x1[:, :], c[:, :], ALU.mult).then_inc(k.mod, 1)
        tt(k.mb[:, :], x2[:, :], s[:, :], ALU.mult).then_inc(k.mod, 1)
        dve.wait_ge(k.mod, n + 2)
        tt(g[:, :], k.ma[:, :], k.mb[:, :], op).then_inc(k.mod, 1)
        dve.wait_ge(k.mod, n + 3)
        if part:
            for g in (gr, gi):
                dve.tensor_tensor_scan(g[:, :], k.s5h[:, 0, q:q + 1].to_broadcast([P, S]), g[:, :], 0.0,
                                       ALU.mult, ALU.add).then_inc(k.mod, 1)

    def s5_sum(j):
        dve.wait_ge(k.yp, count(j, 4, 4))
        stt(k.ma[:, :], k.xb[:, :], k.dh[:, 0:1], ps[5][:, :], ALU.mult, ALU.add).then_inc(k.ysum, 1)

    def mixer(a, j, l):
        split = lambda b: split_lo(k, dve, B_MIX + b + 1, 6, a)
        if a: split(0)
        if l: state(l, 0)
        if j: head_parameters(j)
        if l: state(l, 1); s5_sum(l)
        if j: log_decays(j)
        if l: state(l, 2)
        if j: convolve(j, 0); s5_matrices(j); convolve(j, 1); convolve(j, 2)
        if a: split(1)
        if j: s5_states(j, 0, 0); s5_states(j, 0, 1)
        if l: gated(l)
        if j: differences(j); normed_keys(j)
        if a: split(2)
        if j: normed_queries(j); keys(j); system(j); values(j); s5_states(j, 1, 0); s5_states(j, 1, 1)
        if a: split(3)
        if j: first_level(j); queries(j); level_x(j, 1); s5_states(j, 2, 0); level_p(j, 1); s5_states(j, 2, 1); level_x(j, 2)
        if a: split(4)
        if j: level_p(j, 2); level_x(j, 3); level_p(j, 3); s5_states(j, 3, 0); level_x(j, 4); s5_states(j, 3, 1)
        if a: split(5)
        if j: level_p(j, 4); level_x(j, 5); level_p(j, 5); level_x(j, 6); level_p(j, 6)

    mixer((0, 0), None, None)
    dve.wait_ge(k.pad_zero, 4)
    mixer((1, 0), (0, 0), None)
    with dve.Fori(2, HEADS) as i:
        mixer((i, 0), (i, -1), (i, -2))
    mixer(None, (HEADS, -1), (HEADS, -2))
    mixer(None, None, (HEADS, -1))
    end_phase(k, dve, 3)

    for t in range(KW):
        dve.wait_ge(k.y_hi, t + 1)
        tt(k.gl[:, t, :], k.yst[:, t, :], k.gh[:, t, :].bitcast(F32), ALU.subtract).then_inc(k.y_lo, 1)
    def glu(j):
        for t in range(2):
            gg, zv, gv = [k.gg0, k.gg1][t], [k.zv0, k.zv1][t], [k.gv0, k.gv1][t]
            split_lo(k, dve, B_GLU + t + 1, 2, j)
            dve.wait_ge(k.sig, count(j, t + 1, 2))
            tt(gg[:, :], ps[t][:, :], gg[:, :], ALU.mult).then_inc(gv, 1)
            dve.wait_ge(gv, count(j, 1, 2))
            dve.wait_ge([k.zb_in0, k.zb_in1][t], count(j, 16, 16))
            tt(gg[:, :], gg[:, :], zv[:, :], ALU.mult).then_inc(gv, 1)

    glu((0, 0))
    with dve.Fori(1, KW // 2) as i:
        glu((i, 0))
    end_phase(k, dve, 4)

    for br in range(3):
        for t in range(KW):
            dve.wait_ge(k.g_hi, KW * br + t + 1)
            tt(k.gl[:, t, :], k.gst[:, t, :], k.gh[:, t, :].bitcast(F32), ALU.subtract).then_inc(k.g_lo, 1)
        def merge(j):
            for pair in range(2):
                b0 = B_BR + 24 * br + 3 * pair
                for n in range(3):
                    split_lo(k, dve, b0 + n + 1, 6, j)
                for n in range(2):
                    d = 2 * pair + n
                    t = 16 * br + d
                    sg = [k.sg0, k.sg1][n]
                    m = k.merged[:, bass.ds(count(j, d, 4), 1), :]
                    if n == 0:
                        dve.wait_ge(k.p_ps, count(j, 8 * br + pair + 1, 2))
                    else:
                        dve.wait_ge(k.w_used, count(j, b0 + 3, 6))
                    dve.wait_ge(k.gate_s, count(j, t + 1, 4))
                    o = m if br == 0 else sg[:, :].unsqueeze(1)
                    tt(o, ps[4 + d][:, :].unsqueeze(1), sg[:, :].unsqueeze(1), ALU.mult).then_inc(k.prod, 1)
                    if br:
                        dve.wait_ge(k.prod, count(j, t + 1, 4))
                        tt(m, m, sg[:, :].unsqueeze(1), ALU.add).then_inc(k.mrg, 1)

        merge((0, 0))
        with dve.Fori(1, KD // 4) as i:
            merge((i, 0))
    end_phase(k, dve, 5)

    for t in range(KD):
        dve.wait_ge(k.m_hi, t + 1)
        tt(k.ul[:, t, :], k.merged[:, t, :], k.uh[:, t, :].bitcast(F32), ALU.subtract).then_inc(k.m_lo, 1)
    for c in range(4):
        for kb in range(4):
            w = B_OUT + 4 * c + kb + 1
            if w < N_BLOCKS:
                split_lo(k, dve, w)
        dve.wait_ge(k.xr_in, 64 * (c + 1))
        for m in range(NT):
            if m < 3:
                dve.wait_ge(k.o_ps, 3 * c + m + 1)
            else:
                dve.wait_ge(k.w_used, B_OUT + 4 * c + 4)
            tt(k.hrow[:, m, c * S:(c + 1) * S], ps[4 * (c % 2) + m][:, :], k.xr[:, m, :],
               ALU.add).then_inc(k.h_s, 1)
    dve.wait_ge(k.h_sq, 16)
    dve.reduce_sum(stat[:, 0:4], k.ssq[:, :, :], AX_X).then_inc(k.p_dve, 2)
    dve.wait_ge(k.p_act, 8)
    step(dve.reciprocal(stat[:, 16:20], stat[:, 8:12]))
    dve.wait_ge(k.fg_in, 16)
    for m in range(NT):
        stt(k.hrow[:, m, :], k.hrow[:, m, :], stat[:, 16 + m:17 + m], k.fg[:, :], ALU.mult, ALU.mult).then_inc(k.fin, 1)


_INS = ["x", "mem", "norm_g", "w_in", "conv_w", "gdn_a_log", "gdn_dt_bias", "gdn_norm_g", "s5_lambda_re",
        "s5_lambda_im", "s5_log_dt", "s5_b_re", "s5_b_im", "s5_c_re", "s5_c_im", "s5_d", "s5_w_glu",
        "mem_norm_g", "w_kv_mem", "w_br_a", "w_br_b", "w_br_c", "w_out", "final_g"]


def kernel(**inputs):
    import concourse.bacc as _bacc
    from concourse.bass_utils import run_bass_kernel_spmd as _run

    nc = _bacc.Bacc("TRN2", target_bir_lowering=False, num_devices=1)
    arrays, args = {}, []
    for name in _INS + ["consts"]:
        a = constants() if name == "consts" else np.ascontiguousarray(inputs[name])
        arrays[f"in_{name}_dram"] = a
        args.append(nc.dram_tensor(f"in_{name}_dram", a.shape, mybir.dt.from_np(a.dtype), kind="ExternalInput").ap())
    args.append(nc.dram_tensor("out_0_dram", (1, S, D), F32, kind="ExternalOutput").ap())
    build(nc, *args)
    r = _run(nc, [arrays], core_ids=[0])
    return r.results[0]["out_0_dram"]
```

```python
from contextlib import ExitStack

import numpy as np
import concourse.bass as bass
from concourse import mybir

F32 = mybir.dt.float32
F32R = mybir.dt.float32r
ALU = mybir.AluOpType
ACT = mybir.ActivationFunctionType
AX_X = mybir.AxisListType.X

P = 128
S = 512
D = 2048
KD = D // P
NT = S // P
W = 1024
KW = W // P
MEM = 256
MT = MEM // P
HEADS = 8
XH = 4
GS = 16
NS = 64
PAIRS = 32
EPS = 1e-6
Q0, K0, V0, ZA0, BA0 = 0, W, 2 * W, 3 * W, 4 * W
XB0 = BA0 + 2 * HEADS
ZB0, QC0, ZC0 = XB0 + W, XB0 + 2 * W, XB0 + 3 * W
G0 = XB0 + 4 * W
CONV = 4
LEVELS = [2 ** n for n in range(7)]
MATS = ["ident", "upper", "strict", "ones"] + [f"low{s}" for s in LEVELS] + ["up1"]
C_T = len(MATS) * P
C_COL = C_T + S
COLS = ["eps", "eps128", "quarter", "even", "odd", "neven", "nodd"]
NCONST = C_COL + len(COLS)
TWO_PI = 2 * np.pi
PI_A = 6.28125
PI_B = float(np.float32(int((TWO_PI - PI_A) * 2 ** 20) / 2 ** 20))
PI_C = float(TWO_PI - PI_A - PI_B)
ROUND = 1.5 * 2 ** 23
ROUND14 = 1.5 * 2 ** 9


def constants():
    c = np.zeros((P, NCONST), np.float32)
    i, j = np.indices((P, P))
    m = {"ident": i == j, "upper": i <= j, "strict": i > j, "ones": i >= 0}
    for s in LEVELS:
        m[f"low{s}"] = (i // s % 2 == 1) & (j // s == i // s - 1)
    m["up1"] = m["low1"].T
    for n, name in enumerate(MATS):
        c[:, n * P:(n + 1) * P] = m[name]
    c[:, C_T:C_T + S] = np.arange(S)
    g2 = np.arange(P) // GS % 2
    for n, v in enumerate([EPS, P * EPS, np.pi / 2, g2 == 0, g2 == 1, -(g2 == 0).astype(float), -(g2 == 1).astype(float)]):
        c[:, C_COL + n] = v
    return c



def at(j):
    return j[0] + j[1]


def count(j, first, per):
    return j[0] * per + (first + per * j[1])


def wait(e, s, value):
    if isinstance(value, int) and value <= 0:
        return
    e.wait_ge(s, value)


def wait_apart(k, e, s, value):
    wait(e, s, value)
    if not isinstance(value, int):
        e.sem_inc(k.sp_waits if e is k.sp else k.pool_waits, 1)


class Handles:
    pass


def build(nc, x, mem, norm_g, w_in, conv_w, a_log, dt_bias, gdn_g, lam_re, lam_im, log_dt, b_re, b_im,
          c_re, c_im, s5_d, w_glu, mem_g, w_kv, w_a, w_b, w_c, w_out, final_g, consts, out):
    with ExitStack() as ctx:
        k = Handles()
        k.nc = nc
        k.x, k.mem, k.out = x[0], mem[0], out[0]
        k.norm_g, k.mem_g, k.gdn_g, k.s5_d, k.final_g = norm_g[0], mem_g[0], gdn_g[0], s5_d[0], final_g
        k.w_in, k.conv_w, k.w_glu, k.w_kv, k.w_out = w_in[0], conv_w[0], w_glu[0], w_kv[0], w_out[0]
        k.branch_w = [w_c[0], w_b[0], w_a[0]]
        k.a_log, k.dt_bias, k.consts = a_log[0], dt_bias[0], consts
        k.lam_re, k.lam_im, k.log_dt = lam_re[0], lam_im[0], log_dt[0]
        k.b_re, k.b_im, k.c_re, k.c_im = b_re[0], b_im[0], c_re[0], c_im[0]
        k.gated_d = [nc.dram_tensor(f"gated_{n}", [W, S], F32, kind="Internal").ap() for n in "cba"]
        k.gates_d = nc.dram_tensor("gates_c", [D, S], F32, kind="Internal").ap()
        k.y_d = nc.dram_tensor("s5_out", [W, S], F32, kind="Internal").ap()
        k.zb_d = nc.dram_tensor("z_b", [W, S], F32, kind="Internal").ap()

        def sb(where, name, shape, dt=F32):
            return where.enter_context(nc.sbuf_tensor(name, [P] + shape, dt))

        def sems(*names):
            return [ctx.enter_context(nc.semaphore(name)) for name in names]

        k.ps = [ctx.enter_context(nc.psum_tensor(f"bank{n}", [P, S], F32)) for n in range(8)]

        k.uh = sb(ctx, "uh", [KD, S], F32R)
        k.ul = sb(ctx, "ul", [KD, S], F32R)
        k.raw0 = sb(ctx, "raw0", [2048])
        k.raw1 = sb(ctx, "raw1", [2048])
        k.wh0 = sb(ctx, "wh0", [2048], F32R)
        k.wh1 = sb(ctx, "wh1", [2048], F32R)
        k.wl0 = sb(ctx, "wl0", [2048], F32R)
        k.wl1 = sb(ctx, "wl1", [2048], F32R)
        k.cst = sb(ctx, "cst", [NCONST])
        k.prm1 = sb(ctx, "prm1", [P])
        k.prm2 = sb(ctx, "prm2", [P])
        k.s5p = sb(ctx, "s5p", [5, PAIRS])
        k.hp = sb(ctx, "hp", [4, NT, HEADS])
        k.stat = sb(ctx, "stat", [40])
        k.raw, k.wh, k.wl = [k.raw0, k.raw1], [k.wh0, k.wh1], [k.wl0, k.wl1]
        k.mat = {name: k.cst[:, n * P:(n + 1) * P] for n, name in enumerate(MATS)}
        k.col = {name: k.cst[:, C_COL + n:C_COL + n + 1] for n, name in enumerate(COLS)}
        k.tvec = k.cst[:, C_T:C_T + S]

        k.junk = k.raw1
        k.wbah, k.wbal = k.wh1[:, 1024:1024 + KD * 16], k.wh1[:, 1536:1536 + KD * 16]

        k.ba_rows = k.raw1[0:16, 0:S]

        with ExitStack() as area:
            k.mh = sb(area, "mh", [KD, MEM], F32R)
            k.ml = sb(area, "ml", [KD, MEM], F32R)
            k.alog_b = sb(area, "alog_b", [HEADS])
            k.dtb_b = sb(area, "dtb_b", [HEADS])
            k.tp = sb(area, "tp", [16, PAIRS])
            with ExitStack() as a:
                k.xs = sb(a, "xs", [NT + MT, D])
                k.rows1 = sb(a, "rows1", [P])
                k.rows2 = sb(a, "rows2", [P])
                k.ldt2 = sb(a, "ldt2", [2])
                k.wba = sb(a, "wba", [KD * 16])
            with ExitStack() as a:
                k.kt = sb(a, "kt", [2, MEM])
                k.vt = sb(a, "vt", [2, MEM])
                k.vx = sb(a, "vx", [MT, 256])
                k.qx = sb(a, "qx", [2, S])
                k.zx = sb(a, "zx", [2, S])
                k.px = sb(a, "px", [NT, MEM])
                k.ptx = sb(a, "ptx", [MT, S])
                k.ox = sb(a, "ox", [2, S])
        with ExitStack() as area:
            k.qraw = sb(area, "qraw", [S + 3])
            k.kraw = sb(area, "kraw", [S + 3])
            k.vraw = sb(area, "vraw", [S + 3])
            k.qc = sb(area, "qc", [S])
            k.kc = sb(area, "kc", [S])
            k.vc = sb(area, "vc", [S])
            k.rq = sb(area, "rq", [S])
            k.rk = sb(area, "rk", [S])
            k.zs = sb(area, "zs", [S])
            k.zk = sb(area, "zk", [S])
            k.er = sb(area, "er", [NT, P])
            k.qd = sb(area, "qd", [NT, P])
            k.dl = sb(area, "dl", [NT, P])
            k.du = sb(area, "du", [NT, P])
            k.vb = sb(area, "vb", [NT, P])
            k.kbg = sb(area, "kbg", [NT, P])
            k.kd = sb(area, "kd", [NT, P])
            k.lt = sb(area, "lt", [NT, P])
            k.tl = sb(area, "tl", [NT, P])
            k.tu = sb(area, "tu", [NT, P])
            k.gx = sb(area, "gx", [NT, P])
            k.vn = sb(area, "vn", [NT, P])
            k.st = sb(area, "st", [P])
            k.cwh = sb(area, "cwh", [CONV, 3])
            k.hph = sb(area, "hph", [4, NT])
            k.s5h = sb(area, "s5h", [5, 4])
            k.dh = sb(area, "dh", [1])
            k.xb = sb(area, "xb", [S])
            k.braw = sb(area, "braw", [2, 4, GS])
            k.craw = sb(area, "craw", [2, NS])
            k.bt = sb(area, "bt", [6, 4, GS])
            k.bpad = sb(area, "bpad", [2, 4, 2, GS])
            k.cpad = sb(area, "cpad", [2, 2, NS])
            k.bc = sb(area, "bc", [4, P])
            k.tcos0 = sb(area, "tcos0", [S])
            k.tcos1 = sb(area, "tcos1", [S])
            k.tsin0 = sb(area, "tsin0", [S])
            k.tsin1 = sb(area, "tsin1", [S])
            k.karg = sb(area, "karg", [S])
            k.farg = sb(area, "farg", [S])
            k.ma = sb(area, "ma", [S])
            k.mb = sb(area, "mb", [S])
            k.gr0 = sb(area, "gr0", [S])
            k.gr1 = sb(area, "gr1", [S])
            k.gi0 = sb(area, "gi0", [S])
            k.gi1 = sb(area, "gi1", [S])
            k.hr = sb(area, "hr", [S])
            k.hi = sb(area, "hi", [S])
            k.pt = sb(area, "pt", [S])
            k.zbs = sb(area, "zbs", [S])
        with ExitStack() as area:
            k.zv0 = sb(area, "zv0", [S])
            k.zv1 = sb(area, "zv1", [S])
            k.gg0 = sb(area, "gg0", [S])
            k.gg1 = sb(area, "gg1", [S])
            k.gk0 = sb(area, "gk0", [S])
            k.gk1 = sb(area, "gk1", [S])
        with ExitStack() as area:
            k.merged = sb(area, "merged", [KD, S])
            with ExitStack() as b:
                k.gh = sb(b, "gh", [KW, S], F32R)
                k.gl = sb(b, "gl", [KW, S], F32R)
                with ExitStack() as a:
                    k.gst = sb(a, "gst", [KW, S])
                    k.gates0 = sb(a, "gates0", [2, S])
                    k.gates1 = k.cst[:, P:P + 2 * S].rearrange("p (t s) -> p t s", t=2)
                    k.sg0, k.sg1 = k.gates0[:, 0, :], k.gates0[:, 1, :]
                with ExitStack() as a:
                    k.yst = sb(a, "yst", [KW, S])
            with ExitStack() as b:
                k.hrow = sb(b, "hrow", [NT, D])
                k.xr = sb(b, "xr", [NT, S])
                k.fg = sb(b, "fg", [D])
                k.xsq = sb(b, "xsq", [S])
                k.ssq = sb(b, "ssq", [NT, 4])

        k.sp_waits, k.pool_waits, k.w_in0, k.w_in1, k.w_hi, k.w_lo = \
            sems("sp_waits", "pool_waits", "w_in0", "w_in1", "w_hi", "w_lo")
        k.w_used, k.phase_end = \
            sems("w_used", "phase_end")
        k.w_in_slot = [k.w_in0, k.w_in1]
        k.cst_in, k.rows_in, k.rows_zero, k.mem_in, k.wba_in = \
            sems("cst_in", "rows_in", "rows_zero", "mem_in", "wba_in")
        k.prm_ps, k.prm, k.ldt_rows, k.x_sq, k.x_root, k.x_scale = \
            sems("prm_ps", "prm", "ldt_rows", "x_sq", "x_root", "x_scale")
        k.x_tr, k.u_hi, k.u_lo, k.link, k.alink = \
            sems("x_tr", "u_hi", "u_lo", "link", "alink")
        k.wba_hi, k.wba_lo, k.ba_ps, k.ba_s, k.ba_tr, k.g_done, k.gsum_ps, k.p_act = \
            sems("wba_hi", "wba_lo", "ba_ps", "ba_s", "ba_tr", "g_done", "gsum_ps", "p_act")
        k.p_dve, = \
            sems("p_dve")
        k.x_in = sems("x_in0", "x_in1", "x_in2", "x_in3")
        k.xa_out, k.xa_vtr, k.xa_v, k.xa_sc, k.xa_max, k.xa_exp = \
            sems("xa_out", "xa_vtr", "xa_v", "xa_sc", "xa_max", "xa_exp")
        k.xa_sum, k.xa_p, k.xa_ptr, k.xa_pt, k.xa_o, k.xa_og = \
            sems("xa_sum", "xa_p", "xa_ptr", "xa_pt", "xa_o", "xa_og")
        k.xa_st0, k.xa_st1 = \
            sems("xa_st0", "xa_st1")
        k.mx_out, k.zb_st, k.pad_zero, k.z_kept = \
            sems("mx_out", "zb_st", "pad_zero", "z_kept")
        k.sliced, k.conv, k.gu, k.silu, k.sq, k.ss = \
            sems("sliced", "conv", "gu", "silu", "sq", "ss")
        k.rsum, k.root, k.er_s, k.dd, k.dec, k.rn = \
            sems("rsum", "root", "er_s", "dd", "dec", "rn")
        k.qk, k.vtr, k.vb_s, k.ktr, k.kb, k.kk = \
            sems("qk", "vtr", "vb_s", "ktr", "kb", "kk")
        k.kq, k.pm, k.lm, k.qkt, k.ltr, k.lt_s = \
            sems("kq", "pm", "lm", "qkt", "ltr", "lt_s")
        k.tu_s, k.lx, k.xm, k.lp, k.tus, k.wt = \
            sems("tu_s", "lx", "xm", "lp", "tus", "wt")
        k.wtn, k.vp, k.vn_s, k.op, k.sp_s, k.st_s = \
            sems("wtn", "vp", "vn_s", "op", "sp_s", "st_s")
        k.osq, k.sso, k.oroot, k.orn, k.og, k.g_st = \
            sems("osq", "sso", "oroot", "orn", "og", "g_st")
        k.s5_in, k.s5_w, k.s5_tr, k.bc_s, k.args, k.tab = \
            sems("s5_in", "s5_w", "s5_tr", "bc_s", "args", "tab")
        k.bu, k.mod, k.dem, k.yp, k.ysum, k.y_st = \
            sems("bu", "mod", "dem", "yp", "ysum", "y_st")
        k.gt_st = sems(*(f"gt_st{n}" for n in range(7)))
        k.gt_in = sems("gt_in0", "gt_in1")
        k.y_in, k.y_act, k.y_hi, k.y_lo, k.glu_ps, k.sig = \
            sems("y_in", "y_act", "y_hi", "y_lo", "glu_ps", "sig")
        k.zb_in0, k.zb_in1, k.gv0, k.gv1, k.gb_st0, k.gb_st1 = \
            sems("zb_in0", "zb_in1", "gv0", "gv1", "gb_st0", "gb_st1")
        k.ga_in, k.g_hi, k.g_lo, k.gate_ps, k.p_ps, k.gate_s = \
            sems("ga_in", "g_hi", "g_lo", "gate_ps", "p_ps", "gate_s")
        k.prod, k.mrg, k.m_hi, k.m_lo, k.o_ps, k.xr_in = \
            sems("prod", "mrg", "m_hi", "m_lo", "o_ps", "xr_in")
        k.fg_in, k.h_s, k.h_sq, k.fin, k.o_st = \
            sems("fg_in", "h_s", "h_sq", "fin", "o_st")

        block = ctx.enter_context(nc.Block())

        @block.sync
        def _(sp):
            k.sp = sp
            sync_program(k, sp)

        @block.gpsimd
        def _(pool):
            pool_program(k, pool)

        @block.scalar
        def _(act):
            scalar_program(k, act)

        @block.vector
        def _(dve):
            vector_program(k, dve)

        @block.tensor
        def _(pe):
            tensor_program(k, pe)


B_XA = 0
B_MIX = B_XA + 8 * XH
B_GT = B_MIX + 6 * HEADS
B_GLU = B_GT + KD
B_C = B_GLU + KW
B_BR = B_C + KW
B_OUT = B_BR + 2 * 24
N_BLOCKS = B_OUT + 16


def end_phase(k, e, n):
    e.drain().then_inc(k.phase_end, 1)
    e.wait_ge(k.phase_end, 4 * n)



def load_halves(k, sp, w0, per, j, sources):
    slot = w0 % 2
    wait_apart(k, sp, k.w_lo, count(j, w0 - 1, per))
    for half, src in enumerate(sources):
        n = src.shape[1]
        dst = k.raw[slot][:, half * 1024:(half + 1) * 1024].rearrange("p (k c) -> p k c", k=n)
        sp.dma_start(dst, src).then_inc(k.w_in_slot[slot], 16)


def columns(w, c, n=P):
    return w[:, bass.ds(c, n)].rearrange("(k p) c -> p k c", p=P)


def load_fm(k, sp, w0, per, j, w, c):
    v = columns(w, c)
    load_halves(k, sp, w0, per, j, [v[:, 0:8, :], v[:, 8:16, :]])


def load_fm8(k, sp, w0, per, j, w, c, c2):
    load_halves(k, sp, w0, per, j, [columns(w, c), columns(w, c2)])


def load_tm(k, sp, w0, per, j, w, rows, c):
    v = columns(w, c, S)
    load_halves(k, sp, w0, per, j, [v[:, rows:rows + 2, :], v[:, rows + 2:rows + 4, :]])


def split_hi(k, act, w0, per=0, j=(0, 0)):
    slot = w0 % 2
    wait(act, k.w_in_slot[slot], count(j, 32 * (w0 // 2 + 1), 16 * per))
    wait(act, k.w_used, count(j, w0 - 1, per))
    act.activation(k.wh[slot][:, :], k.raw[slot][:, :], ACT.Copy).then_inc(k.w_hi, 1)


def split_lo(k, dve, w0, per=0, j=(0, 0)):
    slot = w0 % 2
    wait(dve, k.w_hi, count(j, w0 + 1, per))
    wait(dve, k.w_used, count(j, w0 - 1, per))
    dve.tensor_tensor(k.wl[slot][:, :], k.raw[slot][:, :], k.wh[slot][:, :].bitcast(F32),
                      ALU.subtract).then_inc(k.w_lo, 1)


def mm3(pe, o, ah, al, bh, bl, start, stop):
    pe.matmul(o, ah, bh, start=start, stop=False)
    pe.matmul(o, ah, bl, start=False, stop=False)
    return pe.matmul(o, al, bh, start=False, stop=stop)


def row_tiles(k, pe, slot, o, tiles, at_tile, acth, actl, n_tiles):
    for n, t in enumerate(tiles):
        a = bass.ts(at_tile + n, P)
        mm = mm3(pe, o, k.wh[slot][:, a], k.wl[slot][:, a], acth[:, t, :], actl[:, t, :],
                 t == 0, t == n_tiles - 1)
    return mm


def eighth(k, pe, w0, per, j, q, acth, actl, n, outs, before):
    slot = w0 % 2
    if q == 0:
        wait(pe, k.w_lo, count(j, w0 + 1, per))
        wait(pe, outs, count(j, w0 - before - 1, per))
    mm = row_tiles(k, pe, slot, k.ps[slot][:, 0:n], range(2 * q, 2 * q + 2), 2 * q, acth, actl, KD)
    if q == 7:
        mm.then_inc(k.w_used, 1)


def sync_program(k, sp):
    sp.dma_start(k.cst[:, :], k.consts).then_inc(k.cst_in, 16)
    sp.wait_ge(k.rows_zero, 1)
    sp.dma_start(k.rows1[0:96, :], k.conv_w.rearrange("j (t c) -> (j t) c", c=P)).then_inc(k.rows_in, 16)
    sp.dma_start(k.rows1[96:112, :], k.norm_g.rearrange("(t c) -> t c", c=P)).then_inc(k.rows_in, 16)
    sp.dma_start(k.rows1[112:128, :], k.mem_g.rearrange("(t c) -> t c", c=P)).then_inc(k.rows_in, 16)
    sp.dma_start(k.rows2[0:32, :], k.lam_re.rearrange("(q g) s -> q (g s)", g=2)).then_inc(k.rows_in, 16)
    sp.dma_start(k.rows2[32:64, :], k.lam_im.rearrange("(q g) s -> q (g s)", g=2)).then_inc(k.rows_in, 16)
    sp.dma_start(k.rows2[96:104, :], k.s5_d.rearrange("(t c) -> t c", c=P)).then_inc(k.rows_in, 16)
    sp.dma_start(k.rows2[104:105, :], k.gdn_g.rearrange("(t c) -> t c", c=P)).then_inc(k.rows_in, 16)
    sp.dma_start(k.ldt2[64:96, :], k.log_dt.rearrange("(q g) -> q g", g=2)).then_inc(k.rows_in, 16)
    sp.dma_start(k.alog_b[:, :], k.a_log.partition_broadcast(P)).then_inc(k.rows_in, 16)
    sp.dma_start(k.dtb_b[:, :], k.dt_bias.partition_broadcast(P)).then_inc(k.rows_in, 16)
    for m in range(NT):
        sp.dma_start(k.xs[:, m, :], k.x[m * P:(m + 1) * P, :]).then_inc(k.x_in[m], 16)
    for m in range(MT):
        sp.dma_start(k.xs[:, NT + m, :], k.mem[m * P:(m + 1) * P, :]).then_inc(k.mem_in, 16)
    sp.dma_start(k.wba[:, :].rearrange("p (k c) -> p k c", c=16), columns(k.w_in, BA0, 16)).then_inc(k.wba_in, 16)
    def attention_loads(j):
        for b, (w, c0) in enumerate(((k.w_kv, 0), (k.w_kv, W), (k.w_in, QC0), (k.w_in, ZC0))):
            for t in range(2):
                if isinstance(j[0], int) and b == 0 and t == 1:
                    sp.wait_ge(k.ba_tr, 1)
                load_fm(k, sp, B_XA + 2 * b + t, 8, j, w, count(j, c0 + t * P, 2 * P))
    attention_loads((0, 0))
    with sp.Fori(1, XH) as i:
        attention_loads((i, 0))

    def mixer_loads(j):
        for b, c0 in enumerate(MIX_COLS):
            load_fm(k, sp, B_MIX + b, 6, j, k.w_in, count(j, c0, P))

    def s5_loads(j):
        wait_apart(k, sp, k.s5_w, count(j, 0, 13))
        for n, b in enumerate((k.b_re, k.b_im)):
            sp.dma_start(k.braw[:, n, :, :], b[bass.ds(count(j, 0, 8), 8)].rearrange("(q g) s i -> (g s) q i", g=2)).then_inc(k.s5_in, 16)
        for n, c in enumerate((k.c_re, k.c_im)):
            sp.dma_start(k.craw[:, n, :], c[bass.ds(count(j, 0, 8), 8)].rearrange("g i s -> (g i) s")).then_inc(k.s5_in, 16)

    mixer_loads((0, 0))
    sp.wait_ge(k.phase_end, 8)
    s5_loads((0, 0))
    with sp.Fori(1, HEADS) as i:
        mixer_loads((i, 0))
        s5_loads((i, 0))

    with sp.Fori(0, KD // 2) as i:
        for t in range(2):
            load_fm(k, sp, B_GT + t, 2, (i, 0), k.w_in, count((i, 0), G0 + 2 * D + t * P, 2 * P))

    with sp.Fori(0, KW // 2) as i:
        for t in range(2):
            c = count((i, 0), t * P, 2 * P)
            load_fm8(k, sp, B_GLU + t, 2, (i, 0), k.w_glu, c, c + W)

    with sp.Fori(0, KD // 4) as i:
        for pair in range(2):
            c = count((i, 0), 2 * pair * P, 4 * P)
            load_fm8(k, sp, B_C + pair, 2, (i, 0), k.branch_w[0], c, c + P)
    for br in (1, 2):
        gate0 = G0 + (2 - br) * D
        with sp.Fori(0, KD // 4) as i:
            j = (i, 0)
            for pair in range(2):
                b = B_BR + 24 * (br - 1) + 3 * pair
                c = count(j, 2 * pair * P, 4 * P)
                load_fm(k, sp, b, 6, j, k.w_in, c + gate0)
                load_fm(k, sp, b + 1, 6, j, k.w_in, c + (gate0 + P))
                load_fm8(k, sp, b + 2, 6, j, k.branch_w[br], c, c + P)

    with sp.Fori(0, 4) as i:
        for kb in range(4):
            load_tm(k, sp, B_OUT + kb, 4, (i, 0), k.w_out, 4 * kb, i * S)


MIX_COLS = (Q0, K0, V0, ZB0, ZA0, XB0)


def pool_program(k, pool):
    pool.memset(k.rows2[:, :], 0.0).then_inc(k.rows_zero, 1)
    end_phase(k, pool, 1)

    def attention_store(j):
        for t in range(2):
            wait_apart(k, pool, k.xa_og, count(j, t + 1, 2))
            pool.dma_start(k.gated_d[0][bass.ds(count(j, t * P, 2 * P), P), :], k.ox[:, t, :]).then_inc([k.xa_st0, k.xa_st1][t], 16)
    with pool.Fori(0, XH) as i:
        attention_store((i, 0))
    pool.wait_ge(k.xa_st0, 16 * XH)
    pool.wait_ge(k.xa_st1, 16 * XH)
    end_phase(k, pool, 2)

    for t in (k.qraw, k.kraw, k.vraw):
        pool.memset(t[:, 0:3], 0.0).then_inc(k.pad_zero, 1)
    pool.memset(k.bpad[:, :, :, :, :], 0.0).then_inc(k.pad_zero, 1)

    def mixer(j, l):
        tcos, tsin, gr, gi = [k.tcos0, k.tcos1], [k.tsin0, k.tsin1], [k.gr0, k.gr1], [k.gi0, k.gi1]

        def arguments(q):
            hi_, lo_ = k.s5h[:, 1, q:q + 1], k.s5h[:, 2, q:q + 1]
            n = count(j, 7 * q, 28)
            if q == 0:
                wait_apart(k, pool, k.sliced, count(j, 3, 3))
            wait_apart(k, pool, k.tab, count(j, 3 * q, 12))
            ts, tt = pool.tensor_scalar, pool.tensor_tensor
            ts(k.karg[:, :], k.tvec, hi_, ROUND, ALU.mult, ALU.add).then_inc(k.args, 1)
            ts(k.farg[:, :], k.tvec, hi_, None, ALU.mult).then_inc(k.args, 1)
            wait_apart(k, pool, k.args, n + 1)
            ts(k.karg[:, :], k.karg[:, :], -ROUND, None, ALU.add).then_inc(k.args, 1)
            wait_apart(k, pool, k.args, n + 3)
            tt(k.farg[:, :], k.farg[:, :], k.karg[:, :], ALU.subtract).then_inc(k.args, 1)
            wait_apart(k, pool, k.args, n + 4)
            ts(k.karg[:, :], k.tvec, lo_, None, ALU.mult).then_inc(k.args, 1)
            wait_apart(k, pool, k.args, n + 5)
            tt(k.farg[:, :], k.farg[:, :], k.karg[:, :], ALU.add).then_inc(k.args, 1)
            wait_apart(k, pool, k.args, n + 6)
            ts(k.farg[:, :], k.farg[:, :], 0.4999999, -0.4999999, ALU.min, ALU.max).then_inc(k.args, 1)

        def turn_back(q):
            c, s, a, b = tcos[q % 2], tsin[q % 2], gr[q % 2], gi[q % 2]
            n = count(j, 6 * q, 24)
            wait_apart(k, pool, k.mod, count(j, 8 * q + 8, 32))
            wait_apart(k, pool, k.yp, count(j, q, 4))
            for o, (c1, c2, op) in ((k.hr, (c, s, ALU.subtract)), (k.hi, (s, c, ALU.add))):
                pool.tensor_tensor(o[:, :], c1[:, :], a[:, :], ALU.mult).then_inc(k.dem, 1)
                pool.tensor_tensor(k.pt[:, :], c2[:, :], b[:, :], ALU.mult).then_inc(k.dem, 1)
                wait_apart(k, pool, k.dem, n + 2)
                pool.tensor_tensor(o[:, :], o[:, :], k.pt[:, :], op).then_inc(k.dem, 1)
                wait_apart(k, pool, k.dem, n + 3)
                n = n + 3

        def masks():
            wait_apart(k, pool, k.dec, count(j, 2, 2))
            pool.tensor_tensor(k.dl[:, :, :], k.dl[:, :, :],
                               k.mat["strict"].unsqueeze(1).to_broadcast([P, NT, P]), ALU.mult).then_inc(k.pm, 1)
            wait_apart(k, pool, k.pm, count(j, 1, 4))
            pool.tensor_tensor(k.dl[:, :, :], k.dl[:, :, :],
                               k.hph[:, 0, :].unsqueeze(2).to_broadcast([P, NT, P]), ALU.mult).then_inc(k.pm, 1)
            pool.tensor_tensor(k.du[:, :, :], k.du[:, :, :],
                               k.mat["upper"].unsqueeze(1).to_broadcast([P, NT, P]), ALU.mult).then_inc(k.pm, 1)

        def decayed_queries():
            wait_apart(k, pool, k.qk, count(j, 2, 2))
            pool.tensor_tensor(k.qd[:, :, :], k.qc[:, :].rearrange("p (n c) -> p n c", n=NT), k.er[:, :, :],
                               ALU.mult).then_inc(k.pm, 1)

        def store_s5():
            wait_apart(k, pool, k.ysum, count(l, 1, 1))
            pool.dma_start(k.y_d[bass.ds(at(l) * P, P), :], k.ma[:, :]).then_inc(k.y_st, 16)

        def store_head():
            wait_apart(k, pool, k.og, count(l, 2, 2))
            pool.dma_start(k.gated_d[2][bass.ds(at(l) * P, P), :],
                           k.kbg[:, :, :].rearrange("p n c -> p (n c)")).then_inc(k.g_st, 16)

        if j: arguments(0)
        if l: store_s5()
        if j: arguments(1); turn_back(0)
        if l: store_head()
        if j: masks(); arguments(2); decayed_queries(); turn_back(1); arguments(3); turn_back(2); turn_back(3)

    def gate_store(j):
        wait_apart(k, pool, k.mx_out, count(j, 4, 6))
        pool.dma_start(k.zb_d[bass.ds(at(j) * P, P), :], k.zbs[:, :]).then_inc(k.zb_st, 16)

    gate_store((0, 0))
    mixer((0, 0), None)
    gate_store((1, 0))
    with pool.Fori(2, HEADS) as i:
        mixer((i, -1), (i, -2))
        gate_store((i, 0))
    mixer((HEADS, -1), (HEADS, -2))
    mixer(None, (HEADS, -1))
    pool.wait_ge(k.zb_st, 16 * HEADS)
    pool.wait_ge(k.y_st, 16 * HEADS)
    pool.wait_ge(k.g_st, 16 * HEADS)
    end_phase(k, pool, 3)

    pool.dma_start(k.yst[:, :, :], k.y_d.rearrange("(t p) s -> p t s", p=P)).then_inc(k.y_in, 16)

    def glu(j):
        for t in range(2):
            zv, gg = [k.zv0, k.zv1][t], [k.gg0, k.gg1][t]
            row = count(j, t * P, 2 * P)
            wait_apart(k, pool, [k.gv0, k.gv1][t], count(j, 0, 2))
            pool.dma_start(zv[:, :], k.zb_d[bass.ds(row, P), :]).then_inc([k.zb_in0, k.zb_in1][t], 16)
            wait_apart(k, pool, [k.gv0, k.gv1][t], count(j, 2, 2))
            pool.dma_start(k.gated_d[1][bass.ds(row, P), :], gg[:, :]).then_inc([k.gb_st0, k.gb_st1][t], 16)
    glu((0, 0))
    pool.wait_ge(k.y_lo, KW)
    pool.dma_start(k.gst[:, :, :], k.gated_d[0].rearrange("(t p) s -> p t s", p=P)).then_inc(k.ga_in, 16)
    with pool.Fori(1, KW // 2) as i:
        glu((i, 0))
    pool.wait_ge(k.gb_st0, 8 * KW)
    pool.wait_ge(k.gb_st1, 8 * KW)
    end_phase(k, pool, 4)

    for br in range(3):
        if br:
            pool.wait_ge(k.g_lo, KW * br)
            pool.dma_start(k.gst[:, :, :], k.gated_d[br].rearrange("(t p) s -> p t s", p=P)).then_inc(k.ga_in, 16)
        if br == 0:
            for n in range(KW):
                wait(pool, k.prod, 2 * (n - 1))
                pool.dma_start([k.gates0, k.gates1][n % 2][:, :, :], k.gates_d[2 * n * P:(2 * n + 2) * P, :]
                               .rearrange("(t p) s -> p t s", p=P)).then_inc(k.gt_in[n % 2], 16)
    end_phase(k, pool, 5)

    pool.dma_start(k.fg[:, :], k.final_g.partition_broadcast(P)).then_inc(k.fg_in, 16)
    x_v = k.x.rearrange("(m p) c -> p m c", p=P)
    for c in range(4):
        for m in range(NT):
            wait(pool, k.h_s, 4 * (c - 1) + m + 1)
            pool.dma_start(k.xr[:, m, :], x_v[:, m, c * S:(c + 1) * S]).then_inc(k.xr_in, 16)
    for m in range(NT):
        pool.wait_ge(k.fin, m + 1)
        pool.dma_start(k.out[m * P:(m + 1) * P, :], k.hrow[:, m, :]).then_inc(k.o_st, 16)
    pool.wait_ge(k.o_st, 16 * NT)


def tensor_program(k, pe):
    ps, mat = k.ps, k.mat
    ident, ones = mat["ident"], mat["ones"]

    pe.wait_ge(k.cst_in, 16)
    pe.wait_ge(k.rows_in, 160)
    pe.wait_ge(k.ldt_rows, 1)
    pe.transpose(ps[4][:, 0:P], k.rows1[:, :], ident).then_inc(k.prm_ps, 1)
    pe.transpose(ps[5][:, 0:P], k.rows2[:, :], ident).then_inc(k.prm_ps, 1)
    for t in range(KD):
        pe.wait_ge(k.x_scale, NT)
        wait(pe, k.u_lo, t - 3)
        for m in range(NT):
            mm = pe.transpose(ps[t % 4][:, m * P:(m + 1) * P], k.xs[:, m, t * P:(t + 1) * P], ident)
        mm.then_inc(k.x_tr, 1)
    pe.wait_ge(k.wba_lo, 1)
    for t in range(KD):
        pe.wait_ge(k.x_scale, NT + MT)
        pe.wait_ge(k.u_lo, KD + t - 3)
        for m in range(MT):
            mm = pe.transpose(ps[t % 4][:, m * P:(m + 1) * P], k.xs[:, NT + m, t * P:(t + 1) * P], ident)
        mm.then_inc(k.x_tr, 1)
        pe.wait_ge(k.u_lo, t + 1)
        mm = mm3(pe, ps[6][0:16, :], k.wbah[:, t * 16:(t + 1) * 16], k.wbal[:, t * 16:(t + 1) * 16],
                 k.uh[:, t, :], k.ul[:, t, :], t == 0, t == KD - 1)
    mm.then_inc(k.ba_ps, 1)
    pe.wait_ge(k.ba_s, 1)
    for m in range(NT):
        mm = pe.transpose(ps[5][:, m * 16:(m + 1) * 16], k.ba_rows[:, m * P:(m + 1) * P], ident[0:16, 0:16])
    mm.then_inc(k.ba_tr, 1)
    end_phase(k, pe, 1)

    def at_big(j, b):
        hl, n = ((k.uh, k.ul), S) if b >= 4 else ((k.mh, k.ml), MEM)
        for q in range(8):
            eighth(k, pe, B_XA + b, 8, j, q, *hl, n, k.xa_out, 0)

    def at_values(j):
        pe.wait_ge(k.xa_out, count(j, 8, 8))
        wait(pe, k.xa_og, count(j, 0, 2))
        for m in range(MT):
            for t in range(2):
                mm = pe.transpose(ps[2][:, (2 * m + t) * P:(2 * m + t + 1) * P], k.vt[:, t, m * P:(m + 1) * P], ident)
        mm.then_inc(k.xa_vtr, 1)

    def at_scores(j, m):
        wait(pe, k.xa_exp, count(j, m - 1, 4))
        for t in range(2):
            mm = pe.matmul(ps[4 + m % 2][:, 0:MEM], k.qx[:, t, m * P:(m + 1) * P], k.kt[:, t, :], start=t == 0, stop=t == 1)
        mm.then_inc(k.xa_sc, 1)

    def at_turn(j, n):
        pe.wait_ge(k.xa_p, count(j, 4, 4))
        wait(pe, k.xa_pt, count(j, n, 2))
        for m in range(NT):
            mm = pe.transpose(ps[6 + n][:, m * P:(m + 1) * P], k.px[:, m, n * P:(n + 1) * P], ident)
        mm.then_inc(k.xa_ptr, 1)

    def at_output(j, t):
        pe.wait_ge(k.xa_v, count(j, 1, 1))
        pe.wait_ge(k.xa_pt, count(j, 2, 2))
        wait(pe, k.xa_og, count(j, 0, 2))
        for m in range(MT):
            mm = pe.matmul(ps[2 + t][:, :], k.vx[:, m, t * P:(t + 1) * P], k.ptx[:, m, :], start=m == 0, stop=m == MT - 1)
        mm.then_inc(k.xa_o, 1)

    def at_small(j, n):
        if n == 0:
            at_values(j)
            at_scores(j, 0)
            at_scores(j, 1)
        if n == 1:
            at_scores(j, 2)
            at_scores(j, 3)
        if n in (3, 4):
            at_turn(j, n - 3)
        if n == 5:
            at_output(j, 0)
            at_output(j, 1)

    for b in range(8):
        at_big((0, 0), b)
        if b == 6:
            pe.wait_ge(k.g_done, 1)
            pe.matmul(ps[7][:, 0:NT * HEADS], mat["upper"], k.hp[:, 3, :, :], start=True, stop=True).then_inc(k.gsum_ps, 1)
    for b in range(8):
        at_small((0, 0), b)
        at_big((1, 0), b)
    with pe.Fori(2, XH) as i:
        for b in range(8):
            at_small((i, -1), b)
            at_big((i, 0), b)
    for n in range(6):
        at_small((XH, -1), n)
    end_phase(k, pe, 2)

    def big(j, b, *eighths):
        for q in eighths:
            eighth(k, pe, B_MIX + b, 6, j, q, k.uh, k.ul, S, k.mx_out, B_MIX)

    def norm_keys(j):
        pe.wait_ge(k.sq, count(j, 2, 2))
        wait(pe, k.oroot, count(j, 0, 1))
        pe.matmul(ps[6][:, :], ones, k.rk[:, :], start=True, stop=True).then_inc(k.ss, 1)
        pe.wait_ge(k.gu, count(j, 1, 1))
        wait(pe, k.st_s, count(j, 0, 3))
        pe.matmul(ps[7][:, :], ones, k.gx[:, :, :], start=True, stop=True).then_inc(k.rsum, 1)

    def norm_queries(j):
        wait(pe, k.og, count(j, 0, 2))
        pe.matmul(ps[2][:, :], ones, k.rq[:, :], start=True, stop=True).then_inc(k.ss, 1)

    def values(j):
        pe.wait_ge(k.silu, count(j, 3, 3))
        pe.wait_ge(k.root, count(j, 2, 2))
        for n in range(NT):
            mm = pe.transpose(ps[2][:, n * P:(n + 1) * P], k.vc[:, n * P:(n + 1) * P], ident)
        mm.then_inc(k.vtr, 1)

    def keys(j):
        pe.wait_ge(k.qk, count(j, 1, 2))
        for n in range(NT):
            mm = pe.transpose(ps[6][:, n * P:(n + 1) * P], k.kc[:, n * P:(n + 1) * P], ident)
        mm.then_inc(k.ktr, 1)

    def keys_keys(j):
        pe.wait_ge(k.er_s, count(j, 1, 1))
        pe.wait_ge(k.dd, count(j, 1, 3))
        for n in range(NT):
            c = bass.ts(n, P)
            mm = pe.matmul(ps[7][:, c], k.kc[:, c], k.kc[:, c], start=True, stop=True)
        mm.then_inc(k.kk, 1)

    def keys_queries(j):
        pe.wait_ge(k.qk, count(j, 2, 2))
        pe.wait_ge(k.vb_s, count(j, 1, 1))
        for n in range(NT):
            c = bass.ts(n, P)
            mm = pe.matmul(ps[2][:, c], k.kc[:, c], k.qc[:, c], start=True, stop=True)
        mm.then_inc(k.kq, 1)

    def turn_lower(j):
        pe.wait_ge(k.lm, count(j, 1, 1))
        pe.wait_ge(k.kb, count(j, 2, 2))
        for n in range(NT):
            mm = pe.transpose(ps[6][:, n * P:(n + 1) * P], k.dl[:, n, :], ident)
        mm.then_inc(k.ltr, 1)

    def level_x(j, l):
        pe.wait_ge(k.lt_s, count(j, 1, 1))
        if l == 1:
            pe.wait_ge(k.tu_s, count(j, 4, 4))
            pe.wait_ge(k.qkt, count(j, 1, 1))
        else:
            pe.wait_ge(k.tus, count(j, 2 * (l - 1), 11))
        for n in range(NT):
            mm = pe.matmul(ps[2][:, n * P:(n + 1) * P], k.lt[:, n, :], k.tl[:, n, :], start=True, stop=True)
        mm.then_inc(k.lx, 1)

    def level_p(j, l):
        pe.wait_ge(k.xm, count(j, l, 6))
        for n in range(NT):
            c = bass.ts(n, P)
            if l < 6:
                pe.matmul(ps[6][:, c], k.tu[:, n, :], k.gx[:, n, :], start=True, stop=True)
            mm = pe.matmul(ps[7][:, c], k.gx[:, n, :], k.tu[:, n, :], start=True, stop=True)
        mm.then_inc(k.lp, 1)

    def weights(j):
        pe.wait_ge(k.tus, count(j, 11, 11))
        for n in range(NT):
            mm = pe.matmul(ps[2][:, n * P:(n + 1) * P], k.kbg[:, n, :], k.tu[:, n, :], start=True, stop=True)
        mm.then_inc(k.wt, 1)

    def new_values(j, n):
        if n == 0:
            pe.wait_ge(k.wtn, count(j, 1, 1))
        else:
            pe.wait_ge(k.st_s, count(j, n, 3))
            pe.wait_ge(k.vn_s, count(j, n, 4))
        c = bass.ts(n, P)
        mm = pe.matmul(ps[6][:, c], k.tu[:, n, :], k.vb[:, n, :], start=True, stop=n == 0)
        if n:
            mm = pe.matmul(ps[6][:, c], k.dl[:, n, :], k.st[:, :], start=False, stop=True)
        mm.then_inc(k.vp, 1)

    def chunk_output(j, n):
        pe.wait_ge(k.vn_s, count(j, n + 1, 4))
        c = bass.ts(n, P)
        if n < NT - 1:
            pe.matmul(ps[7][:, 0:P], k.kd[:, n, :], k.vn[:, n, :], start=True, stop=True).then_inc(k.sp_s, 1)
        if n == 0:
            pe.wait_ge(k.pm, count(j, 4, 4))
            pe.wait_ge(k.qkt, count(j, 1, 1))
        mm = pe.matmul(ps[2][:, c], k.vn[:, n, :], k.du[:, n, :], start=True, stop=n == 0)
        if n:
            mm = pe.matmul(ps[2][:, c], k.st[:, :], k.qd[:, n, :], start=False, stop=True)
        mm.then_inc(k.op, 1)

    def output_norm(j):
        pe.wait_ge(k.osq, count(j, 1, 1))
        pe.matmul(ps[6][:, :], ones, k.lt[:, :, :], start=True, stop=True).then_inc(k.sso, 1)

    def s5_matrices(j):
        pe.wait_ge(k.s5_w, count(j, 13, 13))
        wait(pe, k.ysum, count(j, 0, 1))
        for n, t in enumerate((k.bpad[:, 0], k.bpad[:, 1])):
            pe.transpose(ps[5][:, n * P:(n + 1) * P], t.rearrange("p q g i -> p (q g i)"), ident)
        for n in range(2):
            mm = pe.transpose(ps[5][:, (2 + n) * P:(3 + n) * P], k.cpad[:, n].rearrange("p g s -> p (g s)"), ident)
        mm.then_inc(k.s5_tr, 1)

    def s5_inputs(j, q):
        pe.wait_ge(k.bc_s, count(j, 1, 1))
        pe.wait_ge(k.mx_out, count(j, 6, 6))
        wait(pe, k.mod, count(j, 8 * q - 2, 32))
        r = slice(32 * q, 32 * q + 32)
        pe.matmul(ps[3][:, :], k.bc[r, 0, :], k.xb[r, :], start=True, stop=True)
        pe.matmul(ps[4][:, :], k.bc[r, 1, :], k.xb[r, :], start=True, stop=True).then_inc(k.bu, 1)

    def s5_outputs(j, q):
        pe.wait_ge(k.dem, count(j, 6 * q + 6, 24))
        r = slice(32 * q, 32 * q + 32)
        pe.matmul(ps[5][r, :], k.bc[:, 2, r], k.hr[:, :], start=True, stop=False)
        pe.matmul(ps[5][r, :], k.bc[:, 3, r], k.hi[:, :], start=False, stop=True).then_inc(k.yp, 1)

    def mixer(a, j, l):
        if a: big(a, 0, 0)
        if l: weights(l)
        if a: big(a, 0, 1)
        if l: new_values(l, 0)
        if a: big(a, 0, 2)
        if l: chunk_output(l, 0)
        if a: big(a, 0, 3)
        if l: new_values(l, 1)
        if a: big(a, 0, 4)
        if l: chunk_output(l, 1); s5_outputs(l, 3)
        if a: big(a, 0, 5)
        if l: new_values(l, 2)
        if a: big(a, 0, 6)
        if l: chunk_output(l, 2)
        if a: big(a, 0, 7)
        if l: new_values(l, 3)
        if a: big(a, 1, 0)
        if l: chunk_output(l, 3)
        if a: big(a, 1, 1)
        if j: s5_matrices(j)
        if a: big(a, 1, 2)
        if l: output_norm(l)
        if a: big(a, 1, 3)
        if j: s5_inputs(j, 0)
        if a: big(a, 1, 4, 5)
        if j: norm_keys(j)
        if a: big(a, 1, 6, 7); big(a, 2, 0, 1)
        if j: norm_queries(j)
        if a: big(a, 2, 2, 3)
        if j: keys(j); keys_keys(j); s5_inputs(j, 1)
        if a: big(a, 2, 4)
        if j: values(j); s5_outputs(j, 0)
        if a: big(a, 2, 5, 6)
        if j: turn_lower(j)
        if a: big(a, 2, 7); big(a, 3, 0)
        if j: keys_queries(j)
        if a: big(a, 3, 1, 2)
        if j: level_x(j, 1); s5_inputs(j, 2)
        if a: big(a, 3, 3, 4)
        if j: level_p(j, 1)
        if a: big(a, 3, 5, 6)
        if j: level_x(j, 2)
        if a: big(a, 3, 7)
        if j: s5_outputs(j, 1)
        if a: big(a, 4, 0)
        if j: level_p(j, 2)
        if a: big(a, 4, 1, 2)
        if j: level_x(j, 3)
        if a: big(a, 4, 3, 4)
        if j: level_p(j, 3); s5_inputs(j, 3)
        if a: big(a, 4, 5, 6)
        if j: level_x(j, 4)
        if a: big(a, 4, 7); big(a, 5, 0)
        if j: level_p(j, 4)
        if a: big(a, 5, 1)
        if j: s5_outputs(j, 2)
        if a: big(a, 5, 2)
        if j: level_x(j, 5)
        if a: big(a, 5, 3)
        if j: level_p(j, 5)
        if a: big(a, 5, 4, 5)
        if j: level_x(j, 6)
        if a: big(a, 5, 6)
        if j: level_p(j, 6)
        if a: big(a, 5, 7)

    mixer((0, 0), None, None)
    mixer((1, 0), (0, 0), None)
    with pe.Fori(2, HEADS) as i:
        mixer((i, 0), (i, -1), (i, -2))
    mixer((HEADS, 0), (HEADS, -1), (HEADS, -2))
    mixer((HEADS + 1, 0), None, (HEADS, -1))
    pe.drain().then_inc(k.phase_end, 1)
    for b in range(4):
        big((HEADS + 2, 0), b, *range(8))
    pe.wait_ge(k.phase_end, 12)

    def glu(j):
        for t in range(2):
            wait(pe, k.w_lo, count(j, B_GLU + t + 1, 2))
            if isinstance(j[0], int):
                pe.wait_ge(k.mx_out, 6 * HEADS + KD - 1 + t)
            wait(pe, [k.gv0, k.gv1][t], count(j, 0, 2))
            if t == 0:
                pe.wait_ge(k.y_lo, KW)
            row_tiles(k, pe, t, ps[t][:, :], range(KW), 0, k.gh, k.gl, KW)
            row_tiles(k, pe, t, ps[2 + t][:, :], range(KW), KW, k.gh, k.gl, KW).then_inc(k.w_used, 1)

    glu((0, 0))
    with pe.Fori(1, KW // 2) as i:
        glu((i, 0))
    end_phase(k, pe, 4)

    def products(br, pair, slot, j):
        for n in range(2):
            d = 2 * pair + n
            wait(pe, k.prod, count(j, 16 * br + d - 3, 4))
            for t in range(KW):
                if isinstance(j[0], int) and d == 0:
                    pe.wait_ge(k.g_lo, KW * br + t + 1)
                mm = row_tiles(k, pe, slot, ps[4 + d][:, :], [t], n * KW + t, k.gh, k.gl, KW)
            mm.then_inc(k.w_used if n else k.p_ps, 1)

    def merge_c(j):
        for pair in range(2):
            wait(pe, k.w_lo, count(j, B_C + pair + 1, 2))
            products(0, pair, pair, j)

    def merge(br, j):
        for pair in range(2):
            b0 = B_BR + 24 * (br - 1) + 3 * pair
            for n in range(2):
                d = 2 * pair + n
                wait(pe, k.w_lo, count(j, b0 + n + 1, 6))
                wait(pe, k.gate_s, count(j, 16 * (br - 1) + d - 3, 4))
                row_tiles(k, pe, (b0 + n) % 2, ps[d][:, :], range(KD), 0, k.uh, k.ul, KD).then_inc(k.w_used, 1)
            wait(pe, k.w_lo, count(j, b0 + 3, 6))
            products(br, pair, b0 % 2, j)

    merge_c((0, 0))
    with pe.Fori(1, KD // 4) as i:
        merge_c((i, 0))
    for br in (1, 2):
        merge(br, (0, 0))
        with pe.Fori(1, KD // 4) as i:
            merge(br, (i, 0))
    end_phase(k, pe, 5)

    for c in range(4):
        for kb in range(4):
            b = B_OUT + 4 * c + kb
            slot = b % 2
            pe.wait_ge(k.w_lo, b + 1)
            if kb == 0:
                wait(pe, k.h_s, 4 * (c - 1))
            for m in range(NT):
                for n in range(4):
                    t = 4 * kb + n
                    if m == 0 and c == 0:
                        pe.wait_ge(k.m_lo, t + 1)
                    a, w = bass.ts(m, P), bass.ts(n, S)
                    mm = mm3(pe, ps[4 * (c % 2) + m][:, :], k.uh[:, t, a], k.ul[:, t, a],
                             k.wh[slot][:, w], k.wl[slot][:, w], t == 0, t == KD - 1)
                if kb == 3 and m < 3:
                    mm.then_inc(k.o_ps, 1)
            mm.then_inc(k.w_used, 1)


def normed_tiles(k):
    return [(k.prm1[:, 96 + t:97 + t], k.uh[:, t, :], k.ul[:, t, :], S) for t in range(KD)] + \
        [(k.prm1[:, 112 + t:113 + t], k.mh[:, t, :], k.ml[:, t, :], MEM) for t in range(KD)]


def scalar_program(k, act):
    ps, col = k.ps, k.col

    done = [0]

    def step(instruction):
        instruction.then_inc(k.alink, 1)
        done[0] += 1
        act.wait_ge(k.alink, done[0])

    act.wait_ge(k.cst_in, 16)
    for m in range(NT):
        act.wait_ge(k.x_in[m], 16)
        step(act.activation(k.junk[:, :], k.xs[:, m, :], ACT.Square, accum_out=k.stat[:, m:m + 1]))
    act.activation(k.stat[:, 8:12], k.stat[:, 0:4], ACT.Sqrt, bias=col["eps"], scale=1 / D).then_inc(k.x_root, 1)

    act.wait_ge(k.mem_in, 16 * MT)
    for m in range(MT):
        step(act.activation(k.junk[:, :], k.xs[:, NT + m, :], ACT.Square, accum_out=k.stat[:, 4 + m:5 + m]))
    act.activation(k.stat[:, 12:14], k.stat[:, 4:6], ACT.Sqrt, bias=col["eps"], scale=1 / D).then_inc(k.x_root, 1)
    act.wait_ge(k.wba_in, 16)
    act.activation(k.wbah[:, :], k.wba[:, :], ACT.Copy).then_inc(k.wba_hi, 1)
    act.wait_ge(k.prm, 2)
    for t, (gain, hi, _, n) in enumerate(normed_tiles(k)):
        act.wait_ge(k.x_tr, t + 1)
        act.activation(hi, ps[t % 4][:, 0:n], ACT.Copy, scale=gain).then_inc(k.u_hi, 1)
    split_hi(k, act, B_XA)
    end_phase(k, act, 1)

    def at_exp(j, m):
        act.wait_ge(k.xa_max, count(j, 2 * m + 2, 8))
        wait(act, k.xa_ptr, count(j, 0, 2))
        act.activation(k.px[:, m, :], ps[4 + m % 2][:, 0:MEM], ACT.Exp, bias=k.stat[:, 24 + m:25 + m],
                       scale=1 / 16, accum_out=k.stat[:, 28 + m:29 + m]).then_inc(k.xa_exp, 1)

    def at_out(j, b):
        act.wait_ge(k.w_used, count(j, B_XA + b + 1, 8))
        o = ps[b % 2]
        if b < 2 or b in (4, 5):
            wait(act, k.xa_sc, count(j, 0, 4))
        elif b < 4:
            wait(act, k.xa_vtr, count(j, 0, 1))
        else:
            wait(act, k.xa_og, count(j, 0, 2))
        t = b % 2
        if b < 4:
            act.activation([k.kt, k.vt][b // 2][:, t, :], o[:, 0:MEM], ACT.Copy).then_inc(k.xa_out, 1)
        else:
            act.activation([k.qx, k.zx][b // 2 - 2][:, t, :], o[:, :], ACT.Copy if b < 6 else ACT.Silu).then_inc(k.xa_out, 1)

    def s5_parameters():
        tp = k.tp
        act.wait_ge(k.prm, 2)
        act.activation(tp[:, 0, :], k.prm2[:, 64:96], ACT.Exp).then_inc(k.p_act, 1)
        act.wait_ge(k.p_dve, 1)
        act.activation(tp[:, 2, :], tp[:, 1, :], ACT.Exp).then_inc(k.p_act, 1)
        act.wait_ge(k.p_dve, 2)
        step(act.activation(tp[:, 4, :], tp[:, 3, :], ACT.Sin, scale=TWO_PI))
        step(act.activation(tp[:, 5, :], tp[:, 3, :], ACT.Abs))
        act.activation(tp[:, 5, :], tp[:, 5, :], ACT.Sin, scale=-TWO_PI, bias=col["quarter"]).then_inc(k.p_act, 1)

    def delta_parameters():
        act.wait_ge(k.ba_tr, 1)
        ba = ps[5][:, 0:NT * 16].rearrange("p (m c) -> p m c", m=NT)
        act.activation(k.hp[:, 0, :, :], ba[:, :, 0:HEADS], ACT.Exp, scale=-1.0).then_inc(k.p_act, 1)
        act.wait_ge(k.p_dve, 3)
        step(act.activation(k.hp[:, 2, :, :], k.hp[:, 1, :, :], ACT.Abs))
        step(act.activation(k.hp[:, 2, :, :], k.hp[:, 2, :, :], ACT.Exp, scale=-1.0))
        act.activation(k.alog_b[:, :], k.alog_b[:, :], ACT.Exp).then_inc(k.p_act, 1)
        act.wait_ge(k.p_dve, 4)
        act.activation(k.hp[:, 2, :, :], k.hp[:, 2, :, :], ACT.Ln).then_inc(k.p_act, 1)

    def summed_decays():
        act.wait_ge(k.gsum_ps, 1)
        act.activation(k.hp[:, 2, :, :], ps[7][:, 0:NT * HEADS].rearrange("p (m h) -> p m h", m=NT), ACT.Exp).then_inc(k.p_act, 1)

    def attention(a, j):
        for b in range(8):
            if a: split_hi(k, act, B_XA + b + 1, 8, a)
            if not j and b in (3, 5, 7):
                {3: s5_parameters, 5: delta_parameters, 7: summed_decays}[b]()
            if j and b < 2: at_exp(j, 2 * b); at_exp(j, 2 * b + 1)
            if a: at_out(a, b)

    attention((0, 0), None)
    attention((1, 0), (0, 0))
    with act.Fori(2, XH) as i:
        attention((i, 0), (i, -1))
    attention(None, (XH, -1))
    end_phase(k, act, 2)

    def tile_out(a, b):
        act.wait_ge(k.w_used, count(a, B_MIX + b + 1, 6))
        o = ps[b % 2]
        if b < 3:
            wait(act, k.conv, count(a, 4 * b + 4 - 12, 12))
            act.activation([k.qraw, k.kraw, k.vraw][b][:, 3:3 + S], o[:, :], ACT.Copy).then_inc(k.mx_out, 1)
        elif b == 3:
            wait(act, k.zb_st, count(a, 0, 16))
            act.activation(k.zbs[:, :], o[:, :], ACT.Silu).then_inc(k.mx_out, 1)
        elif b == 4:
            wait(act, k.z_kept, count(a, 0, 1))
            act.activation(k.zs[:, :], o[:, :], ACT.Silu).then_inc(k.mx_out, 1)
        else:
            wait(act, k.ysum, count(a, 0, 1))
            wait(act, k.bu, count(a, 0, 4))
            act.activation(k.xb[:, :], o[:, :], ACT.Copy).then_inc(k.mx_out, 1)

    def gate_out(g):
        n = g % 5 if g < 12 else 5 + g % 2
        buf = [k.qraw[:, 3:3 + S], k.kraw[:, 3:3 + S], k.vraw[:, 3:3 + S], k.zbs[:, :], k.zs[:, :], k.gk0[:, :], k.gk1[:, :]][n]
        act.wait_ge(k.w_used, B_GT + g + 1)
        if g < 3:
            act.wait_ge(k.conv, 12 * HEADS - 8 + 4 * g)
        elif g == 3:
            act.wait_ge(k.zb_st, 16 * HEADS)
        elif g == 4:
            act.wait_ge(k.z_kept, HEADS)
        elif g < 12:
            act.wait_ge(k.gt_st[n], 16 * (g // 5))
        else:
            wait(act, k.gt_st[n], 16 * (g // 2 - 6))
        act.activation(buf, ps[g % 2][:, :], ACT.Sigmoid).then_inc(k.mx_out, 1)
        act.wait_ge(k.mx_out, 6 * HEADS + g + 1)
        act.dma_start(k.gates_d[g * P:(g + 1) * P, :], buf).then_inc(k.gt_st[n], 16)

    def s5_tables(j, q):
        c, s = [k.tcos0, k.tcos1][q % 2], [k.tsin0, k.tsin1][q % 2]
        n = count(j, 3 * q, 12)
        act.wait_ge(k.args, count(j, 7 * q + 7, 28))
        wait(act, k.dem, count(j, 6 * (q - 1), 24))
        wait(act, k.mod, count(j, 8 * (q - 1), 32))
        act.activation(s[:, :], k.farg[:, :], ACT.Sin, scale=TWO_PI).then_inc(k.tab, 1)
        act.activation(c[:, :], k.farg[:, :], ACT.Abs).then_inc(k.tab, 1)
        act.wait_ge(k.tab, n + 2)
        act.activation(c[:, :], c[:, :], ACT.Sin, scale=-TWO_PI, bias=col["quarter"]).then_inc(k.tab, 1)

    def s5_matrices(j):
        act.wait_ge(k.s5_tr, count(j, 1, 1))
        wait(act, k.yp, count(j, 0, 4))
        act.activation(k.bc[:, :, :], ps[5][:, :].rearrange("p (n c) -> p n c", n=4), ACT.Copy).then_inc(k.bc_s, 1)

    def activation_of(j, n):
        t, sq = ((k.qc, k.rq), (k.kc, k.rk), (k.vc, None))[n]
        act.wait_ge(k.conv, count(j, 4 * n + 4, 12))
        act.activation(t[:, :], t[:, :], ACT.Silu).then_inc(k.silu, 1)
        if sq is not None:
            act.wait_ge(k.silu, count(j, n + 1, 3))
            act.activation(sq[:, :], t[:, :], ACT.Square).then_inc(k.sq, 1)

    def key_root(j):
        act.wait_ge(k.ss, count(j, 1, 2))
        act.activation(k.rk[:, :], ps[6][:, :], ACT.Sqrt, bias=col["eps"]).then_inc(k.root, 1)
        act.wait_ge(k.rsum, count(j, 1, 1))
        act.activation(k.er[:, :, :], ps[7][:, :].rearrange("p (n c) -> p n c", n=NT), ACT.Exp).then_inc(k.er_s, 1)

    def query_root(j):
        act.wait_ge(k.ss, count(j, 2, 2))
        act.activation(k.rq[:, :], ps[2][:, :], ACT.Sqrt, bias=col["eps128"], scale=float(P)).then_inc(k.root, 1)

    def decays(j):
        act.wait_ge(k.dd, count(j, 2, 3))
        act.activation(k.du[:, :, :], k.du[:, :, :], ACT.Exp).then_inc(k.dec, 1)
        act.wait_ge(k.dd, count(j, 3, 3))
        act.activation(k.dl[:, :, :], k.dl[:, :, :], ACT.Exp, scale=-1.0).then_inc(k.dec, 1)

    def keep_z(j):
        wait(act, k.og, count(j, 0, 2))
        act.activation(k.zk[:, :], k.zs[:, :], ACT.Copy).then_inc(k.z_kept, 1)

    def lower_turned(j):
        act.wait_ge(k.ltr, count(j, 1, 1))
        wait(act, k.lx, count(j, 0, 6))
        wait(act, k.og, count(j, 0, 2))
        act.activation(k.lt[:, :, :], ps[6][:, :].rearrange("p (n c) -> p n c", n=NT), ACT.Copy).then_inc(k.lt_s, 1)

    def weights_out(l):
        act.wait_ge(k.wt, count(l, 1, 1))
        act.activation(k.dl[:, :, :], ps[2][:, :].rearrange("p (n c) -> p n c", n=NT), ACT.Copy, scale=-1.0).then_inc(k.wtn, 1)

    def new_values(l, n):
        act.wait_ge(k.vp, count(l, n + 1, 4))
        act.activation(k.vn[:, n, :], ps[6][:, n * P:(n + 1) * P], ACT.Copy).then_inc(k.vn_s, 1)

    def output_squares(l):
        act.wait_ge(k.op, count(l, 4, 4))
        act.activation(k.lt[:, :, :], ps[2][:, :].rearrange("p (n c) -> p n c", n=NT), ACT.Square).then_inc(k.osq, 1)

    def output_root(l):
        act.wait_ge(k.sso, count(l, 1, 1))
        act.activation(k.lt[:, :, :], ps[6][:, :].rearrange("p (n c) -> p n c", n=NT), ACT.Sqrt, bias=col["eps"],
                       scale=1 / P).then_inc(k.oroot, 1)

    def mixer(a, j, l, gate=None):
        split = lambda b: split_hi(k, act, B_MIX + b + 1, 6, a)
        out = lambda b: tile_out(a, b) if gate is None else gate_out(gate + b)
        if a: split(0)
        if l: weights_out(l); new_values(l, 0); new_values(l, 1); new_values(l, 2)
        if j: tile_out(j, 5)
        if l: new_values(l, 3)
        if j: activation_of(j, 0)
        if a: out(0); split(1)
        if l: output_squares(l)
        if j: s5_matrices(j); activation_of(j, 1); activation_of(j, 2); s5_tables(j, 0)
        if l: output_root(l)
        if j: key_root(j); s5_tables(j, 1)
        if a: out(1); split(2)
        if j: query_root(j); decays(j); keep_z(j)
        if j: lower_turned(j)
        if a: out(2); split(3)
        if j: s5_tables(j, 2)
        if a: out(3); split(4)
        if j: s5_tables(j, 3)
        if a: out(4); split(5)
        if gate is not None: out(5)

    mixer((0, 0), None, None)
    mixer((1, 0), (0, 0), None)
    with act.Fori(2, HEADS) as i:
        mixer((i, 0), (i, -1), (i, -2))
    mixer((HEADS, 0), (HEADS, -1), (HEADS, -2), gate=0)
    mixer((HEADS + 1, 0), None, (HEADS, -1), gate=6)
    for n, stores in enumerate((3, 3, 2, 2, 2)):
        act.wait_ge(k.gt_st[n], 16 * stores)
    end_phase(k, act, 3)

    split_hi(k, act, B_GT + 13)
    gate_out(12)
    split_hi(k, act, B_GT + 14)
    act.wait_ge(k.y_in, 16)
    for t in range(KW):
        act.activation(k.yst[:, t, :], k.yst[:, t, :], ACT.Gelu_apprx_tanh).then_inc(k.y_act, 1)
    for t in range(KW):
        act.wait_ge(k.y_act, t + 1)
        act.activation(k.gh[:, t, :], k.yst[:, t, :], ACT.Copy).then_inc(k.y_hi, 1)
    gate_out(13)
    split_hi(k, act, B_GT + 15)
    gate_out(14)
    split_hi(k, act, B_GLU)
    gate_out(15)

    def glu(j):
        for t in range(2):
            split_hi(k, act, B_GLU + t + 1, 2, j)
            act.wait_ge(k.w_used, count(j, B_GLU + t + 1, 2))
            wait(act, [k.gb_st0, k.gb_st1][t], count(j, 0, 16))
            act.activation([k.gg0, k.gg1][t][:, :], ps[2 + t][:, :], ACT.Sigmoid).then_inc(k.sig, 1)

    glu((0, 0))
    with act.Fori(1, KW // 2) as i:
        glu((i, 0))
    act.wait_ge(k.gt_st[5], 32)
    act.wait_ge(k.gt_st[6], 32)
    end_phase(k, act, 4)

    def branch_hi(br):
        act.wait_ge(k.ga_in, 16 * (br + 1))
        for t in range(KW):
            act.activation(k.gh[:, t, :], k.gst[:, t, :], ACT.Copy).then_inc(k.g_hi, 1)

    def merge_c(j):
        for pair in range(2):
            split_hi(k, act, B_C + pair + 1, 2, j)

    branch_hi(0)
    merge_c((0, 0))
    with act.Fori(1, KD // 4) as i:
        merge_c((i, 0))
    for br in (1, 2):
        act.wait_ge(k.w_used, B_BR + 24 * (br - 1))
        branch_hi(br)

        def merge(j):
            for pair in range(2):
                b0 = B_BR + 24 * (br - 1) + 3 * pair
                for n in range(2):
                    d = 2 * pair + n
                    split_hi(k, act, b0 + n + 1, 6, j)
                    act.wait_ge(k.w_used, count(j, b0 + n + 1, 6))
                    wait(act, k.prod, count(j, 16 * br + d - 1, 4))
                    wait(act, k.mrg, count(j, 16 * br + d - 17, 4))
                    act.activation([k.sg0, k.sg1][n][:, :], ps[d][:, :], ACT.Sigmoid).then_inc(k.gate_s, 1)
                split_hi(k, act, b0 + 3, 6, j)

        merge((0, 0))
        with act.Fori(1, KD // 4) as i:
            merge((i, 0))
    end_phase(k, act, 5)

    for t in range(KD):
        act.activation(k.uh[:, t, :], k.merged[:, t, :], ACT.Copy).then_inc(k.m_hi, 1)
    for c in range(4):
        for kb in range(4):
            w = B_OUT + 4 * c + kb + 1
            if w < N_BLOCKS:
                split_hi(k, act, w)
        for m in range(NT):
            n = 4 * c + m
            act.wait_ge(k.h_s, n + 1)
            wait(act, k.h_sq, n)
            act.activation(k.xsq[:, :], k.hrow[:, m, c * S:(c + 1) * S], ACT.Square,
                           accum_out=k.ssq[:, m, c:c + 1]).then_inc(k.h_sq, 1)
    act.wait_ge(k.p_dve, 6)
    act.activation(k.stat[:, 8:12], k.stat[:, 0:4], ACT.Sqrt, bias=col["eps"], scale=1 / D).then_inc(k.p_act, 1)


def vector_program(k, dve):
    ps, mat, col, stat, tp, hp = k.ps, k.mat, k.col, k.stat, k.tp, k.hp
    done = [0]

    def step(instruction):
        instruction.then_inc(k.link, 1)
        done[0] += 1
        dve.wait_ge(k.link, done[0])

    tt, ts, stt = dve.tensor_tensor, dve.tensor_scalar, dve.scalar_tensor_tensor

    dve.wait_ge(k.rows_in, 160)
    dve.tensor_copy(k.rows2[64:96, :].rearrange("q (g s) -> q g s", g=2),
                    k.ldt2[64:96, :].unsqueeze(2).to_broadcast([32, 2, NS])).then_inc(k.ldt_rows, 1)
    dve.wait_ge(k.prm_ps, 2)
    dve.tensor_copy(k.prm1[:, :], ps[4][:, 0:P]).then_inc(k.prm, 1)
    dve.tensor_copy(k.prm2[:, :], ps[5][:, 0:P]).then_inc(k.prm, 1)
    dve.wait_ge(k.prm, 2)

    def scale_rows(first, n, at_root):
        dve.wait_ge(k.x_root, at_root)
        step(dve.reciprocal(stat[:, 16 + first:16 + first + n], stat[:, 8 + first:8 + first + n]))
        for m in range(n):
            ts(k.xs[:, first + m, :], k.xs[:, first + m, :], stat[:, 16 + first + m:17 + first + m], None, ALU.mult).then_inc(k.x_scale, 1)

    scale_rows(0, NT, 1)
    scale_rows(NT, MT, 2)
    dve.wait_ge(k.wba_hi, 1)
    tt(k.wbal[:, :], k.wba[:, :], k.wbah[:, :].bitcast(F32), ALU.subtract).then_inc(k.wba_lo, 1)
    for t, (gain, hi, lo, n) in enumerate(normed_tiles(k)):
        dve.wait_ge(k.u_hi, t + 1)
        stt(lo, ps[t % 4][:, 0:n], gain, hi.bitcast(F32), ALU.mult, ALU.subtract).then_inc(k.u_lo, 1)
    dve.wait_ge(k.ba_ps, 1)
    dve.tensor_copy(k.ba_rows, ps[6][0:16, :]).then_inc(k.ba_s, 1)
    split_lo(k, dve, B_XA)
    end_phase(k, dve, 1)

    def at_max(j, m):
        dve.wait_ge(k.xa_sc, count(j, m + 1, 4))
        wait(dve, k.xa_exp, count(j, m - 3, 4))
        dve.reduce_max(stat[:, 20 + m:21 + m], ps[4 + m % 2][:, 0:MEM], AX_X).then_inc(k.xa_max, 1)
        dve.wait_ge(k.xa_max, count(j, 2 * m + 1, 8))
        ts(stat[:, 24 + m:25 + m], stat[:, 20 + m:21 + m], -1 / 16, None, ALU.mult).then_inc(k.xa_max, 1)

    def at_norm(j, m):
        dve.wait_ge(k.xa_exp, count(j, m + 1, 4))
        dve.reciprocal(stat[:, 32 + m:33 + m], stat[:, 28 + m:29 + m]).then_inc(k.xa_sum, 1)
        dve.wait_ge(k.xa_sum, count(j, m + 1, 4))
        ts(k.px[:, m, :], k.px[:, m, :], stat[:, 32 + m:33 + m], None, ALU.mult).then_inc(k.xa_p, 1)

    def at_small(j, n):
        if n == 0:
            dve.wait_ge(k.xa_vtr, count(j, 1, 1))
            wait(dve, k.xa_o, count(j, 0, 2))
            dve.tensor_copy(k.vx[:, :, :], ps[2][:, :].rearrange("p (m c) -> p m c", m=MT)).then_inc(k.xa_v, 1)
        if n < 2:
            at_max(j, 2 * n)
            at_max(j, 2 * n + 1)
            at_norm(j, 2 * n)
            at_norm(j, 2 * n + 1)
        elif n in (3, 4):
            dve.wait_ge(k.xa_ptr, count(j, n - 2, 2))
            wait(dve, k.xa_o, count(j, 0, 2))
            dve.tensor_copy(k.ptx[:, n - 3, :], ps[3 + n][:, :]).then_inc(k.xa_pt, 1)
        elif n == 5:
            for t in range(2):
                dve.wait_ge(k.xa_o, count(j, t + 1, 2))
                wait(dve, [k.xa_st0, k.xa_st1][t], count(j, 0, 16))
                tt(k.ox[:, t, :], ps[2 + t][:, :], k.zx[:, t, :], ALU.mult).then_inc(k.xa_og, 1)

    lr, li = k.prm2[:, 0:32], k.prm2[:, 32:64]
    T = lambda n: tp[:, n, :]

    def s5_angles():
        dve.wait_ge(k.p_act, 1)
        tt(T(1), lr, T(0), ALU.mult).then_inc(k.p_dve, 1)
        step(tt(T(6), li, T(0), ALU.mult))
        step(ts(T(7), T(6), 1 / TWO_PI, ROUND, ALU.mult, ALU.add))
        step(ts(T(7), T(7), -ROUND, None, ALU.add))
        for part in (PI_A, PI_B, PI_C):
            step(stt(T(6), T(7), -part, T(6), ALU.mult, ALU.add))
        step(ts(T(8), T(6), 1 / TWO_PI, ROUND14, ALU.mult, ALU.add))
        step(ts(k.s5p[:, 1, :], T(8), -ROUND14, None, ALU.add))
        for part in (PI_A, PI_B, PI_C):
            step(stt(T(6), k.s5p[:, 1, :], -part, T(6), ALU.mult, ALU.add))
        step(ts(k.s5p[:, 2, :], T(6), 1 / TWO_PI, None, ALU.mult))
        step(tt(T(3), k.s5p[:, 1, :], k.s5p[:, 2, :], ALU.add))
        ts(T(3), T(3), 0.4999999, -0.4999999, ALU.min, ALU.max).then_inc(k.p_dve, 1)

    def s5_factors():
        dve.wait_ge(k.p_act, 3)
        step(dve.tensor_copy(k.s5p[:, 0, :], T(2)))
        step(tt(T(5), T(2), T(5), ALU.mult))
        step(ts(T(5), T(5), -1.0, None, ALU.add))
        step(tt(T(4), T(2), T(4), ALU.mult))
        step(tt(T(9), lr, lr, ALU.mult))
        step(tt(T(10), li, li, ALU.mult))
        step(tt(T(9), T(9), T(10), ALU.add))
        step(dve.reciprocal(T(9), T(9)))
        for n, (a, b, op) in enumerate(((T(5), T(4), ALU.add), (T(4), T(5), ALU.subtract))):
            step(tt(T(11), a, lr, ALU.mult))
            step(tt(T(12), b, li, ALU.mult))
            step(tt(T(11), T(11), T(12), op))
            step(tt(k.s5p[:, 3 + n, :], T(11), T(9), ALU.mult))

    def delta_parameters():
        ba = ps[5][:, 0:NT * 16].rearrange("p (m c) -> p m c", m=NT)
        rep = lambda v: v.unsqueeze(1).to_broadcast([P, NT, HEADS])
        dve.wait_ge(k.p_act, 4)
        step(ts(hp[:, 0, :, :], hp[:, 0, :, :], 1.0, None, ALU.add))
        step(dve.reciprocal(hp[:, 0, :, :], hp[:, 0, :, :]))
        tt(hp[:, 1, :, :], ba[:, :, HEADS:16], rep(k.dtb_b[:, :]), ALU.add).then_inc(k.p_dve, 1)
        dve.wait_ge(k.p_act, 5)
        ts(hp[:, 2, :, :], hp[:, 2, :, :], 1.0, None, ALU.add).then_inc(k.p_dve, 1)
        dve.wait_ge(k.p_act, 6)
        step(stt(hp[:, 2, :, :], hp[:, 1, :, :], 0.0, hp[:, 2, :, :], ALU.max, ALU.add))
        step(tt(hp[:, 2, :, :], hp[:, 2, :, :], rep(k.alog_b[:, :]), ALU.mult))
        ts(hp[:, 3, :, :], hp[:, 2, :, :], -1.0, None, ALU.mult).then_inc(k.g_done, 1)

    def summed_decays():
        dve.wait_ge(k.p_act, 7)
        step(dve.tensor_copy(hp[:, 1, :, :], ps[7][:, 0:NT * HEADS].rearrange("p (m h) -> p m h", m=NT)))
        step(tt(hp[:, 2, :, :], hp[:, 2, :, :], hp[:, 0, :, :], ALU.mult))

    def attention(a, j):
        for b in range(8):
            if a: split_lo(k, dve, B_XA + b + 1, 8, a)
            if not j and b >= 3 and b != 6:
                {3: s5_angles, 4: s5_factors, 5: delta_parameters, 7: summed_decays}[b]()
            if j: at_small(j, b)

    attention((0, 0), None)
    attention((1, 0), (0, 0))
    with dve.Fori(2, XH) as i:
        attention((i, 0), (i, -1))
    attention(None, (XH, -1))
    end_phase(k, dve, 2)

    def chunked(v):
        return v.rearrange("p (n c) -> p n c", n=NT)

    def rows(v):
        return v.unsqueeze(2).to_broadcast([P, NT, P])

    def rep_chunks(m):
        return m.unsqueeze(1).to_broadcast([P, NT, P])

    def head_parameters(j):
        h = at(j)
        wait(dve, k.args, count(j, 0, 28))
        wait(dve, k.pm, count(j, 0, 4))
        dve.tensor_copy(k.s5h[:, :, :], k.s5p[:, :, bass.ds(4 * h, 4)]).then_inc(k.sliced, 1)
        dve.tensor_copy(k.cwh[:, :, :], k.prm1[:, 0:96].rearrange("p (n r h) -> p n r h", n=CONV, r=3)[:, :, :, bass.ds(h, 1)]).then_inc(k.sliced, 1)
        dve.tensor_copy(k.hph[:, :, :], hp[:, :, :, bass.ds(h, 1)]).then_inc(k.sliced, 1)
        dve.wait_ge(k.sliced, count(j, 3, 3))

    def s5_matrices(j):
        w = k.s5_w
        dve.tensor_copy(k.dh[:, :], k.prm2[:, 96:104][:, bass.ds(at(j), 1)]).then_inc(w, 1)
        dve.wait_ge(k.s5_in, count(j, 64, 64))
        cre, cim = (k.s5h[:, n, :].unsqueeze(2).to_broadcast([P, 4, GS]) for n in (3, 4))
        br, bi = k.braw[:, 0, :, :], k.braw[:, 1, :, :]
        for n, (b, c) in enumerate(((br, cre), (bi, cim), (bi, cre), (br, cim))):
            tt(k.bt[:, n, :, :], b, c, ALU.mult).then_inc(w, 1)
        dve.wait_ge(w, count(j, 5, 13))
        wait(dve, k.s5_tr, count(j, 0, 1))
        for n, op in ((0, ALU.subtract), (1, ALU.add)):
            for g in range(2):
                r = slice(64 * g, 64 * g + 64)
                tt(k.bpad[r, n, :, g, :], k.bt[r, 2 * n, :, :], k.bt[r, 2 * n + 1, :, :], op).then_inc(w, 1)
        for n, names in enumerate((("even", "odd"), ("neven", "nodd"))):
            for g in range(2):
                ts(k.cpad[:, n, g, :], k.craw[:, n, :], col[names[g]], None, ALU.mult).then_inc(w, 1)

    def convolve(j, part):
        src, dst = [k.qraw, k.kraw, k.vraw][part], [k.qc, k.kc, k.vc][part]
        n = count(j, 4 * part, 12)
        dve.wait_ge(k.mx_out, count(j, part + 1, 6))
        wait(dve, k.kq, count(j, 0, 1))
        wait(dve, k.kk, count(j, 0, 1))
        wait(dve, k.vtr, count(j, 0, 1))
        ts(dst[:, :], src[:, 0:S], k.cwh[:, 0, part:part + 1], None, ALU.mult).then_inc(k.conv, 1)
        for t in range(1, CONV):
            dve.wait_ge(k.conv, n + t)
            stt(dst[:, :], src[:, t:t + S], k.cwh[:, t, part:part + 1], dst[:, :], ALU.mult, ALU.add).then_inc(k.conv, 1)

    def log_decays(j):
        tt(k.gx[:, :, :], rep_chunks(mat["upper"]), rows(k.hph[:, 3, :]), ALU.mult).then_inc(k.gu, 1)

    def differences(j):
        dve.wait_ge(k.rsum, count(j, 1, 1))
        dve.wait_ge(k.er_s, count(j, 1, 1))
        wait(dve, k.vp, count(j, 0, 4))
        wait(dve, k.op, count(j, 0, 4))
        tt(k.dl[:, :, :], chunked(ps[7][:, :]), rows(k.hph[:, 1, :]), ALU.subtract).then_inc(k.dd, 1)
        dve.wait_ge(k.dd, count(j, 1, 3))
        ts(k.du[:, :, :], k.dl[:, :, :], 0.0, None, ALU.min).then_inc(k.dd, 1)
        ts(k.dl[:, :, :], k.dl[:, :, :], 0.0, None, ALU.max).then_inc(k.dd, 1)

    def normed_keys(j):
        dve.wait_ge(k.root, count(j, 1, 2))
        dve.reciprocal(k.rk[:, :], k.rk[:, :]).then_inc(k.rn, 1)
        dve.wait_ge(k.rn, count(j, 1, 2))
        tt(k.kc[:, :], k.kc[:, :], k.rk[:, :], ALU.mult).then_inc(k.qk, 1)

    def normed_queries(j):
        dve.wait_ge(k.root, count(j, 2, 2))
        dve.reciprocal(k.rq[:, :], k.rq[:, :]).then_inc(k.rn, 1)
        dve.wait_ge(k.rn, count(j, 2, 2))
        tt(k.qc[:, :], k.qc[:, :], k.rq[:, :], ALU.mult).then_inc(k.qk, 1)

    def values(j):
        dve.wait_ge(k.vtr, count(j, 1, 1))
        tt(k.vb[:, :, :], chunked(ps[2][:, :]), rows(k.hph[:, 0, :]), ALU.mult).then_inc(k.vb_s, 1)

    def keys(j):
        dve.wait_ge(k.ktr, count(j, 1, 1))
        dve.wait_ge(k.dec, count(j, 2, 2))
        wait(dve, k.wt, count(j, 0, 1))
        wait(dve, k.sp_s, count(j, 0, 3))
        dve.wait_ge(k.pm, count(j, 3, 4))
        wait(dve, k.g_st, count(j, 0, 16))
        tt(k.kbg[:, :, :], chunked(ps[6][:, :]), rows(k.hph[:, 2, :]), ALU.mult).then_inc(k.kb, 1)
        tt(k.kd[:, :, :], chunked(ps[6][:, :]), k.du[:, :, P - 1:P].to_broadcast([P, NT, P]), ALU.mult).then_inc(k.kb, 1)

    def system(j):
        dve.wait_ge(k.kk, count(j, 1, 1))
        dve.wait_ge(k.pm, count(j, 2, 4))
        tt(k.dl[:, :, :], chunked(ps[7][:, :]), k.dl[:, :, :], ALU.mult).then_inc(k.lm, 1)

    def queries(j):
        dve.wait_ge(k.kq, count(j, 1, 1))
        dve.wait_ge(k.pm, count(j, 3, 4))
        tt(k.du[:, :, :], chunked(ps[2][:, :]), k.du[:, :, :], ALU.mult).then_inc(k.qkt, 1)

    def first_level(j):
        dve.wait_ge(k.lm, count(j, 1, 1))
        wait(dve, k.lx, count(j, 0, 6))
        tt(k.tl[:, :, :], k.dl[:, :, :], rep_chunks(mat["low1"]), ALU.mult).then_inc(k.tu_s, 1)
        dve.wait_ge(k.lt_s, count(j, 1, 1))
        tt(k.tu[:, :, :], k.lt[:, :, :], rep_chunks(mat["up1"]), ALU.mult).then_inc(k.tu_s, 1)
        dve.wait_ge(k.tu_s, count(j, 1, 4))
        tt(k.tl[:, :, :], rep_chunks(mat["ident"]), k.tl[:, :, :], ALU.subtract).then_inc(k.tu_s, 1)
        dve.wait_ge(k.tu_s, count(j, 2, 4))
        tt(k.tu[:, :, :], rep_chunks(mat["ident"]), k.tu[:, :, :], ALU.subtract).then_inc(k.tu_s, 1)

    def level_x(j, l):
        dve.wait_ge(k.lx, count(j, l, 6))
        tt(k.gx[:, :, :], chunked(ps[2][:, :]), rep_chunks(mat[f"low{2 ** l}"]), ALU.mult).then_inc(k.xm, 1)

    def level_p(j, l):
        dve.wait_ge(k.lp, count(j, l, 6))
        if l < 6:
            tt(k.tl[:, :, :], k.tl[:, :, :], chunked(ps[6][:, :]), ALU.subtract).then_inc(k.tus, 1)
        tt(k.tu[:, :, :], k.tu[:, :, :], chunked(ps[7][:, :]), ALU.subtract).then_inc(k.tus, 1)

    def state(j, n):
        dve.wait_ge(k.sp_s, count(j, n + 1, 3))
        dve.wait_ge(k.op, count(j, n + 1, 4))
        if n == 0:
            dve.tensor_copy(k.st[:, :], ps[7][:, 0:P]).then_inc(k.st_s, 1)
        else:
            stt(k.st[:, :], k.st[:, :], k.er[:, n, P - 1:P], ps[7][:, 0:P], ALU.mult, ALU.add).then_inc(k.st_s, 1)

    def gated(j):
        dve.wait_ge(k.oroot, count(j, 1, 1))
        dve.reciprocal(k.tl[:, :, :], k.lt[:, :, :]).then_inc(k.orn, 1)
        dve.wait_ge(k.orn, count(j, 1, 1))
        stt(k.kbg[:, :, :], chunked(ps[2][:, :]), k.prm2[:, 104:105], k.tl[:, :, :], ALU.mult, ALU.mult).then_inc(k.og, 1)
        dve.wait_ge(k.og, count(j, 1, 2))
        dve.wait_ge(k.z_kept, count(j, 1, 1))
        tt(k.kbg[:, :, :], k.kbg[:, :, :], chunked(k.zk[:, :]), ALU.mult).then_inc(k.og, 1)

    def s5_states(j, q, part):
        c, s = [k.tcos0, k.tcos1][q % 2], [k.tsin0, k.tsin1][q % 2]
        gr, gi = [k.gr0, k.gr1][q % 2], [k.gi0, k.gi1][q % 2]
        n = count(j, 8 * q + 3 * part, 32)
        re, im = ps[3], ps[4]
        if part == 0:
            dve.wait_ge(k.tab, count(j, 3 * q + 3, 12))
            dve.wait_ge(k.bu, count(j, q + 1, 4))
            wait(dve, k.dem, count(j, 6 * (q - 1), 24))
            if q == 0:
                wait(dve, k.y_st, count(j, 0, 16))
        g, x1, x2, op = (gi, im, re, ALU.subtract) if part else (gr, re, im, ALU.add)
        tt(k.ma[:, :], x1[:, :], c[:, :], ALU.mult).then_inc(k.mod, 1)
        tt(k.mb[:, :], x2[:, :], s[:, :], ALU.mult).then_inc(k.mod, 1)
        dve.wait_ge(k.mod, n + 2)
        tt(g[:, :], k.ma[:, :], k.mb[:, :], op).then_inc(k.mod, 1)
        dve.wait_ge(k.mod, n + 3)
        if part:
            for g in (gr, gi):
                dve.tensor_tensor_scan(g[:, :], k.s5h[:, 0, q:q + 1].to_broadcast([P, S]), g[:, :], 0.0,
                                       ALU.mult, ALU.add).then_inc(k.mod, 1)

    def s5_sum(j):
        dve.wait_ge(k.yp, count(j, 4, 4))
        stt(k.ma[:, :], k.xb[:, :], k.dh[:, 0:1], ps[5][:, :], ALU.mult, ALU.add).then_inc(k.ysum, 1)

    def mixer(a, j, l):
        split = lambda b: split_lo(k, dve, B_MIX + b + 1, 6, a)
        if a: split(0)
        if l: state(l, 0)
        if j: head_parameters(j)
        if l: state(l, 1); s5_sum(l)
        if j: log_decays(j)
        if l: state(l, 2)
        if j: convolve(j, 0); s5_matrices(j); convolve(j, 1); convolve(j, 2)
        if a: split(1)
        if j: s5_states(j, 0, 0); s5_states(j, 0, 1)
        if l: gated(l)
        if j: differences(j); normed_keys(j)
        if a: split(2)
        if j: normed_queries(j); keys(j); system(j); values(j); s5_states(j, 1, 0); s5_states(j, 1, 1)
        if j: first_level(j); queries(j)
        if a: split(3)
        if j: level_x(j, 1); s5_states(j, 2, 0); level_p(j, 1); s5_states(j, 2, 1); level_x(j, 2)
        if a: split(4)
        if j: level_p(j, 2); level_x(j, 3); level_p(j, 3); s5_states(j, 3, 0); level_x(j, 4); s5_states(j, 3, 1)
        if a: split(5)
        if j: level_p(j, 4); level_x(j, 5); level_p(j, 5); level_x(j, 6); level_p(j, 6)

    mixer((0, 0), None, None)
    dve.wait_ge(k.pad_zero, 4)
    mixer((1, 0), (0, 0), None)
    with dve.Fori(2, HEADS) as i:
        mixer((i, 0), (i, -1), (i, -2))
    mixer((HEADS, 0), (HEADS, -1), (HEADS, -2))
    mixer((HEADS + 1, 0), None, (HEADS, -1))
    end_phase(k, dve, 3)

    split_lo(k, dve, B_GT + 13)
    split_lo(k, dve, B_GT + 14)
    for t in range(KW):
        dve.wait_ge(k.y_hi, t + 1)
        tt(k.gl[:, t, :], k.yst[:, t, :], k.gh[:, t, :].bitcast(F32), ALU.subtract).then_inc(k.y_lo, 1)
    split_lo(k, dve, B_GT + 15)
    split_lo(k, dve, B_GLU)
    def glu(j):
        for t in range(2):
            gg, zv, gv = [k.gg0, k.gg1][t], [k.zv0, k.zv1][t], [k.gv0, k.gv1][t]
            split_lo(k, dve, B_GLU + t + 1, 2, j)
            dve.wait_ge(k.sig, count(j, t + 1, 2))
            tt(gg[:, :], ps[t][:, :], gg[:, :], ALU.mult).then_inc(gv, 1)
            dve.wait_ge(gv, count(j, 1, 2))
            dve.wait_ge([k.zb_in0, k.zb_in1][t], count(j, 16, 16))
            tt(gg[:, :], gg[:, :], zv[:, :], ALU.mult).then_inc(gv, 1)

    glu((0, 0))
    with dve.Fori(1, KW // 2) as i:
        glu((i, 0))
    end_phase(k, dve, 4)

    def branch_lo(br):
        for t in range(KW):
            dve.wait_ge(k.g_hi, KW * br + t + 1)
            tt(k.gl[:, t, :], k.gst[:, t, :], k.gh[:, t, :].bitcast(F32), ALU.subtract).then_inc(k.g_lo, 1)

    def tile_made(n, products, blocks):
        if n == 0:
            dve.wait_ge(k.p_ps, products)
        else:
            dve.wait_ge(k.w_used, blocks)

    def merge_c(j):
        for pair in range(2):
            split_lo(k, dve, B_C + pair + 1, 2, j)
            dve.wait_ge(k.gt_in[pair], count(j, 16, 16))
            for n in range(2):
                d = 2 * pair + n
                tile_made(n, count(j, pair + 1, 2), count(j, B_C + pair + 1, 2))
                tt(k.merged[:, bass.ds(count(j, d, 4), 1), :], ps[4 + d][:, :].unsqueeze(1),
                   [k.gates0, k.gates1][pair][:, n:n + 1, :], ALU.mult).then_inc(k.prod, 1)

    branch_lo(0)
    merge_c((0, 0))
    with dve.Fori(1, KD // 4) as i:
        merge_c((i, 0))
    for br in (1, 2):
        branch_lo(br)

        def merge(j):
            for pair in range(2):
                b0 = B_BR + 24 * (br - 1) + 3 * pair
                for n in range(3):
                    split_lo(k, dve, b0 + n + 1, 6, j)
                for n in range(2):
                    d = 2 * pair + n
                    t = 16 * br + d
                    sg = [k.sg0, k.sg1][n]
                    m = k.merged[:, bass.ds(count(j, d, 4), 1), :]
                    tile_made(n, count(j, 8 * br + pair + 1, 2), count(j, b0 + 3, 6))
                    dve.wait_ge(k.gate_s, count(j, t - 15, 4))
                    tt(sg[:, :].unsqueeze(1), ps[4 + d][:, :].unsqueeze(1), sg[:, :].unsqueeze(1), ALU.mult).then_inc(k.prod, 1)
                    dve.wait_ge(k.prod, count(j, t + 1, 4))
                    tt(m, m, sg[:, :].unsqueeze(1), ALU.add).then_inc(k.mrg, 1)

        merge((0, 0))
        with dve.Fori(1, KD // 4) as i:
            merge((i, 0))
    end_phase(k, dve, 5)

    for t in range(KD):
        dve.wait_ge(k.m_hi, t + 1)
        tt(k.ul[:, t, :], k.merged[:, t, :], k.uh[:, t, :].bitcast(F32), ALU.subtract).then_inc(k.m_lo, 1)
    for c in range(4):
        for kb in range(4):
            w = B_OUT + 4 * c + kb + 1
            if w < N_BLOCKS:
                split_lo(k, dve, w)
        dve.wait_ge(k.xr_in, 64 * (c + 1))
        for m in range(NT):
            if m < 3:
                dve.wait_ge(k.o_ps, 3 * c + m + 1)
            else:
                dve.wait_ge(k.w_used, B_OUT + 4 * c + 4)
            tt(k.hrow[:, m, c * S:(c + 1) * S], ps[4 * (c % 2) + m][:, :], k.xr[:, m, :],
               ALU.add).then_inc(k.h_s, 1)
    dve.wait_ge(k.h_sq, 16)
    dve.reduce_sum(stat[:, 0:4], k.ssq[:, :, :], AX_X).then_inc(k.p_dve, 2)
    dve.wait_ge(k.p_act, 8)
    step(dve.reciprocal(stat[:, 16:20], stat[:, 8:12]))
    dve.wait_ge(k.fg_in, 16)
    for m in range(NT):
        stt(k.hrow[:, m, :], k.hrow[:, m, :], stat[:, 16 + m:17 + m], k.fg[:, :], ALU.mult, ALU.mult).then_inc(k.fin, 1)


_INS = ["x", "mem", "norm_g", "w_in", "conv_w", "gdn_a_log", "gdn_dt_bias", "gdn_norm_g", "s5_lambda_re",
        "s5_lambda_im", "s5_log_dt", "s5_b_re", "s5_b_im", "s5_c_re", "s5_c_im", "s5_d", "s5_w_glu",
        "mem_norm_g", "w_kv_mem", "w_br_a", "w_br_b", "w_br_c", "w_out", "final_g"]


def kernel(**inputs):
    import concourse.bacc as _bacc
    from concourse.bass_utils import run_bass_kernel_spmd as _run

    nc = _bacc.Bacc("TRN2", target_bir_lowering=False, num_devices=1)
    arrays, args = {}, []
    for name in _INS + ["consts"]:
        a = constants() if name == "consts" else np.ascontiguousarray(inputs[name])
        arrays[f"in_{name}_dram"] = a
        args.append(nc.dram_tensor(f"in_{name}_dram", a.shape, mybir.dt.from_np(a.dtype), kind="ExternalInput").ap())
    args.append(nc.dram_tensor("out_0_dram", (1, S, D), F32, kind="ExternalOutput").ap())
    build(nc, *args)
    r = _run(nc, [arrays], core_ids=[0])
    return r.results[0]["out_0_dram"]
```
